# Optimizing a Trainium2 kernel written in Bass

```python
import math
import jax, jax.numpy as jnp
from jax import lax
import numpy as np

D_MODEL = 1024
BATCH = 1
SEQ = 256
DEPTH = 1

D_MIX = D_MODEL
NSA_HEADS = 8
NSA_KV_GROUPS = 2
NSA_HEAD_DIM = 64
NSA_HPG = NSA_HEADS // NSA_KV_GROUPS
CMP_BLOCK = 32
CMP_STRIDE = 16
CMP_HIDDEN = 256
SLC_BLOCK = 64
SLC_TOPK = 8
WINDOW = 512
FORCE_SCORE = 1e4
GLA_HEADS = 4
GLA_DK = 64
GLA_DV = 128
GLA_GATE_RANK = 16
GLA_TAU = 16.0
GLA_CHUNK = 64
ROPE_THETA = 500000.0
ROT_DIM = NSA_HEAD_DIM // 4
D_FF = 2816
CONV_W = 3
EPS = 1e-6
Q_BLOCK = 64
NEG = -1e30

NSA_Q_W = NSA_HEADS * NSA_HEAD_DIM
NSA_KV_W = NSA_KV_GROUPS * NSA_HEAD_DIM
GLA_QK_W = GLA_HEADS * GLA_DK
GLA_V_W = GLA_HEADS * GLA_DV
IN_SPLITS = [NSA_Q_W, 6 * NSA_KV_W, 3 * NSA_HEADS, GLA_QK_W, GLA_QK_W, GLA_V_W, GLA_GATE_RANK, GLA_V_W]
D_IN = sum(IN_SPLITS)


def rms_norm(x, g):
    xf = x.astype(jnp.float32)
    y = xf * lax.rsqrt(jnp.mean(xf * xf, axis=-1, keepdims=True) + EPS)
    return (y * g.astype(jnp.float32)).astype(x.dtype)

def partial_rope(x, pos):
    half = ROT_DIM // 2
    inv = ROPE_THETA ** (-jnp.arange(half, dtype=jnp.float32) / half)
    ang = pos.astype(jnp.float32)[:, None] * inv[None, :]
    cos = jnp.cos(ang)[:, None, :]
    sin = jnp.sin(ang)[:, None, :]
    xr = x[..., :ROT_DIM].astype(jnp.float32)
    x1, x2 = xr[..., :half], xr[..., half:]
    rot = jnp.concatenate([x1 * cos - x2 * sin, x2 * cos + x1 * sin], axis=-1).astype(x.dtype)
    return jnp.concatenate([rot, x[..., ROT_DIM:]], axis=-1)

def masked_softmax(s, mask):
    s = jnp.where(mask, s.astype(jnp.float32), NEG)
    return jax.nn.softmax(s, axis=-1) * mask

def nsa_mixer(q, kv, gate_logits, q_gain, k_gains, pe_k, pe_v, w1_k, w2_k, w1_v, w2_v):
    B, S = q.shape[0], q.shape[1]
    dt = q.dtype
    G, HPG, D = NSA_KV_GROUPS, NSA_HPG, NSA_HEAD_DIM
    scale = D ** -0.5
    pos = jnp.arange(S)
    kc, vc, ks, vs, kw, vw = [c.reshape(B, S, G, D) for c in jnp.split(kv, 6, axis=-1)]
    q = partial_rope(rms_norm(q.reshape(B, S, NSA_HEADS, D), q_gain), pos)
    q = q.reshape(B, S, G, HPG, D) * scale

    n_cmp = (S - CMP_BLOCK) // CMP_STRIDE + 1
    blk = np.arange(n_cmp)[:, None] * CMP_STRIDE + np.arange(CMP_BLOCK)[None, :]

    def compress(t, pe, w1, w2):
        tb = t[:, blk] + pe[:, None, :]
        tb = jnp.moveaxis(tb, 3, 2).reshape(B, n_cmp, G, CMP_BLOCK * D)
        return jax.nn.gelu(tb @ w1) @ w2

    cmp_end = jnp.arange(n_cmp) * CMP_STRIDE + CMP_BLOCK - 1
    k_cmp = partial_rope(rms_norm(compress(kc, pe_k, w1_k, w2_k), k_gains[0]), cmp_end)
    v_cmp = compress(vc, pe_v, w1_v, w2_v)
    s_cmp = jnp.einsum('bsghd,bngd->bghsn', q, k_cmp)
    p_cmp = masked_softmax(s_cmp, cmp_end[None, :] <= pos[:, None])
    o_cmp = jnp.einsum('bghsn,bngd->bsghd', p_cmp.astype(dt), v_cmp).reshape(B, S, NSA_HEADS, D)

    n_slc = S // SLC_BLOCK
    top_k = min(SLC_TOPK, n_slc)
    ci = np.arange(n_cmp)[:, None]
    sj = np.arange(n_slc)[None, :]
    overlap = ((ci * CMP_STRIDE < (sj + 1) * SLC_BLOCK) &
               (ci * CMP_STRIDE + CMP_BLOCK > sj * SLC_BLOCK)).astype(np.float32)
    p_slc = jnp.einsum('bghsn,nj->bgsj', p_cmp, jnp.asarray(overlap))
    j = jnp.arange(n_slc)[None, :]
    cur = (pos // SLC_BLOCK)[:, None]
    forced = (j == 0) | (j == cur) | (j == cur - 1)
    causal_blk = j * SLC_BLOCK <= pos[:, None]
    score = jnp.where(causal_blk, jnp.where(forced, FORCE_SCORE, p_slc), -jnp.inf)
    _, sel_idx = lax.top_k(score, top_k)

    ks = partial_rope(rms_norm(ks, k_gains[1]), pos)
    kw = partial_rope(rms_norm(kw, k_gains[2]), pos)
    ks_blk = jnp.moveaxis(ks.reshape(B, n_slc, SLC_BLOCK, G, D), 3, 1)
    vs_blk = jnp.moveaxis(vs.reshape(B, n_slc, SLC_BLOCK, G, D), 3, 1)
    pad = ((0, 0), (WINDOW, 0), (0, 0), (0, 0))
    kw_pad = jnp.pad(kw, pad)
    vw_pad = jnp.pad(vw, pad)
    n_qb = S // Q_BLOCK
    q_blocks = jnp.moveaxis(q.reshape(B, n_qb, Q_BLOCK, G, HPG, D), 1, 0)
    idx_blocks = jnp.moveaxis(sel_idx.reshape(B, G, n_qb, Q_BLOCK, top_k), 2, 0)
    bi = jnp.arange(B)[:, None, None, None]
    gi = jnp.arange(G)[None, :, None, None]

    def block_fn(args):
        i, qb, ib = args
        start = i * Q_BLOCK
        tq = start + jnp.arange(Q_BLOCK)
        k_sel = ks_blk[bi, gi, ib].reshape(B, G, Q_BLOCK, top_k * SLC_BLOCK, D)
        v_sel = vs_blk[bi, gi, ib].reshape(B, G, Q_BLOCK, top_k * SLC_BLOCK, D)
        kpos = (ib[..., None] * SLC_BLOCK + jnp.arange(SLC_BLOCK)).reshape(B, G, Q_BLOCK, top_k * SLC_BLOCK)
        m_sel = kpos <= tq[None, None, :, None]
        s = jnp.einsum('bqghd,bgqkd->bghqk', qb, k_sel)
        p = masked_softmax(s, m_sel[:, :, None])
        o_sel = jnp.einsum('bghqk,bgqkd->bqghd', p.astype(dt), v_sel)
        k_win = lax.dynamic_slice_in_dim(kw_pad, start, WINDOW + Q_BLOCK, axis=1)
        v_win = lax.dynamic_slice_in_dim(vw_pad, start, WINDOW + Q_BLOCK, axis=1)
        wpos = start - WINDOW + jnp.arange(WINDOW + Q_BLOCK)
        m_win = ((wpos[None, :] <= tq[:, None]) & (wpos[None, :] > tq[:, None] - WINDOW)
                 & (wpos[None, :] >= 0))
        s = jnp.einsum('bqghd,bkgd->bghqk', qb, k_win)
        p = masked_softmax(s, m_win)
        o_win = jnp.einsum('bghqk,bkgd->bqghd', p.astype(dt), v_win)
        return o_sel, o_win

    o_sel, o_win = lax.map(block_fn, (jnp.arange(n_qb), q_blocks, idx_blocks))
    o_sel = jnp.moveaxis(o_sel, 0, 1).reshape(B, S, NSA_HEADS, D)
    o_win = jnp.moveaxis(o_win, 0, 1).reshape(B, S, NSA_HEADS, D)

    g = jax.nn.sigmoid(gate_logits.reshape(B, S, NSA_HEADS, 3).astype(jnp.float32)).astype(dt)
    o = g[..., 0:1] * o_cmp + g[..., 1:2] * o_sel + g[..., 2:3] * o_win
    return o.reshape(B, S, NSA_Q_W)

def gla_mixer(q, k, v, g_lr, g_out, w_gate2, b_gate, out_gain):
    B, S = q.shape[0], q.shape[1]
    dt = q.dtype
    H, L = GLA_HEADS, GLA_CHUNK
    C = S // L

    def heads(t, d):
        return t.astype(jnp.float32).reshape(B, C, L, H, d).transpose(0, 3, 1, 2, 4)

    log_a = jax.nn.log_sigmoid((g_lr @ w_gate2 + b_gate).astype(jnp.float32)) / GLA_TAU
    qh = heads(q, GLA_DK) * (GLA_DK ** -0.5)
    kh = heads(k, GLA_DK)
    vh = heads(v, GLA_DV)
    b = jnp.cumsum(heads(log_a, GLA_DK), axis=3)
    b_last = b[:, :, :, -1:, :]
    q_t = qh * jnp.exp(b)
    k_t = kh * jnp.exp(-b)
    tril = jnp.tril(jnp.ones((L, L), dtype=bool))
    A = jnp.where(tril, jnp.einsum('bhcid,bhcjd->bhcij', q_t, k_t), 0.0)
    o_intra = jnp.einsum('bhcij,bhcjv->bhciv', A, vh)
    dS = jnp.einsum('bhcjd,bhcjv->bhcdv', kh * jnp.exp(b_last - b), vh)
    decay = jnp.exp(b_last[:, :, :, 0, :])

    def step(state, xs):
        dec, ds = xs
        return dec[..., None] * state + ds, state

    init = jnp.zeros((B, H, GLA_DK, GLA_DV), jnp.float32)
    _, s_prev = lax.scan(step, init, (jnp.moveaxis(decay, 2, 0), jnp.moveaxis(dS, 2, 0)))
    s_prev = jnp.moveaxis(s_prev, 0, 2)
    o = o_intra + jnp.einsum('bhcid,bhcdv->bhciv', q_t, s_prev)
    o = o.transpose(0, 2, 3, 1, 4).reshape(B, S, H, GLA_DV)
    o = rms_norm(o, out_gain) * jax.nn.silu(g_out.astype(jnp.float32).reshape(B, S, H, GLA_DV))
    return o.reshape(B, S, GLA_V_W).astype(dt)

def causal_dwconv(u, w, b):
    C = u.shape[-1]
    y = lax.conv_general_dilated(u, w[:, None, :].astype(u.dtype), window_strides=(1,),
                                 padding=[(CONV_W - 1, 0)],
                                 dimension_numbers=('NWC', 'WIO', 'NWC'),
                                 feature_group_count=C)
    return y + b

def first_inputs(seed: int = 0) -> dict:
    key = jax.random.key(seed)
    ks = jax.random.split(key, 24)
    L = DEPTH

    def nrm(k, shape, scale):
        return jax.random.normal(k, shape, jnp.float32) * scale

    def gain(k, shape):
        return 1.0 + 0.05 * jax.random.normal(k, shape, jnp.float32)

    cmp_in = CMP_BLOCK * NSA_HEAD_DIM
    return {
        'x': nrm(ks[0], (BATCH, SEQ, D_MODEL), 1.0),
        'attn_norm': gain(ks[1], (L, D_MODEL)),
        'w_in': nrm(ks[2], (L, D_MODEL, D_IN), D_MODEL ** -0.5),
        'nsa_q_norm': gain(ks[3], (L, NSA_HEAD_DIM)),
        'nsa_k_norm': gain(ks[4], (L, 3, NSA_HEAD_DIM)),
        'cmp_pos_k': nrm(ks[5], (L, CMP_BLOCK, NSA_HEAD_DIM), 0.1),
        'cmp_pos_v': nrm(ks[6], (L, CMP_BLOCK, NSA_HEAD_DIM), 0.1),
        'cmp_w1_k': nrm(ks[7], (L, cmp_in, CMP_HIDDEN), cmp_in ** -0.5),
        'cmp_w2_k': nrm(ks[8], (L, CMP_HIDDEN, NSA_HEAD_DIM), CMP_HIDDEN ** -0.5),
        'cmp_w1_v': nrm(ks[9], (L, cmp_in, CMP_HIDDEN), cmp_in ** -0.5),
        'cmp_w2_v': nrm(ks[10], (L, CMP_HIDDEN, NSA_HEAD_DIM), CMP_HIDDEN ** -0.5),
        'gla_w_gate2': nrm(ks[11], (L, GLA_GATE_RANK, GLA_QK_W), GLA_GATE_RANK ** -0.5),
        'gla_b_gate': nrm(ks[12], (L, GLA_QK_W), 0.1),
        'gla_out_norm': gain(ks[13], (L, GLA_DV)),
        'w_out': nrm(ks[14], (L, D_MIX, D_MODEL), D_MIX ** -0.5),
        'ffn_norm': gain(ks[15], (L, D_MODEL)),
        'w_up': nrm(ks[16], (L, D_MODEL, 2 * D_FF), D_MODEL ** -0.5),
        'conv_w': nrm(ks[17], (L, CONV_W, 2 * D_FF), CONV_W ** -0.5),
        'conv_b': nrm(ks[18], (L, 2 * D_FF), 0.02),
        'w_down': nrm(ks[19], (L, D_FF, D_MODEL), D_FF ** -0.5),
    }

def first_block(x, attn_norm, w_in, nsa_q_norm, nsa_k_norm, cmp_pos_k, cmp_pos_v, cmp_w1_k, cmp_w2_k,
              cmp_w1_v, cmp_w2_v, gla_w_gate2, gla_b_gate, gla_out_norm, w_out, ffn_norm, w_up,
              conv_w, conv_b, w_down):
    offs = [int(o) for o in np.cumsum(IN_SPLITS)[:-1]]
    h = x
    for l in range(DEPTH):
        z = rms_norm(h, attn_norm[l]) @ w_in[l]
        nq, nkv, ngate, gq, gk, gv, glr, gout = jnp.split(z, offs, axis=-1)
        o_nsa = nsa_mixer(nq, nkv, ngate, nsa_q_norm[l], nsa_k_norm[l], cmp_pos_k[l], cmp_pos_v[l],
                          cmp_w1_k[l], cmp_w2_k[l], cmp_w1_v[l], cmp_w2_v[l])
        o_gla = gla_mixer(gq, gk, gv, glr, gout, gla_w_gate2[l], gla_b_gate[l], gla_out_norm[l])
        h = h + jnp.concatenate([o_nsa, o_gla], axis=-1) @ w_out[l]
        u = causal_dwconv(rms_norm(h, ffn_norm[l]) @ w_up[l], conv_w[l], conv_b[l])
        gate, up = jnp.split(u, 2, axis=-1)
        h = h + (jax.nn.silu(gate) * up) @ w_down[l]
    return h


GRID_W = 64
D_CONV = 1024
CONV_WIDTH = 3
N_HEADS = 8
N_KV_HEADS = 2
HEAD_DIM = 128
AXIS_DIM = HEAD_DIM // 2
ROPE_THETA_2 = 10000.0
Q_BLOCK_2 = 128
D_Q = N_HEADS * HEAD_DIM
D_KV = N_KV_HEADS * HEAD_DIM
N_GROUPS = 8
EXPERTS_PER_GROUP = 8
N_EXPERTS = N_GROUPS * EXPERTS_PER_GROUP
TOP_K = 2
D_EXPERT = 512
MOE_BLOCK = 128
IN_SPLITS_2 = (D_CONV, D_CONV, D_CONV, D_Q, D_KV, D_KV, D_MODEL, D_MODEL)
D_IN_2 = D_CONV * 3 + D_Q + 2 * D_KV + 2 * D_MODEL


def rmsnorm(x, g):
    xf = x.astype(jnp.float32)
    y = xf * lax.rsqrt(jnp.mean(xf * xf, axis=-1, keepdims=True) + EPS)
    return (y * g.astype(jnp.float32)).astype(x.dtype)

def split_columns(p):
    parts, off = [], 0
    for w in IN_SPLITS_2:
        parts.append(p[..., off:off + w])
        off += w
    return parts

def axial_rope_tables(S):
    rows = S // GRID_W
    row = jnp.repeat(jnp.arange(rows, dtype=jnp.float32), GRID_W)
    col = jnp.tile(jnp.arange(GRID_W, dtype=jnp.float32), rows)
    inv = ROPE_THETA_2 ** (-jnp.arange(0, AXIS_DIM, 2, dtype=jnp.float32) / AXIS_DIM)
    ang = jnp.concatenate([row[:, None] * inv, col[:, None] * inv], axis=-1)
    return jnp.cos(ang), jnp.sin(ang)

def apply_rope(x, cos, sin):
    xf = x.astype(jnp.float32).reshape(*x.shape[:-1], HEAD_DIM // 2, 2)
    x0, x1 = xf[..., 0], xf[..., 1]
    c = cos[None, :, None, :]
    s = sin[None, :, None, :]
    out = jnp.stack([x0 * c - x1 * s, x0 * s + x1 * c], axis=-1)
    return out.reshape(x.shape).astype(x.dtype)

def bidirectional_gqa(q, k, v):
    B, S = q.shape[0], q.shape[1]
    G = N_HEADS // N_KV_HEADS
    nq = S // Q_BLOCK_2
    qb = q.reshape(B, nq, Q_BLOCK_2, N_KV_HEADS, G, HEAD_DIM).transpose(1, 0, 2, 3, 4, 5)

    def attend(qblk):
        s = jnp.einsum('bqkgd,bskd->bkgqs', qblk, k, preferred_element_type=jnp.float32)
        p = jax.nn.softmax(s, axis=-1)
        return jnp.einsum('bkgqs,bskd->bqkgd', p.astype(v.dtype), v)

    o = lax.map(attend, qb)
    return o.transpose(1, 0, 2, 3, 4, 5).reshape(B, S, D_Q)

def depthwise_conv_centred(z, w):
    rhs = w.reshape(CONV_WIDTH, 1, D_CONV)
    pad = (CONV_WIDTH - 1) // 2
    return lax.conv_general_dilated(z, rhs, window_strides=(1,), padding=((pad, pad),),
                                    dimension_numbers=('NWC', 'WIO', 'NWC'),
                                    feature_group_count=D_CONV)

def mixer_block(u, cos, sin, w_in, conv_w, q_norm_g, k_norm_g, w_conv_out, w_attn_out, w_o):
    B, S, _ = u.shape
    proj = u @ w_in
    cb, cc, cx, q, k, v, gc, ga = split_columns(proj)
    z = depthwise_conv_centred(cc * cx, conv_w)
    y_conv = (cb * z) @ w_conv_out
    q = rmsnorm(q.reshape(B, S, N_HEADS, HEAD_DIM), q_norm_g)
    k = rmsnorm(k.reshape(B, S, N_KV_HEADS, HEAD_DIM), k_norm_g)
    v = v.reshape(B, S, N_KV_HEADS, HEAD_DIM)
    q = apply_rope(q, cos, sin) * (HEAD_DIM ** -0.5)
    k = apply_rope(k, cos, sin)
    y_attn = bidirectional_gqa(q, k, v) @ w_attn_out
    merged = jax.nn.sigmoid(gc) * y_conv + jax.nn.sigmoid(ga) * y_attn
    return merged @ w_o

def hier_moe(u, w_group, w_router, w1, w3, w2):
    B, S, D = u.shape
    T = B * S
    hf = u.reshape(T, D)
    grp_logits = (hf @ w_group).astype(jnp.float32)
    grp_prob = jax.nn.softmax(grp_logits, axis=-1)
    g = jnp.argmax(grp_logits, axis=-1)
    pg = jnp.take_along_axis(grp_prob, g[:, None], axis=1)
    exp_logits = (hf @ w_router).astype(jnp.float32).reshape(T, N_GROUPS, EXPERTS_PER_GROUP)
    sel = jnp.take_along_axis(exp_logits, g[:, None, None], axis=1)[:, 0]
    top_v, top_i = lax.top_k(sel, TOP_K)
    weights = pg * jax.nn.softmax(top_v, axis=-1)
    expert_ids = g[:, None] * EXPERTS_PER_GROUP + top_i
    A = T * TOP_K
    e_flat = expert_ids.reshape(A).astype(jnp.int32)
    w_flat = weights.reshape(A)
    tok_flat = jnp.arange(A, dtype=jnp.int32) // TOP_K
    order = jnp.argsort(e_flat)
    se, st, sw = e_flat[order], tok_flat[order], w_flat[order]
    counts = jnp.bincount(e_flat, length=N_EXPERTS).astype(jnp.int32)
    starts = jnp.cumsum(counts) - counts
    pcounts = ((counts + MOE_BLOCK - 1) // MOE_BLOCK) * MOE_BLOCK
    pends = jnp.cumsum(pcounts)
    pstarts = pends - pcounts
    dest = pstarts[se] + (jnp.arange(A, dtype=jnp.int32) - starts[se])
    P = A + N_EXPERTS * MOE_BLOCK
    NB = P // MOE_BLOCK
    row_tok = jnp.full((P,), T, jnp.int32).at[dest].set(st)
    row_w = jnp.zeros((P,), jnp.float32).at[dest].set(sw)
    blk_expert = jnp.minimum(
        jnp.searchsorted(pends, jnp.arange(NB, dtype=jnp.int32) * MOE_BLOCK, side='right'),
        N_EXPERTS - 1).astype(jnp.int32)
    x_pad = jnp.concatenate([hf, jnp.zeros((1, D), hf.dtype)], axis=0)
    xs = x_pad[row_tok].reshape(NB, MOE_BLOCK, D)

    def expert_block(args):
        xb, e = args
        return (jax.nn.silu(xb @ w1[e]) * (xb @ w3[e])) @ w2[e]

    ys = lax.map(expert_block, (xs, blk_expert)).reshape(P, D)
    ys = ys * row_w[:, None].astype(ys.dtype)
    out = jnp.zeros((T + 1, D), ys.dtype).at[row_tok].add(ys)[:T]
    return out.reshape(B, S, D)

def second_inputs(seed: int = 0) -> dict:
    key = jax.random.key(seed)
    ks = jax.random.split(key, 16)

    def nrm(k, shape, scale):
        return jax.random.normal(k, shape, jnp.float32) * scale

    return {
        "x": nrm(ks[0], (BATCH, SEQ, D_MODEL), 1.0),
        "norm1_g": 1.0 + nrm(ks[1], (DEPTH, D_MODEL), 0.02),
        "w_in": nrm(ks[2], (DEPTH, D_MODEL, D_IN_2), D_MODEL ** -0.5),
        "conv_w": nrm(ks[3], (DEPTH, CONV_WIDTH, D_CONV), CONV_WIDTH ** -0.5),
        "q_norm_g": 1.0 + nrm(ks[4], (DEPTH, HEAD_DIM), 0.02),
        "k_norm_g": 1.0 + nrm(ks[5], (DEPTH, HEAD_DIM), 0.02),
        "w_conv_out": nrm(ks[6], (DEPTH, D_CONV, D_MODEL), D_CONV ** -0.5),
        "w_attn_out": nrm(ks[7], (DEPTH, D_Q, D_MODEL), D_Q ** -0.5),
        "w_o": nrm(ks[8], (DEPTH, D_MODEL, D_MODEL), D_MODEL ** -0.5),
        "norm2_g": 1.0 + nrm(ks[9], (DEPTH, D_MODEL), 0.02),
        "w_group": nrm(ks[10], (DEPTH, D_MODEL, N_GROUPS), D_MODEL ** -0.5),
        "w_router": nrm(ks[11], (DEPTH, D_MODEL, N_EXPERTS), D_MODEL ** -0.5),
        "w1": nrm(ks[12], (DEPTH, N_EXPERTS, D_MODEL, D_EXPERT), D_MODEL ** -0.5),
        "w3": nrm(ks[13], (DEPTH, N_EXPERTS, D_MODEL, D_EXPERT), D_MODEL ** -0.5),
        "w2": nrm(ks[14], (DEPTH, N_EXPERTS, D_EXPERT, D_MODEL), D_EXPERT ** -0.5),
    }

def second_block(x, norm1_g, w_in, conv_w, q_norm_g, k_norm_g, w_conv_out, w_attn_out, w_o,
              norm2_g, w_group, w_router, w1, w3, w2):
    S = x.shape[1]
    cos, sin = axial_rope_tables(S)
    h = x
    for l in range(DEPTH):
        h = h + mixer_block(rmsnorm(h, norm1_g[l]), cos, sin, w_in[l], conv_w[l],
                            q_norm_g[l], k_norm_g[l], w_conv_out[l], w_attn_out[l], w_o[l])
        h = h + hier_moe(rmsnorm(h, norm2_g[l]), w_group[l], w_router[l], w1[l], w3[l], w2[l])
    return h


def setup_inputs(seed=0):
    out = dict(first_inputs(seed))
    for name, value in second_inputs(seed + 1).items():
        if name != "x":
            out[name + "_2"] = value
    return out


def reference(
    x, attn_norm, w_in, nsa_q_norm, nsa_k_norm, cmp_pos_k, cmp_pos_v, cmp_w1_k, cmp_w2_k,
    cmp_w1_v, cmp_w2_v, gla_w_gate2, gla_b_gate, gla_out_norm, w_out, ffn_norm, w_up, conv_w,
    conv_b, w_down, norm1_g_2, w_in_2, conv_w_2, q_norm_g_2, k_norm_g_2, w_conv_out_2,
    w_attn_out_2, w_o_2, norm2_g_2, w_group_2, w_router_2, w1_2, w3_2, w2_2,
):
    x = first_block(
        x, attn_norm, w_in, nsa_q_norm, nsa_k_norm, cmp_pos_k, cmp_pos_v, cmp_w1_k, cmp_w2_k,
        cmp_w1_v, cmp_w2_v, gla_w_gate2, gla_b_gate, gla_out_norm, w_out, ffn_norm, w_up,
        conv_w, conv_b, w_down,
    )
    return second_block(
        x, norm1_g_2, w_in_2, conv_w_2, q_norm_g_2, k_norm_g_2, w_conv_out_2, w_attn_out_2,
        w_o_2, norm2_g_2, w_group_2, w_router_2, w1_2, w3_2, w2_2,
    )


_drawn_inputs = setup_inputs


def setup_inputs(seed=0):
    import zlib

    import numpy as np

    out = dict(_drawn_inputs(seed))
    spreads = {}
    factors = {'nsa_q_norm': 3.837,
     'nsa_k_norm': 4.188,
     'cmp_pos_k': 5.382,
     'norm1_g_2': 2.675,
     'q_norm_g_2': 8.0,
     'k_norm_g_2': 8.0,
     'norm2_g_2': 3.097}
    for name, (base, spread) in spreads.items():
        noise = np.random.default_rng([zlib.crc32(name.encode()), seed]).standard_normal(out[name].shape)
        drawn = base * np.exp(spread * noise) if base else spread * noise
        out[name] = __import__('jax').numpy.asarray(drawn.astype(out[name].dtype))
    for name, factor in factors.items():
        out[name] = (out[name] * factor).astype(out[name].dtype)
    return out
```

```python
from contextlib import ExitStack

import numpy as np
import concourse.bass as bass
from concourse import mybir

F32 = mybir.dt.float32
I32 = mybir.dt.int32
U32 = mybir.dt.uint32
ALU = mybir.AluOpType
ACT = mybir.ActivationFunctionType
AX = mybir.AxisListType

P = 128
S = 256
D = 1024
KC = D // P
EPS = 1e-6
NEG = -1e30

QH, HD, G = 8, 64, 2
NCMP, CMP_STRIDE, CMP_BLOCK = 15, 16, 32
GH, GDK, GDV, L = 4, 64, 128, 64
TAU = 16.0
FF = 2816
FCH = FF // P
QKV0, KV0, GATE0, GQ0, GV0, GLR0, GOUT0 = 0, 512, 1280, 1304, 1816, 2328, 2344
D_IN = 2856

H2, HD2 = 8, 128
D_IN2 = 6656
CB0, CC0, CX0, Q20, KV20, GC0, GA0 = 0, 1024, 2048, 3072, 4096, 4608, 5632
NE, NG, EPG, DE = 64, 8, 8, 512
CAP = 32
ROUNDS = S // CAP
GRP = P // CAP

CONST_COLS = dict(ident=P, causal3=3 * P, chunk_mask=P, before=P, ones=P, slot_iota=P, iota64=NE,
                  cos1=16, sin1=16, cosc=8, sinc=8, cmp_bias=2 * NCMP, cmp_keep=2 * NCMP,
                  cos2=2 * 64, sin2=2 * 64)
CONST_AT, _n = {}, 0
for _k, _w in CONST_COLS.items():
    CONST_AT[_k] = (_n, _n + _w)
    _n += _w
N_CONST = _n


def shape_constants():
    c = np.zeros((P, N_CONST), np.float32)

    def put(name, a):
        a = np.asarray(a, np.float32)
        a = a.reshape(a.shape[0], -1)
        lo, hi = CONST_AT[name]
        c[:a.shape[0], lo:hi] = a

    i = np.arange(P)
    put("ident", np.eye(P))
    diag = np.where(i[None, :] <= i[:, None], 0.0, NEG)
    put("causal3", np.stack([diag, np.zeros((P, P)), diag], 1))
    put("chunk_mask", (i[:, None] <= i[None, :]) & (i[:, None] // L == i[None, :] // L))
    put("before", i[:, None] < i[None, :])
    put("ones", np.ones((P, P)))
    put("slot_iota", np.broadcast_to(np.tile(np.arange(CAP), GRP), (P, P)))
    put("iota64", np.broadcast_to(np.arange(NE), (P, NE)))
    f = np.float32
    inv = f(500000.0) ** (-np.arange(8, dtype=f) / f(8))
    tok = (np.arange(2)[None, :] * P + i[:, None]).astype(f)
    ang = (tok[:, :, None] * inv).astype(f)
    put("cos1", np.cos(ang))
    put("sin1", np.sin(ang))
    end = (np.arange(NCMP) * CMP_STRIDE + CMP_BLOCK - 1).astype(f)
    angc = (end[:, None] * inv).astype(f)
    put("cosc", np.cos(angc))
    put("sinc", np.sin(angc))
    seen = end[None, None, :] <= tok[:, :, None]
    put("cmp_bias", np.where(seen, 0.0, NEG))
    put("cmp_keep", seen)
    inv2 = f(10000.0) ** (-np.arange(0, 64, 2, dtype=f) / f(64))
    row, col = np.floor(tok / 64), tok % 64
    ang2 = np.concatenate([(row[:, :, None] * inv2), (col[:, :, None] * inv2)], -1).astype(f)
    put("cos2", np.cos(ang2))
    put("sin2", np.sin(ang2))
    return c


UNITS = ["cmp_in", "kv_tok", "q_tok", "cmp1k", "cmp1v", "gqk", "gv", "gout", "wout0", "wout1"]
U_FFN = len(UNITS)
for _i in range(FCH // 2):
    UNITS += [f"up{_i}", f"down{_i}"]
U_BLK2 = len(UNITS)
UNITS += ["q0", "q1", "kv2", "cc0", "cx0", "cb0", "cc1", "cx1", "cb1",
          "gc0", "wco0", "ga0", "wao0", "gc1", "wco1", "ga1", "wao1", "wo0", "wo1"]
UNIT = {n: i for i, n in enumerate(UNITS)}
RING = 4

PRODUCTS = [("cmp_in", "DA"), ("kv_tok", "DA"), ("q_tok", "DA"), ("gqk", "DA"), ("gv", "DA"),
            ("gout", "AA"), ("wout0", "DD"), ("wout1", "DD"),
            ("q0", "DA"), ("q1", "DA"), ("kv2", "DA"),
            ("cc0", "AA"), ("cx0", "DD"), ("cb0", "DD"), ("cc1", "AA"), ("cx1", "DD"), ("cb1", "DD"),
            ("gc0", "AA"), ("wco0", "DD"), ("ga0", "AA"), ("wao0", "DD"),
            ("gc1", "AA"), ("wco1", "DD"), ("ga1", "AA"), ("wao1", "DD"), ("wo0", "DD"), ("wo1", "DD")]
PROD = {n: i for i, (n, _) in enumerate(PRODUCTS)}


def emptied(engine, step, bank):
    flat = "".join(e for _, e in PRODUCTS[:step]) + PRODUCTS[step][1][:bank + 1]
    return flat.count(engine)


def filled(step, bank):
    return 2 * step + bank + 1


ATTN_STEPS = H2 + 2
SCHEDULE2, _k = [], 0
for _n in ("q0", "q1", "kv2", "cc0", "cx0"):
    SCHEDULE2 += [("part", _n, _q) for _q in range(4)]
SCHEDULE2.append(("turn", 0, 0))
for _n in ("cb0", "cc1", "cx1", "cb1"):
    for _q in range(4):
        SCHEDULE2.append(("part", _n, _q))
        if _k < ATTN_STEPS:
            SCHEDULE2.append(("attn", _k, 0))
            _k += 1
for _n in ("gc0", "wco0", "ga0", "wao0", "gc1", "wco1", "ga1", "wao1", "wo0", "wo1"):
    SCHEDULE2 += [("part", _n, _q) for _q in range(4)]


def two_blocks(nc, t, out):
    with ExitStack() as ctx:
        def sb(name, shape, dt=F32):
            return ctx.enter_context(nc.sbuf_tensor(name, shape, dt))

        def sem(name):
            return ctx.enter_context(nc.semaphore(name))

        ps = ctx.enter_context(nc.psum_tensor("ps", [P, 8, 512], F32))
        dense_ring = sb("dense_ring", [P, RING, 4096])
        expert_ring = sb("expert_ring", [P, 2, 3, 4096])
        h = sb("h", [P, 2, D])
        hT = sb("hT", [P, KC, S])
        consts = sb("consts", [P, N_CONST])
        chunk_mask = sb("chunk_mask", [P, P], U32)
        gains = sb("gains", [P, 64 + 192 + 128 + 128 + D])
        gcol = sb("gcol", [P, 3, KC])
        prm_rows = sb("prm_rows", [P, 2, P])
        prm = sb("prm", [P, 2, P])
        router_w = sb("router_w", [P, KC, NG + NE])
        wgate2 = sb("wgate2", [P, S])
        cmp_w2 = sb("cmp_w2", [P, 2, 2, HD])
        ssq = sb("ssq", [P, 2])
        msq = sb("msq", [P, 2])
        rms = sb("rms", [P, 2])
        rstd = sb("rstd", [P, 2])
        tail = sb("tail", [P, 64])

        def const(name, rows=P):
            lo, hi = CONST_AT[name]
            return consts[0:rows, lo:hi]

        def by_pairs(z):
            return z.rearrange("p (j g d) -> p g j d", g=G, j=4)

        def gla_index(head, half):
            return (head % 2) * 4 + (head // 2) * 2 + half

        ident = const("ident")
        q_gain1, k_gains1 = gains[:, 0:64], gains[:, 64:256]
        q_gain2, k_gain2, norm_gain2 = gains[:, 256:384], gains[:, 384:512], gains[:, 512:512 + D]
        pe_kT, pe_vT, b_gateT = prm[:, 0, 88:104], prm[:, 0, 104:120], prm[:, 0, 120:122]
        out_gainT = prm[:, 1, 112:113]

        flat0 = expert_ring[:, 0, :, :].rearrange("p a b -> p (a b)")
        flat1 = expert_ring[:, 1, :, :].rearrange("p a b -> p (a b)")
        flatd = dense_ring[:, :, :].rearrange("p a b -> p (a b)")

        def carve(flat):
            at = [0]

            def take(*shape):
                n = int(np.prod(shape))
                v = flat[:, at[0]:at[0] + n]
                at[0] += n
                assert at[0] <= flat.shape[1]
                if len(shape) == 2:
                    v = v.rearrange("p (a b) -> p a b", a=shape[0])
                elif len(shape) == 3:
                    v = v.rearrange("p (a b c) -> p a b c", a=shape[0], b=shape[1])
                return v
            return take

        s0 = carve(flat0)
        zq, zkv, ckv = s0(2, 512), s0(2, 512), s0(256)
        sq1 = s0(2, 1024)
        qT, kT, kcT = s0(4, S), s0(2, S), s0(16)
        rope_tmp = s0(4, 64)
        kk = s0(2, 3, S)
        hid_bias = s0(4)
        gelu_h = s0(2, 2, 30)
        ss1, r1 = s0(26), s0(26)
        gates = s0(2, 24)
        s_buf = s0(2, 798)
        pT = s0(2, 1024)
        mx, nmx, sums, wts = s0(2, 8), s0(2, 8), s0(2, 8), s0(2, 8)
        s1 = carve(flat1)
        xn = s1(2, D)
        glrT, gq, gk = s1(S), s1(2, S), s1(2, S)
        gla_tmp = s1(4, S)
        gt, ga_ = gla_tmp[:, 0:2, :], gla_tmp[:, 2:4, :]
        gl_, cum, e_pos, e_neg, khatT = (s1(2, S) for _ in range(5))
        blast, decay = s1(2, 4), s1(2, 4)
        qt, kt, khat = s1(2, S), s1(2, S), s1(2, S)
        gv, sil = s1(2, 512), s1(4, S)
        attT = s1(8, P)
        state = gla_tmp.rearrange("p a b -> p (a b)")[:, 0:768].rearrange("p (a b c) -> p a b c", a=2, b=3)
        ogla_ss, ogla_r = s1(8), s1(8)
        oT = hT
        ogla, osq = xn[:, 0, :], xn[:, 1, :]
        f0 = carve(flat0)
        conv_y = f0(2, 2, S)
        sil_g = f0(2, S)
        act_T = f0(2, S)
        b0 = carve(flat0)
        z2 = b0(2, 1280)
        v2 = b0(2, 256)
        sq2 = b0(2, 1280)
        q2T, k2T = b0(H2, S), b0(2, S)
        p2 = b0(2, 512)
        p2T = b0(2, 512)
        mx2, nmx2, sum2, rs2 = b0(2, 2), b0(2, 2), b0(2, 2), b0(2, 2)
        ss2, r2 = b0(20), b0(20)
        b1 = carve(flat1)
        xn2 = b1(2, D)
        cc_s, u_s, z_s = b1(4, S), b1(4, S), b1(4, S)
        cbz, o2T = b1(KC, S), b1(KC, S)
        sg, sg2 = b1(4, S), b1(4, S)
        mtmp = b1(512)
        mrg = xn2.rearrange("p a b -> p (a b)").rearrange("p (c s) -> p c s", c=KC)
        m0 = carve(flatd)
        uN = m0(2, D)
        lg = m0(2, NG + NE)
        g8, e8 = m0(2, 8), m0(2, 8)
        gi8u, ei8u = m0(2, 8).bitcast(U32), m0(2, 8).bitcast(U32)
        gi8, ei8 = m0(2, 8), m0(2, 8)
        gexp, gsum, pg = m0(2, 8), m0(2, 1), m0(2, 1)
        goh, gohb = m0(2, 8), m0(2, 8)
        elm = m0(2, NE)
        dv, ex, den, rden, w1t, w2t, ngm = (m0(2, 1) for _ in range(7))
        oh1, oh2, assign, wmat = (m0(2, NE) for _ in range(4))
        slot = m0(2, NE)
        cnt = m0(NE)
        cmax_f = m0(1)
        cmax = m0(1).bitcast(I32)
        sel, selw = m0(2, P), m0(2, P)
        selwT = m0(S)
        xg = m0(KC, P)
        hsil, hid = m0(2, DE), m0(2, DE)
        aT = m0(2, P)
        y = m0(D)
        xn_moe = m0(2, D)

        consts_in, x_in, rows_in, gains_in = sem("consts_in"), sem("x_in"), sem("rows_in"), sem("gains_in")
        small_in, out_done = sem("small_in"), sem("out_done")
        dense_loaded = [sem(f"dense_loaded{i}") for i in range(RING)]
        dense_used = sem("dense_used")
        up_loaded = [sem(f"up_loaded{i}") for i in range(2)]
        dn_loaded = [sem(f"dn_loaded{i}") for i in range(2)]
        up_free, dn_free = sem("up_free"), sem("dn_free")
        dve_step, act_step = sem("dve_step"), sem("act_step")
        zeroed = sem("zeroed")
        prm_turned, prm_ready = sem("prm_turned"), sem("prm_ready")
        h_ready = sem("h_ready")
        ssq_ready, msq_ready, rms_ready, rstd_ready = (sem(n) for n in ("ssq_ready", "msq_ready", "rms_ready", "rstd_ready"))
        xn_dve, xn_act = sem("xn_dve"), sem("xn_act")
        xT_turned, hT_dve, hT_act = sem("xT_turned"), sem("hT_dve"), sem("hT_act")
        bank_filled, bank_emptied_dve, bank_emptied_act = sem("bank_filled"), sem("bank_emptied_dve"), sem("bank_emptied_act")
        emptied_sem = {"D": bank_emptied_dve, "A": bank_emptied_act}
        cmp_hidden, cmp_bias_ready, gelu_ready, cmp_kv_ready = (sem(n) for n in ("cmp_hidden", "cmp_bias_ready", "gelu_ready", "cmp_kv_ready"))
        sq_q, ms_heads, rms_heads = sem("sq_q"), sem("ms_heads"), sem("rms_heads")
        roped, qk_turned, qkT_dve, qkT_act = (sem(n) for n in ("roped", "qk_turned", "qkT_dve", "qkT_act"))
        gate_logits, gate_abs, gate_log, cum_ready = (sem(n) for n in ("gate_logits", "gate_abs", "gate_log", "cum_ready"))
        exps_ready, gla_qk_ready, khat_ready, khat_turned, khat_rows = (sem(n) for n in ("exps_ready", "gla_qk_ready", "khat_ready", "khat_turned", "khat_rows"))
        att_filled, att_masked, ds_filled, states_ready = (sem(n) for n in ("att_filled", "att_masked", "ds_filled", "states_ready"))
        gla_o, gla_sq, gla_ms, gla_rms, gla_on, gla_turned, gla_oT = (sem(n) for n in ("gla_o", "gla_sq", "gla_ms", "gla_rms", "gla_on", "gla_turned", "gla_oT"))
        scores1, nmx1, exp1, scaled1, turned1, pT1_dve, pT1_act, o1, oT1 = (sem(n) for n in (
            "scores1", "nmx1", "exp1", "scaled1", "turned1", "pT1_dve", "pT1_act", "o1", "oT1"))
        ff_filled, ff_read_act, ff_read_dve, ff_gated, ff_silu, ff_act = (sem(n) for n in (
            "ff_filled", "ff_read_act", "ff_read_dve", "ff_gated", "ff_silu", "ff_act"))
        ff_down, ff_added, ffn_chain = sem("ff_down"), sem("ff_added"), sem("ffn_chain")
        cc_ready, conv_in, conv_mid, cbz_ready = (sem(n) for n in ("cc_ready", "conv_in", "conv_mid", "cbz_ready"))
        sq2_ready, ms2_ready, rms2_ready, roped2, turned_q2, q2T_dve, q2T_act = (sem(n) for n in (
            "sq2_ready", "ms2_ready", "rms2_ready", "roped2", "turned_q2", "q2T_dve", "q2T_act"))
        scores2, nmx_2, exp2, scaled2, turned2, pT2, o2, o2T_ready = (sem(n) for n in (
            "scores2", "nmx_2", "exp2", "scaled2", "turned2", "pT2", "o2", "o2T_ready"))
        sig_ready, merged = sem("sig_ready"), sem("merged")
        logits_ready, lg_ready, grp_nmax, grp_exp, top_diff, top_exp = (sem(n) for n in (
            "logits_ready", "lg_ready", "grp_nmax", "grp_exp", "top_diff", "top_exp"))
        assigned, ranks_ready, slots_ready = sem("assigned"), sem("ranks_ready"), sem("slots_ready")
        sel_ready, selw_turned, selwT_ready = sem("sel_ready"), sem("selw_turned"), sem("selwT_ready")
        gathered, xg_dve, xg_act, up_filled, silu_ready, act_ready, hid_turned, aT_ready = (sem(n) for n in (
            "gathered", "xg_dve", "xg_act", "up_filled", "silu_ready", "act_ready", "hid_turned", "aT_ready"))
        y_filled, y_dve, y_act, scattered, summed = (sem(n) for n in ("y_filled", "y_dve", "y_act", "scattered", "summed"))
        moe_step, moe_round = sem("moe_step"), sem("moe_round")
        last_ready = sem("last_ready")

        block = ctx.enter_context(nc.Block())

        def w_in_view(w, c0, n):
            return t[w][:, c0:c0 + n].rearrange("(p c) n -> p c n", c=KC)

        def w_nat_view(w, c0, n):
            return t[w][:, c0:c0 + n].rearrange("(c p) n -> p c n", p=P)

        def unit_loads(name, slot):
            full = dense_ring[:, slot, :].rearrange("p (c n) -> p c n", c=KC)
            cols2 = {"q": Q20, "cc": CC0, "cx": CX0, "cb": CB0, "gc": GC0, "ga": GA0}
            if name == "cmp_in":
                return [(full[:, :, 0:256], w_in_view("w_in", KV0, 256)),
                        (full[:, :, 256:280], w_in_view("w_in", GATE0, 24)),
                        (full[:, :, 280:296], w_in_view("w_in", GLR0, 16))]
            if name in ("kv_tok", "q_tok", "gqk", "gv", "gout"):
                c0 = {"kv_tok": KV0 + 256, "q_tok": QKV0, "gqk": GQ0, "gv": GV0, "gout": GOUT0}[name]
                return [(full, w_in_view("w_in", c0, 512))]
            if name in ("cmp1k", "cmp1v"):
                src = t["cmp_w1_k" if name == "cmp1k" else "cmp_w1_v"]
                return [(dense_ring[:, slot, :].rearrange("p (c n) -> p c n", n=256),
                         src.rearrange("(c p) n -> p c n", p=P))]
            m = int(name[-1])
            if name[:-1] == "kv":
                return [(full, w_in_view("w_in_2", KV20, 512))]
            if name[:-1] in cols2:
                return [(full, w_in_view("w_in_2", cols2[name[:-1]] + 512 * m, 512))]
            src = {"wout": "w_out", "wco": "w_conv_out_2", "wao": "w_attn_out_2", "wo": "w_o_2"}[name[:-1]]
            return [(full, w_nat_view(src, 512 * m, 512))]

        @block.sync
        def _(sp):
            for half in range(2):
                sp.dma_start(h[:, half, :], t["x"][half * P:(half + 1) * P, :]).then_inc(x_in, 16)

            def static_units(lo, hi):
                for u in range(lo, hi):
                    if u >= RING:
                        sp.wait_ge(dense_used, u - RING + 1)
                    for dst, src in unit_loads(UNITS[u], u % RING):
                        sp.dma_start(dst, src).then_inc(dense_loaded[u % RING], 16)

            static_units(0, 1)
            sp.dma_start(consts[:], t["consts"]).then_inc(consts_in, 16)
            static_units(1, U_FFN)

            w_up = t["w_up"].rearrange("(p c) n -> p c n", c=KC)
            w_down = t["w_down"].rearrange("(a p) n -> p a n", p=P)

            def ffn_unit(k, s, base):
                up_slot, dn_slot = (U_FFN + 2 * s) % RING, (U_FFN + 2 * s + 1) % RING
                up = dense_ring[:, up_slot, :].rearrange("p (c g n) -> p c g n", c=KC, g=2)
                sp.wait_ge(dense_used, base)
                for g in range(2):
                    sp.dma_start(up[:, :, g, :], w_up[:, :, bass.ds(g * FF + k * 256, 256)]
                                 ).then_inc(dense_loaded[up_slot], 8 * 2)
                dn = dense_ring[:, dn_slot, 0:2048].rearrange("p (a n) -> p a n", a=2)
                sp.wait_ge(dense_used, base + 1)
                sp.dma_start(dn, w_down[:, bass.ds(k * 2, 2), :]).then_inc(dense_loaded[dn_slot], 16)

            with nc.sync.Fori(0, FCH // 4) as i:
                for s in range(2):
                    ffn_unit(2 * i + s, s, U_FFN + 4 * i + 2 * s - RING + 1)
            ffn_unit(FCH // 2 - 1, 0, U_FFN + FCH - 2 - RING + 1)
            static_units(U_BLK2, len(UNITS))

            def expert_loads(it, j):
                e = (it % (NE // GRP)) * GRP + j
                sp.wait_ge(up_free, it * GRP + j + 1)
                for k, w in ((0, "w1"), (1, "w3")):
                    sp.dma_start(expert_ring[:, j % 2, k, :],
                                 t[w][bass.ds(e, 1), :, :].rearrange("o p n -> p (o n)")
                                 ).then_inc(up_loaded[j % 2], 16)
                sp.wait_ge(dn_free, it * GRP + j + 1)
                sp.dma_start(expert_ring[:, j % 2, 2, :],
                             t["w2"][bass.ds(e, 1), :, :].rearrange("o p n -> p (o n)")
                             ).then_inc(dn_loaded[j % 2], 16)

            with nc.sync.Fori(0, NE // GRP) as it:
                for j in range(GRP):
                    expert_loads(it, j)
            sp.wait_ge(slots_ready, 1)
            fullest = nc.sync.value_load(cmax[0:1, 0:1], min_val=0, max_val=S)
            with nc.sync.Fori(1, ROUNDS) as r:
                with nc.sync.If(fullest > r * CAP):
                    with nc.sync.Fori(0, NE // GRP) as g:
                        for j in range(GRP):
                            expert_loads(r * (NE // GRP) + g, j)
            sp.wait_ge(last_ready, 1)
            for half in range(2):
                sp.dma_start(out[half * P:(half + 1) * P, :], h[:, half, :]).then_inc(out_done, 16)
            sp.wait_ge(out_done, 32)

        @block.gpsimd
        def _(pool):
            A = prm_rows[:, 0, :]
            B = prm_rows[:, 1, :]
            cw = t["conv_w"].rearrange("k (c n) -> (k c) n", n=P)
            for dst, src in ((A[0:88, :], cw[0:88, :]), (A[88:104, :], t["pe_k"].rearrange("(a b) n -> a (b n)", b=2)),
                             (A[104:120, :], t["pe_v"].rearrange("(a b) n -> a (b n)", b=2)),
                             (A[120:122, :], t["b_gate"].rearrange("o (c n) -> (o c) n", n=P)),
                             (B[0:44, :], cw[88:132, :]),
                             (B[44:88, :], t["conv_b"].rearrange("o (c n) -> (o c) n", n=P)),
                             (B[88:112, :], t["conv_w_2"].rearrange("k (c n) -> (k c) n", n=P)),
                             (B[112:113, :], t["gla_out_norm"])):
                pool.dma_start(dst, src).then_inc(rows_in, 16)
            for i, n in enumerate(("attn_norm", "ffn_norm", "norm1_g_2")):
                pool.dma_start(gcol[:, i, :], t[n].rearrange("o (p c) -> p (o c)", c=KC)).then_inc(small_in, 16)
            pool.dma_start(wgate2[0:16, :], t["gla_w_gate2"]).then_inc(small_in, 16)
            for i, n in enumerate(("cmp_w2_k", "cmp_w2_v")):
                pool.dma_start(cmp_w2[:, i, :, :], t[n].rearrange("(m p) d -> p m d", p=P)).then_inc(small_in, 16)
            pool.dma_start(router_w[:, :, 0:NG], t["w_group_2"].rearrange("(p c) n -> p c n", c=KC)).then_inc(small_in, 16)
            pool.dma_start(router_w[:, :, NG:], t["w_router_2"].rearrange("(p c) n -> p c n", c=KC)).then_inc(small_in, 16)
            for dst, n in ((q_gain1, "nsa_q_norm"), (k_gains1, "nsa_k_norm"), (q_gain2, "q_norm_g_2"),
                           (k_gain2, "k_norm_g_2"), (norm_gain2, "norm2_g_2")):
                pool.dma_start(dst, t[n].rearrange("a b -> (a b)").partition_broadcast(P)).then_inc(gains_in, 16)

        ROWS_IN, SMALL_IN, GAINS_IN = 16 * 8, 16 * 8, 16 * 5

        @block.tensor
        def _(pe):
            mm = nc.tensor.matmul
            turn = nc.tensor.transpose

            def slot_view(u):
                return dense_ring[:, u % RING, :].rearrange("p (c n) -> p c n", c=KC)

            def norm_turn(k, src):
                pe.wait_ge(xn_dve, k + 1)
                pe.wait_ge(xn_act, k + 1)
                if k == 0:
                    pe.wait_ge(consts_in, 16)
                view = src.rearrange("p a (n c) -> p a c n", c=KC)
                for c in range(KC):
                    for half in range(2):
                        last = turn(ps[:, c // 2, (c % 2) * S + half * P:(c % 2) * S + (half + 1) * P],
                                    view[:, half, c, :], ident)
                    if c % 2:
                        last.then_inc(xT_turned, 1)

            def wait_hT(k):
                pe.wait_ge(hT_dve, 4 * (k + 1))
                pe.wait_ge(hT_act, 4 * (k + 1))

            def wait_bank(step, bank):
                if step >= 2:
                    eng = PRODUCTS[step - 2][1][bank]
                    pe.wait_ge(emptied_sem[eng], emptied(eng, step - 2, bank))

            def part(name, xT, rows, q):
                u, step = UNIT[name], PROD[name]
                w = slot_view(u)
                if q == 0:
                    pe.wait_ge(dense_loaded[u % RING], dense_value(u))
                pair = 2 * (step % 2)
                bank = q // 2
                if q % 2 == 0:
                    wait_bank(step, bank)
                if rows:
                    for c in range(4 * (q % 2), 4 * (q % 2) + 4):
                        last = mm(ps[:, pair + bank, :], xT[:, c, bank * P:(bank + 1) * P], w[:, c, :],
                                  start=(c == 0), stop=(c == KC - 1))
                else:
                    o = ps[:, pair + bank, (q % 2) * S:(q % 2 + 1) * S]
                    for c in range(KC):
                        last = mm(o, w[:, c, q * P:(q + 1) * P], xT[:, c, :], start=(c == 0), stop=(c == KC - 1))
                if q % 2 == 1:
                    last.then_inc(bank_filled, 1)
                if q == 3:
                    pe.wait_ge(bank_filled, filled(step, 1))
                    pe.sem_inc(dense_used, 1)

            def dense_value(u):
                n = 0
                for v in range(u % RING, u + 1, RING):
                    n += 3 if v == 0 else 2 if UNITS[v].startswith("up") else 1
                return 16 * n

            pe.wait_ge(rows_in, ROWS_IN)
            pe.wait_ge(consts_in, 16)
            turn(ps[:, 7, 0:122], prm_rows[0:122, 0, :], ident[0:122, 0:122])
            turn(ps[:, 7, 128:241], prm_rows[0:113, 1, :], ident[0:113, 0:113]).then_inc(prm_turned, 1)

            norm_turn(0, xn)
            wait_hT(0)
            u, w = UNIT["cmp_in"], slot_view(UNIT["cmp_in"])
            pe.wait_ge(dense_loaded[u % RING], dense_value(u))
            for i in range(2):
                for c in range(KC):
                    last = mm(ps[:, 0, i * S:(i + 1) * S], w[:, c, i * P:(i + 1) * P], hT[:, c, :],
                              start=(c == 0), stop=(c == KC - 1))
            last.then_inc(bank_filled, 1)
            for half in range(2):
                for c in range(KC):
                    mm(ps[:, 1, half * 24:(half + 1) * 24], hT[:, c, half * P:(half + 1) * P], w[:, c, 256:280],
                       start=(c == 0), stop=(c == KC - 1))
            for c in range(KC):
                last = mm(ps[0:16, 1, P:P + S], w[:, c, 280:296], hT[:, c, :], start=(c == 0), stop=(c == KC - 1))
            last.then_inc(bank_filled, 1)
            pe.wait_ge(bank_filled, filled(0, 1))
            pe.sem_inc(dense_used, 1)
            for q in range(4):
                part("kv_tok", hT, True, q)
            pe.wait_ge(small_in, SMALL_IN)
            pe.wait_ge(bank_emptied_act, 1)
            pe.wait_ge(prm_ready, 1)
            for c in range(2):
                last = mm(ps[:, 7, c * S:(c + 1) * S], wgate2[0:16, c * P:(c + 1) * P], glrT[0:16, :],
                          start=True, stop=True)
            last.then_inc(gate_logits, 1)
            for q in range(4):
                part("q_tok", hT, True, q)

            pe.wait_ge(bank_emptied_dve, 1)
            for i, name in enumerate(("cmp1k", "cmp1v")):
                u = UNIT[name]
                w = dense_ring[:, u % RING, :].rearrange("p (c n) -> p c n", n=256)
                pe.wait_ge(dense_loaded[u % RING], dense_value(u))
                for m in range(2):
                    for c in range(16):
                        last = mm(ps[:, 4 + i, m * 64:m * 64 + 45].rearrange("p (a b) -> p a b", a=3),
                                  w[:, c, m * P:(m + 1) * P],
                                  kk[:, i, :, 2 * c:2 * c + CMP_STRIDE * (NCMP - 1) + 1:CMP_STRIDE],
                                  start=(c == 0), stop=(c == 15))
                last.then_inc(cmp_hidden, 1)
                pe.wait_ge(cmp_hidden, i + 1)
                pe.sem_inc(dense_used, 1)
            for q in range(4):
                part("gqk", hT, False, q)
            for i in range(2):
                pe.wait_ge(gelu_ready, i + 1)
                for g in range(G):
                    for m in range(2):
                        last = mm(ps[0:NCMP, 6, i * P + g * HD:i * P + (g + 1) * HD],
                                  gelu_h[:, i, m, g * NCMP:(g + 1) * NCMP], cmp_w2[:, i, m, :],
                                  start=(m == 0), stop=(m == 1))
            last.then_inc(cmp_kv_ready, 1)
            for q in range(4):
                part("gv", hT, True, q)
            for q in range(4):
                part("gout", hT, False, q)

            pe.wait_ge(roped, 1)
            pe.wait_ge(bank_emptied_dve, emptied("D", PROD["gv"], 1))
            pe.wait_ge(bank_emptied_act, emptied("A", PROD["gout"], 1))
            for j in range(4):
                for half in range(2):
                    last = turn(ps[:, j // 2, (j % 2) * S + half * P:(j % 2) * S + (half + 1) * P],
                                zq[:, half, j * P:(j + 1) * P], ident)
            for br in range(2):
                for half in range(2):
                    turn(ps[:, 2, br * S + half * P:br * S + (half + 1) * P],
                         zkv[:, half, br * 256:br * 256 + P], ident)
            turn(ps[:, 3, 0:NCMP], ckv[0:NCMP, 0:P], ident[0:NCMP, 0:NCMP]).then_inc(qk_turned, 1)

            pe.wait_ge(khat_ready, 1)
            pe.wait_ge(gate_abs, 1)
            for c in range(2):
                for half in range(2):
                    last = turn(ps[:, 7, half * S + c * P:half * S + (c + 1) * P],
                                khatT[:, c, half * P:(half + 1) * P], ident)
            last.then_inc(khat_turned, 1)
            pe.wait_ge(gla_qk_ready, 2)
            pe.wait_ge(cmp_bias_ready, 1)
            pe.wait_ge(gelu_ready, 2)
            for hh in range(GH):
                r0 = GDK * (hh % 2)
                for half in range(2):
                    i = gla_index(hh, half)
                    last = mm(ps[:, 4 + i // 4, (i % 4) * P:(i % 4 + 1) * P],
                              kt[r0:r0 + GDK, hh // 2, half * P:(half + 1) * P],
                              qt[r0:r0 + GDK, hh // 2, half * P:(half + 1) * P], start=True, stop=True)
            last.then_inc(att_filled, 1)
            pe.wait_ge(khat_rows, 1)
            pe.wait_ge(qkT_dve, 2)
            pe.wait_ge(qkT_act, 2)
            for hh in range(GH):
                for c in range(3):
                    r0 = L * (c % 2)
                    col = (hh // 2 * 2 + c // 2) * P
                    last = mm(ps[GDK * (hh % 2):GDK * (hh % 2) + GDK, c % 2, col:col + P],
                              khat[r0:r0 + L, c // 2, hh * GDK:(hh + 1) * GDK],
                              gv[r0:r0 + L, c // 2, hh * GDV:(hh + 1) * GDV], start=True, stop=True,
                              skip_group_check=True)
            last.then_inc(ds_filled, 1)
            pe.wait_ge(att_masked, 1)
            pe.wait_ge(states_ready, 1)
            for hh in range(GH):
                for half in range(2):
                    i = gla_index(hh, half)
                    bank, col = 2 + i // 4, (i % 4) * P
                    mm(ps[:, bank, col:col + P], attT[:, i, :], gv[:, half, hh * GDV:(hh + 1) * GDV],
                       start=True, stop=False, skip_group_check=True)
                    for c in (2 * half, 2 * half + 1):
                        if c == 0:
                            continue
                        r0, t0 = GDK * (hh % 2), L * (c % 2)
                        last = mm(ps[t0:t0 + L, bank, col:col + P],
                                  qt[r0:r0 + GDK, hh // 2, c * L:(c + 1) * L],
                                  state[r0:r0 + GDK, hh // 2, c - 1, :], start=False, stop=(c % 2 == 1),
                                  skip_group_check=True)
            last.then_inc(gla_o, 1)
            pe.wait_ge(gla_on, 1)
            for hh in range(GH):
                for half in range(2):
                    last = turn(ps[:, 4 + hh // 2, (hh % 2) * S + half * P:(hh % 2) * S + (half + 1) * P],
                                ogla[:, gla_index(hh, half) * P:(gla_index(hh, half) + 1) * P], ident)
            last.then_inc(gla_turned, 1)
            pe.wait_ge(gla_oT, 2)

            for k in range(QH + 2):
                if k < QH:
                    g, j = k // 4, k % 4
                    r0, b = HD * g, 2 * (k % 2)
                    if k >= 2:
                        pe.wait_ge(nmx1, k - 1)
                    for br in range(2):
                        mm(ps[:, b + br, 0:P], qT[r0:r0 + HD, j, 0:P], kT[r0:r0 + HD, br, 0:P], start=True, stop=True)
                        mm(ps[:, b + br, P:3 * P], qT[r0:r0 + HD, j, P:S], kT[r0:r0 + HD, br, :], start=True, stop=True)
                    for half in range(2):
                        last = mm(ps[:, b, 384 + half * NCMP:384 + (half + 1) * NCMP],
                                  qT[r0:r0 + HD, j, half * P:(half + 1) * P], kcT[r0:r0 + HD, 0:NCMP],
                                  start=True, stop=True)
                    last.then_inc(scores1, 1)
                if 1 <= k <= QH:
                    i = k - 1
                    pe.wait_ge(scaled1, i + 1)
                    if i >= 1:
                        pe.wait_ge(pT1_dve, i)
                        pe.wait_ge(pT1_act, i)
                    for blk in range(6):
                        turn(ps[:, 4 + blk // 4, (blk % 4) * P:(blk % 4 + 1) * P],
                             s_buf[:, i % 2, blk * P:(blk + 1) * P], ident)
                    for half in range(2):
                        last = turn(ps[0:NCMP, 5, S + half * P:S + (half + 1) * P],
                                    s_buf[:, i % 2, 768 + half * NCMP:768 + (half + 1) * NCMP], ident)
                    last.then_inc(turned1, 1)
                if k >= 2:
                    i = k - 2
                    g = i // 4
                    pe.wait_ge(pT1_dve, i + 1)
                    pe.wait_ge(pT1_act, i + 1)
                    if i >= 1:
                        pe.wait_ge(oT1, i)
                    r0 = HD * (i % 2)
                    o = ps[r0:r0 + HD, 6, (i % 2) * S:(i % 2 + 1) * S]
                    pt = pT[:, i % 2, :]
                    for br in range(2):
                        vcol = br * 256 + P + g * HD
                        mm(o, zkv[:, 0, vcol:vcol + HD], pt[:, br * 384:br * 384 + S], start=(br == 0), stop=False,
                           skip_group_check=True)
                        mm(o[:, P:S], zkv[:, 1, vcol:vcol + HD], pt[:, br * 384 + S:br * 384 + 384], start=False,
                           stop=False, skip_group_check=True)
                    mm(o, ckv[0:NCMP, P + g * HD:P + (g + 1) * HD], pt[0:NCMP, 768:1024], start=False, stop=True,
                       skip_group_check=True).then_inc(o1, 1)

            pe.wait_ge(oT1, QH)
            for n in range(2):
                for q in range(4):
                    part(f"wout{n}", oT, True, q)

            norm_turn(1, xn)
            wait_hT(1)

            def ffn_step(s, up_value, dn_value, done):
                up_slot, dn_slot = (U_FFN + 2 * s) % RING, (U_FFN + 2 * s + 1) % RING
                up = dense_ring[:, up_slot, :].rearrange("p (c g n) -> p c g n", c=KC, g=2)
                dn = dense_ring[:, dn_slot, 0:2048].rearrange("p (a n) -> p a n", a=2)
                pe.wait_ge(dense_loaded[up_slot], up_value)
                for a in range(2):
                    pe.wait_ge(ff_read_act, 2 * (2 * done + a) + 1)
                    pe.wait_ge(ff_read_dve, 2 * (2 * done + a) + 1)
                    for g in range(2):
                        for c in range(KC):
                            last = mm(ps[:, a, g * S:(g + 1) * S], up[:, c, g, a * P:(a + 1) * P], hT[:, c, :],
                                      start=(c == 0), stop=(c == KC - 1))
                    last.then_inc(ff_filled, 1)
                pe.wait_ge(ff_filled, 2 * done + 2)
                pe.sem_inc(dense_used, 1)
                pe.wait_ge(dense_loaded[dn_slot], dn_value)
                pe.wait_ge(ff_added, done + 1)
                for a in range(2):
                    pe.wait_ge(ff_act, 2 * done + a + 2)
                    for half in range(2):
                        for n in range(2):
                            last = mm(ps[:, 4 + half * 2 + n, :], act_T[:, a, half * P:(half + 1) * P],
                                      dn[:, a, n * 512:(n + 1) * 512], start=(a == 0), stop=(a == 1))
                last.then_inc(ff_down, 1)
                pe.wait_ge(ff_down, done + 2)
                pe.sem_inc(dense_used, 1)

            u0 = U_FFN
            pe.sem_inc(ff_down, 1)
            with nc.tensor.Fori(0, FCH // 4) as i:
                for s in range(2):
                    ffn_step(s, dense_value(u0 + 2 * s) + 32 * i, dense_value(u0 + 2 * s + 1) + 16 * i, 2 * i + s)
            ffn_step(0, dense_value(u0 + FCH - 2), dense_value(u0 + FCH - 1), FCH // 2 - 1)

            norm_turn(2, xn2)
            wait_hT(2)
            for kind, a, q in SCHEDULE2:
                if kind == "part":
                    if a in ("q0", "q1", "kv2"):
                        part(a, hT, True, q)
                    elif a[:2] in ("cc", "cx", "cb", "gc", "ga"):
                        part(a, hT, False, q)
                    elif a[:3] == "wco":
                        pe.wait_ge(cbz_ready, 4)
                        part(a, cbz, False, q)
                    elif a[:3] == "wao":
                        pe.wait_ge(o2T_ready, H2)
                        part(a, o2T, False, q)
                    else:
                        pe.wait_ge(merged, 4)
                        part(a, mrg, True, q)
                elif kind == "turn":
                    for rnd, heads in enumerate(((0, 1, 2, 3, 4, 5, 6, 7), (8, 9))):
                        pe.wait_ge(roped2, 1)
                        if rnd:
                            pe.wait_ge(q2T_dve, 2)
                            pe.wait_ge(q2T_act, 2)
                        for n, hh in enumerate(heads):
                            for half in range(2):
                                last = turn(ps[:, 4 + n // 2, (n % 2) * S + half * P:(n % 2) * S + (half + 1) * P],
                                            z2[:, half, hh * P:(hh + 1) * P], ident)
                        last.then_inc(turned_q2, 1)
                    pe.wait_ge(q2T_dve, 3)
                else:
                    k = a
                    if k < H2:
                        if k >= 2:
                            pe.wait_ge(exp2, k - 1)
                        for half in range(2):
                            last = mm(ps[:, 4 + k % 2, half * S:(half + 1) * S], q2T[:, k, half * P:(half + 1) * P],
                                      k2T[:, k // 4, :], start=True, stop=True)
                        last.then_inc(scores2, 1)
                    if 1 <= k <= H2:
                        i = k - 1
                        pe.wait_ge(scaled2, i + 1)
                        if i >= 1:
                            pe.wait_ge(pT2, i)
                        for kb in range(2):
                            for half in range(2):
                                last = turn(ps[:, 6, kb * S + half * P:kb * S + (half + 1) * P],
                                            p2[:, i % 2, half * S + kb * P:half * S + (kb + 1) * P], ident)
                        last.then_inc(turned2, 1)
                    if k >= 2:
                        i = k - 2
                        pe.wait_ge(pT2, i + 1)
                        if i >= 1:
                            pe.wait_ge(o2T_ready, i)
                        for kb in range(2):
                            last = mm(ps[:, 7, (i % 2) * S:(i % 2 + 1) * S], v2[:, kb, (i // 4) * P:(i // 4 + 1) * P],
                                      p2T[:, i % 2, kb * S:(kb + 1) * S], start=(kb == 0), stop=(kb == 1))
                        last.then_inc(o2, 1)
                        if k == ATTN_STEPS - 1:
                            pe.wait_ge(o2, H2)
                            pe.sem_inc(up_free, 1)
                            pe.sem_inc(dn_free, 1)
            pe.sem_inc(up_free, 1)
            pe.sem_inc(dn_free, 1)

            norm_turn(3, uN)
            wait_hT(3)
            for half in range(2):
                for c in range(KC):
                    last = mm(ps[:, 4, half * P:half * P + NG + NE], hT[:, c, half * P:(half + 1) * P],
                              router_w[:, c, :], start=(c == 0), stop=(c == KC - 1))
            last.then_inc(logits_ready, 1)
            pe.wait_ge(assigned, 1)
            before, ones = const("before"), const("ones")
            mm(ps[:, 5, 0:NE], before, assign[:, 0, :], start=True, stop=True)
            mm(ps[:, 5, NE:2 * NE], ones, assign[:, 0, :], start=True, stop=False)
            mm(ps[:, 5, NE:2 * NE], before, assign[:, 1, :], start=False, stop=True)
            mm(ps[:, 5, 2 * NE:3 * NE], ones, assign[:, 0, :], start=True, stop=False)
            mm(ps[:, 5, 2 * NE:3 * NE], ones, assign[:, 1, :], start=False, stop=True).then_inc(ranks_ready, 1)

            uview = uN.rearrange("p a (n c) -> p a c n", c=KC)

            def gather(it):
                for c in range(KC):
                    for half in range(2):
                        last = mm(ps[:, (0, 7)[c // 4], (c % 4) * P:(c % 4 + 1) * P], uview[:, half, c, :],
                                  sel[:, half, :], start=(half == 0), stop=(half == 1))
                    if c % 4 == 3:
                        last.then_inc(gathered, 1)

            def turn_hidden(it, j):
                pe.wait_ge(act_ready, 4 * it + j + 1)
                rows = hid[0:CAP, j % 2, :].rearrange("p (n m) -> p m n", m=4)
                for m in range(4):
                    last = mm(ps[:, 5 + j % 2, m * CAP:(m + 1) * CAP], rows[:, m, :], ident[0:CAP, 0:CAP],
                              start=True, stop=True)
                last.then_inc(hid_turned, 1)

            def expert_up(it, j):
                pe.wait_ge(up_loaded[j % 2], 32 * (2 * it + j // 2 + 1))
                if j == 0:
                    pe.wait_ge(xg_dve, it + 1)
                    pe.wait_ge(xg_act, it + 1)
                for c in range(KC):
                    for k, q in ((0, j), (1, j ^ 1)):
                        last = mm(ps[q * CAP:(q + 1) * CAP, 1 + k, :], xg[:, c, j * CAP:(j + 1) * CAP],
                                  expert_ring[:, j % 2, k, c * DE:(c + 1) * DE], start=(c == 0), stop=(c == KC - 1))
                    if c == 5 and j >= 1:
                        if j == 1:
                            pe.wait_ge(selwT_ready, it + 1)
                        turn_hidden(it, j - 1)
                last.then_inc(up_filled, 1)
                pe.wait_ge(up_filled, 4 * it + j + 1)
                pe.sem_inc(up_free, 1)

            def expert_down(it, j):
                pe.wait_ge(dn_loaded[j % 2], 16 * (2 * it + j // 2 + 1))
                pe.wait_ge(aT_ready, 4 * it + j + 1)
                w = expert_ring[:, j % 2, 2, :].rearrange("p (m n) -> p m n", m=4)
                for m in range(4):
                    for n, q in ((0, j), (1, j ^ 1)):
                        last = mm(ps[q * CAP:(q + 1) * CAP, 3 + n, :], aT[:, j % 2, m * CAP:(m + 1) * CAP],
                                  w[:, m, n * 512:(n + 1) * 512], start=(m == 0), stop=(m == 3))
                last.then_inc(y_filled, 1)
                pe.wait_ge(y_filled, 4 * it + j + 1)
                pe.sem_inc(dn_free, 1)

            def moe_iter(it):
                pe.wait_ge(sel_ready, it + 1)
                gather(it)
                pe.wait_ge(summed, 2 * it + 1)
                for half in range(2):
                    last = turn(ps[:, 5, half * P:(half + 1) * P], selw[:, half, :], ident)
                last.then_inc(selw_turned, 1)
                expert_up(it, 0)
                for j in range(1, GRP):
                    expert_up(it, j)
                    expert_down(it, j - 1)
                turn_hidden(it, GRP - 1)
                expert_down(it, GRP - 1)
                pe.wait_ge(y_dve, it + 1)
                pe.wait_ge(y_act, 4 * it + 4)
                for half in range(2):
                    b = (5, 3)[half]
                    for n in range(2):
                        last = mm(ps[:, b + n, :], selwT[:, half * P:(half + 1) * P], y[:, n * 512:(n + 1) * 512],
                                  start=True, stop=True)
                    last.then_inc(scattered, 1)

            pe.wait_ge(slots_ready, 1)
            with nc.tensor.Fori(0, NE // GRP) as it:
                moe_iter(it)
            fullest = nc.tensor.value_load(cmax[0:1, 0:1], min_val=0, max_val=S)
            with nc.tensor.Fori(1, ROUNDS) as r:
                with nc.tensor.If(fullest > r * CAP):
                    with nc.tensor.Fori(0, NE // GRP) as g:
                        moe_iter(r * (NE // GRP) + g)

        @block.vector
        def _(dve):
            v = nc.vector
            steps = [0]

            def then(ins):
                steps[0] += 1
                ins.then_inc(dve_step, 1)
                dve.wait_ge(dve_step, steps[0])

            v.memset(kk[:, :, 2, :], 0.0).then_inc(zeroed, 1)
            v.memset(attT, 0.0).then_inc(zeroed, 1)
            v.memset(ss1, 1.0).then_inc(zeroed, 1)
            dve.wait_ge(zeroed, 3)
            dve.wait_ge(prm_turned, 1)
            v.tensor_copy(prm.rearrange("p a b -> p (a b)")[:, 0:122], ps[:, 7, 0:122])
            then(v.tensor_copy(prm.rearrange("p a b -> p (a b)")[:, 128:241], ps[:, 7, 128:241]))
            v.tensor_copy(kk[:, 0, 2, 0:32:2], pe_kT)
            then(v.tensor_copy(kk[:, 1, 2, 0:32:2], pe_vT))
            dve.wait_ge(consts_in, 16)
            v.tensor_copy(chunk_mask[:], const("chunk_mask")).then_inc(prm_ready, 1)

            def norm(k, dst, gain=None):
                dve.wait_ge(ssq_ready, k + 1)
                v.tensor_scalar(msq[:], ssq[:], 1.0 / D, EPS, ALU.mult, ALU.add).then_inc(msq_ready, 1)
                dve.wait_ge(rms_ready, k + 1)
                v.reciprocal(rstd[:], rms[:]).then_inc(rstd_ready, 1)
                dve.wait_ge(rstd_ready, k + 1)
                if gain is None:
                    v.tensor_scalar(dst[:, 0, :], h[:, 0, :], rstd[:, 0:1], None, ALU.mult).then_inc(xn_dve, 1)
                else:
                    dve.wait_ge(gains_in, GAINS_IN)
                    for half in range(2):
                        last = v.scalar_tensor_tensor(dst[:, half, :], h[:, half, :], rstd[:, half:half + 1], gain,
                                                      ALU.mult, ALU.mult)
                    last.then_inc(xn_dve, 1)
                if k == 0:
                    dve.wait_ge(small_in, SMALL_IN)
                for c in (0, 1, 4, 5):
                    dve.wait_ge(xT_turned, 4 * k + c // 2 + 1)
                    src = ps[:, c // 2, (c % 2) * S:(c % 2 + 1) * S]
                    if gain is None:
                        v.tensor_scalar(hT[:, c, :], src, gcol[:, k, c:c + 1], None, ALU.mult).then_inc(hT_dve, 1)
                    else:
                        v.tensor_copy(hT[:, c, :], src).then_inc(hT_dve, 1)

            def filled_bank(name, bank):
                step = PROD[name]
                dve.wait_ge(bank_filled, filled(step, bank))
                return ps[:, 2 * (step % 2) + bank, :]

            norm(0, xn)
            b = filled_bank("cmp_in", 0)
            for i in range(2):
                for g in range(G):
                    r0 = HD * g
                    v.tensor_copy(kk[0:HD, i, g, :], b[r0:r0 + HD, i * S:(i + 1) * S])
                    last = v.tensor_copy(kk[HD:P, i, g, 0:S - 1], b[r0:r0 + HD, i * S + 1:(i + 1) * S])
            last.then_inc(bank_emptied_dve, 1)
            b = filled_bank("kv_tok", 0)
            v.tensor_copy(zkv[:, 0, :], b).then_inc(bank_emptied_dve, 1)
            dve.wait_ge(gate_logits, 1)
            for c in range(2):
                last = v.tensor_scalar(gt[:, c, :], ps[:, 7, c * S:(c + 1) * S], b_gateT[:, c:c + 1], None, ALU.add)
            then(last)
            v.scalar_tensor_tensor(ga_, gt, -1.0, gt, ALU.mult, ALU.max).then_inc(gate_abs, 1)
            b = filled_bank("q_tok", 0)
            v.tensor_copy(by_pairs(zq[:, 0, :]), b.rearrange("p (g j d) -> p g j d", g=G, j=4)
                          ).then_inc(bank_emptied_dve, 1)
            dve.wait_ge(gate_log, 1)
            then(v.scalar_tensor_tensor(gt, gt, 0.0, gl_, ALU.min, ALU.subtract))
            for c in range(2):
                for k in range(S // L):
                    last = v.tensor_tensor_scan(cum[:, c, k * L:(k + 1) * L], const("ones")[:, 0:L],
                                                gt[:, c, k * L:(k + 1) * L], 0.0, ALU.mult, ALU.add)
            then(last)
            v.tensor_scalar(blast, cum[:, :, L - 1::L], 1.0 / TAU, None, ALU.mult).then_inc(cum_ready, 1)
            for i in range(2):
                dve.wait_ge(cmp_hidden, i + 1)
                last = v.tensor_copy(hid_bias[:, 2 * i:2 * i + 2], ps[:, 4 + i, 30:30 + 65:64])
            last.then_inc(cmp_bias_ready, 1)
            b = filled_bank("gqk", 0)
            v.tensor_copy(gq.rearrange("p a b -> p (a b)"), b).then_inc(bank_emptied_dve, 1)
            dve.wait_ge(sq_q, 1)
            v.tensor_reduce(ss1[:, 0:16].rearrange("p (a b) -> p a b", a=2),
                            sq1[:, :, 0:512].rearrange("p a (b d) -> p a b d", d=HD), AX.X, ALU.add)
            v.tensor_reduce(ss1[:, 16:24], sq1[:, :, 512:768].rearrange("p a (b d) -> p a b d", d=HD), AX.X, ALU.add)
            dve.wait_ge(cmp_kv_ready, 1)
            then(v.tensor_copy(ckv[0:NCMP, :], ps[0:NCMP, 6, 0:256]))
            then(v.tensor_tensor(sq1[0:NCMP, 0, 768:896], ckv[0:NCMP, 0:P], ckv[0:NCMP, 0:P], ALU.mult))
            then(v.tensor_reduce(ss1[0:NCMP, 24:26], sq1[0:NCMP, 0, 768:896].rearrange("p (b d) -> p b d", d=HD),
                                 AX.X, ALU.add))
            v.tensor_scalar(r1, ss1, 1.0 / HD, EPS, ALU.mult, ALU.add).then_inc(ms_heads, 1)
            dve.wait_ge(exps_ready, 1)
            v.scalar_tensor_tensor(qt, gq, GDK ** -0.5, e_pos, ALU.mult, ALU.mult).then_inc(gla_qk_ready, 1)
            dve.wait_ge(bank_emptied_act, emptied("A", PROD["gqk"], 1))
            v.tensor_tensor(kt, gk, e_neg, ALU.mult).then_inc(gla_qk_ready, 1)
            v.tensor_tensor(khatT, gk, khatT, ALU.mult).then_inc(khat_ready, 1)
            b = filled_bank("gv", 0)
            v.tensor_copy(gv[:, 0, :], b).then_inc(bank_emptied_dve, 1)

            dve.wait_ge(rms_heads, 1)
            then(v.reciprocal(r1, ss1))
            dve.wait_ge(gains_in, GAINS_IN)
            dve.wait_ge(bank_emptied_act, emptied("A", PROD["q_tok"], 1))
            zq4 = zq.rearrange("p a (b d) -> p (a b) d", d=HD)
            zk4 = zkv.rearrange("p a (r x d) -> p a r x d", r=2, d=HD)
            v.tensor_tensor(zq4, zq4, r1[:, 0:16].unsqueeze(2).to_broadcast([P, 16, HD]), ALU.mult)
            for half in range(2):
                for br in range(2):
                    zk = zk4[:, half, br, 0:2, :]
                    i = 16 + half * 4 + br * 2
                    v.tensor_tensor(zk, zk, r1[:, i:i + 2].unsqueeze(2).to_broadcast([P, 2, HD]), ALU.mult)
            ck = ckv[0:NCMP, 0:P].rearrange("p (b d) -> p b d", d=HD)
            then(v.tensor_tensor(ck, ck, r1[0:NCMP, 24:26].unsqueeze(2).to_broadcast([NCMP, 2, HD]), ALU.mult))
            v.tensor_tensor(zq4, zq4, q_gain1.unsqueeze(1).to_broadcast([P, 16, HD]), ALU.mult)
            for half in range(2):
                for br in range(2):
                    zk = zk4[:, half, br, 0:2, :]
                    gn = k_gains1[:, (1 + br) * HD:(2 + br) * HD]
                    v.tensor_tensor(zk, zk, gn.unsqueeze(1).to_broadcast([P, 2, HD]), ALU.mult)
            then(v.tensor_tensor(ck, ck, k_gains1[0:NCMP, 0:HD].unsqueeze(1).to_broadcast([NCMP, 2, HD]), ALU.mult))

            def rope(x, cos, sin, rows, n):
                x1, x2 = x[:, :, 0:8], x[:, :, 8:16]
                c, s_ = cos.unsqueeze(1).to_broadcast([rows, n, 8]), sin.unsqueeze(1).to_broadcast([rows, n, 8])
                tm = [rope_tmp[0:rows, i, 0:n * 8].rearrange("p (a b) -> p a b", b=8) for i in range(4)]
                v.tensor_tensor(tm[0], x1, c, ALU.mult)
                v.tensor_tensor(tm[1], x2, s_, ALU.mult)
                v.tensor_tensor(tm[2], x2, c, ALU.mult)
                then(v.tensor_tensor(tm[3], x1, s_, ALU.mult))
                v.tensor_tensor(x1, tm[0], tm[1], ALU.subtract)
                then(v.tensor_tensor(x2, tm[2], tm[3], ALU.add))

            cos1, sin1 = const("cos1"), const("sin1")
            for half in range(2):
                c, s_ = cos1[:, half * 8:(half + 1) * 8], sin1[:, half * 8:(half + 1) * 8]
                rope(zq.rearrange("p a (b d) -> p a b d", d=HD)[:, half], c, s_, P, QH)
                for br in range(2):
                    rope(zk4[:, half, br, 0:2, :], c, s_, P, 2)
            rope(ck, const("cosc", NCMP), const("sinc", NCMP), NCMP, 2)
            v.memset(tail[:, 0:1], 0.0).then_inc(roped, 1)
            dve.wait_ge(qk_turned, 1)
            v.tensor_copy(qT[:, 0:2, :].rearrange("p a b -> p (a b)"), ps[:, 0, :]).then_inc(qkT_dve, 1)
            v.tensor_copy(kcT[:, 0:NCMP], ps[:, 3, 0:NCMP]).then_inc(qkT_dve, 1)

            dve.wait_ge(khat_turned, 1)
            v.tensor_copy(khat.rearrange("p a b -> p (a b)"), ps[:, 7, :]).then_inc(khat_rows, 1)
            dve.wait_ge(att_filled, 1)
            for i in range(2):
                last = v.copy_predicated(attT[:, 4 * i:4 * i + 4, :],
                                         chunk_mask[:].unsqueeze(1).to_broadcast([P, 4, P]),
                                         ps[:, 4 + i, :].rearrange("p (a b) -> p a b", a=4))
            last.then_inc(att_masked, 1)
            dve.wait_ge(ds_filled, 1)
            dS = ps[:, 0:2, :].rearrange("p b (a c n) -> p a b c n", a=2, c=2)
            then(v.tensor_copy(state[:, :, 0, :], dS[:, :, 0, 0, :]))
            for c in range(1, 3):
                for i in range(2):
                    last = v.scalar_tensor_tensor(state[:, i, c, :], state[:, i, c - 1, :], decay[:, i, c:c + 1],
                                                  dS[:, i, c % 2, c // 2, :], ALU.mult, ALU.add)
                then(last) if c == 1 else last.then_inc(states_ready, 1)
            dve.wait_ge(gla_sq, 1)
            then(v.tensor_reduce(ogla_ss, osq.rearrange("p (a b) -> p a b", b=P), AX.X, ALU.add))
            v.tensor_scalar(ogla_r, ogla_ss, 1.0 / GDV, EPS, ALU.mult, ALU.add).then_inc(gla_ms, 1)
            dve.wait_ge(gla_rms, 1)
            then(v.reciprocal(ogla_r, ogla_ss))
            v.tensor_tensor(ogla.rearrange("p (a b) -> p a b", b=P),
                            ps[:, 2:4, :].rearrange("p a b -> p (a b)").rearrange("p (a b) -> p a b", b=P),
                            ogla_r.unsqueeze(2).to_broadcast([P, 8, P]), ALU.mult).then_inc(gla_on, 1)
            dve.wait_ge(gla_turned, 1)
            for i in range(2):
                v.scalar_tensor_tensor(oT[:, 4 + 2 * i:6 + 2 * i, :], ps[:, 4 + i, :].rearrange("p (a b) -> p a b", a=2),
                                       out_gainT, sil[:, 2 * i:2 * i + 2, :], ALU.mult, ALU.mult).then_inc(gla_oT, 1)

            causal3 = const("causal3")
            for k in range(QH + 2):
                if k < QH:
                    b, s_ = 2 * (k % 2), s_buf[:, k % 2, :]
                    m, nm = mx[:, k % 2, :], nmx[:, k % 2, :]
                    dve.wait_ge(scores1, k + 1)
                    if k >= 2:
                        dve.wait_ge(turned1, k - 1)
                        dve.wait_ge(exp1, k - 1)
                    v.tensor_tensor(s_[:, 0:768].rearrange("p (a b) -> p a b", a=2), ps[:, b:b + 2, 0:384],
                                    causal3.unsqueeze(1).to_broadcast([P, 2, 384]), ALU.add)
                    then(v.tensor_tensor(s_[:, 768:798], ps[:, b, 384:414], const("cmp_bias"), ALU.add))
                    v.tensor_reduce(m[:, 0:6], s_[:, 0:768].rearrange("p (a b) -> p a b", b=P), AX.X, ALU.max)
                    then(v.tensor_reduce(m[:, 6:8], s_[:, 768:798].rearrange("p (a b) -> p a b", b=NCMP), AX.X, ALU.max))
                    then(v.tensor_tensor(m[:, 1:6:3], m[:, 1:6:3], m[:, 2:6:3], ALU.max))
                    v.tensor_scalar(nm, m, -(HD ** -0.5), None, ALU.mult).then_inc(nmx1, 1)
                if k >= 2:
                    i = k - 2
                    dve.wait_ge(turned1, i + 1)
                    if i >= 2:
                        dve.wait_ge(o1, i - 1)
                    v.tensor_copy(pT[:, i % 2, 512:768], ps[:, 5, 0:S])
                    v.tensor_copy(pT[0:NCMP, i % 2, 768:1024], ps[0:NCMP, 5, S:2 * S]).then_inc(pT1_dve, 1)
                if 1 <= k <= QH:
                    i = k - 1
                    s_, sm, wt = s_buf[:, i % 2, :], sums[:, i % 2, :], wts[:, i % 2, :]
                    dve.wait_ge(exp1, i + 1)
                    then(v.reciprocal(wt[:, 0:6], sm[:, 0:6]))
                    gate = gates[:, :, 3 * i:3 * i + 3].rearrange("p a b -> p b a")
                    v.tensor_tensor(wt[:, 0:4].rearrange("p (a b) -> p a b", a=2),
                                    wt[:, 0:4].rearrange("p (a b) -> p a b", a=2), gate[:, 1:3, :], ALU.mult)
                    then(v.tensor_tensor(wt[:, 4:6], wt[:, 4:6], gate[:, 0, :], ALU.mult))
                    for br in range(2):
                        o = br * 384
                        v.tensor_scalar(s_[:, o:o + P], s_[:, o:o + P], wt[:, 2 * br:2 * br + 1], None, ALU.mult)
                        v.tensor_scalar(s_[:, o + P:o + 384], s_[:, o + P:o + 384], wt[:, 2 * br + 1:2 * br + 2],
                                        None, ALU.mult)
                    for half in range(2):
                        o = 768 + half * NCMP
                        last = v.scalar_tensor_tensor(s_[:, o:o + NCMP], s_[:, o:o + NCMP], wt[:, 4 + half:5 + half],
                                                      const("cmp_keep")[:, half * NCMP:(half + 1) * NCMP],
                                                      ALU.mult, ALU.mult)
                    last.then_inc(scaled1, 1)

            def add_rows(name, n):
                for half in range(2):
                    b = filled_bank(name, half)
                    o = h[:, half, n * 512:(n + 1) * 512]
                    v.tensor_tensor(o, o, b, ALU.add).then_inc(bank_emptied_dve, 1)

            for n in range(2):
                add_rows(f"wout{n}", n)
            dve.wait_ge(bank_emptied_dve, emptied("D", PROD["wout1"], 1))
            v.memset(tail[:, 1:2], 0.0).then_inc(h_ready, 1)
            norm(1, xn)

            def taps(k):
                return [prm[:, 0, bass.ds(k, 1)], prm[:, 0, bass.ds(k + 44, 1)]]

            def ffn_step(k, done):
                for a in range(2):
                    dve.wait_ge(ff_read_act, 2 * (2 * done + a) + 3)
                    for g in range(2):
                        u = ps[:, a, g * S:(g + 1) * S]
                        w0, w1 = taps(2 * k + a + g * FCH)
                        yy = conv_y[:, a, g, :]
                        v.scalar_tensor_tensor(yy[:, 1:S], u[:, 0:S - 1], w1, yy[:, 1:S], ALU.mult, ALU.add
                                               ).then_inc(ffn_chain, 1)
                        dve.wait_ge(ffn_chain, 2 * (2 * done + a) + g + 1)
                        v.scalar_tensor_tensor(yy[:, 2:S], u[:, 0:S - 2], w0, yy[:, 2:S], ALU.mult, ALU.add
                                               ).then_inc(ff_read_dve, 1)
                    dve.wait_ge(ff_silu, 2 * done + a + 1)
                    dve.wait_ge(ff_read_dve, 2 * (2 * done + a) + 3)
                    dve.wait_ge(ff_down, done + 1)
                    v.tensor_tensor(act_T[:, a, :], sil_g[:, a, :], conv_y[:, a, 1, :], ALU.mult).then_inc(ff_act, 1)
                dve.wait_ge(ff_down, done + 2)
                for half in range(2):
                    for n in range(2):
                        o = h[:, half, n * 512:(n + 1) * 512]
                        last = v.tensor_tensor(o, o, ps[:, 4 + half * 2 + n, :], ALU.add)
                last.then_inc(ff_added, 1)
                dve.wait_ge(ff_added, done + 2)
                v.memset(tail[:, 9:10], 0.0)

            for s_one in (ff_read_dve, ff_act, ff_added):
                dve.sem_inc(s_one, 1)
            with nc.vector.Fori(0, FCH // 4) as i:
                for s in range(2):
                    ffn_step(2 * i + s, 2 * i + s)
            ffn_step(FCH // 2 - 1, FCH // 2 - 1)
            v.memset(tail[:, 2:3], 0.0).then_inc(h_ready, 1)

            norm(2, xn2)
            z5 = z2.rearrange("p a (b d) -> p (a b) d", d=P)
            cos2, sin2 = const("cos2"), const("sin2")

            def heads_norm():
                dve.wait_ge(sq2_ready, 2)
                then(v.tensor_reduce(ss2, sq2.rearrange("p a (b d) -> p (a b) d", d=P), AX.X, ALU.add))
                v.tensor_scalar(r2, ss2, 1.0 / HD2, EPS, ALU.mult, ALU.add).then_inc(ms2_ready, 1)

            def heads_rope():
                dve.wait_ge(rms2_ready, 1)
                then(v.reciprocal(r2, ss2))
                then(v.tensor_tensor(z5, z5, r2.unsqueeze(2).to_broadcast([P, 20, P]), ALU.mult))
                for half in range(2):
                    zh = z2[:, half, :].rearrange("p (b d) -> p b d", d=P)
                    v.tensor_tensor(zh[:, 0:8, :], zh[:, 0:8, :], q_gain2.unsqueeze(1).to_broadcast([P, 8, P]), ALU.mult)
                    last = v.tensor_tensor(zh[:, 8:10, :], zh[:, 8:10, :],
                                           k_gain2.unsqueeze(1).to_broadcast([P, 2, P]), ALU.mult)
                then(last)
                for half in range(2):
                    zh = z2[:, half, :].rearrange("p (b i e) -> p b i e", i=64, e=2)
                    x0, x1 = zh[:, :, :, 0], zh[:, :, :, 1]
                    c = cos2[:, half * 64:(half + 1) * 64].unsqueeze(1).to_broadcast([P, 10, 64])
                    s_ = sin2[:, half * 64:(half + 1) * 64].unsqueeze(1).to_broadcast([P, 10, 64])
                    tm = [sq2[:, i // 2, (i % 2) * 640:(i % 2 + 1) * 640].rearrange("p (b i) -> p b i", i=64)
                          for i in range(4)]
                    v.tensor_tensor(tm[0], x0, c, ALU.mult)
                    v.tensor_tensor(tm[1], x1, s_, ALU.mult)
                    v.tensor_tensor(tm[2], x0, s_, ALU.mult)
                    then(v.tensor_tensor(tm[3], x1, c, ALU.mult))
                    v.tensor_tensor(x0, tm[0], tm[1], ALU.subtract)
                    then(v.tensor_tensor(x1, tm[2], tm[3], ALU.add))
                v.memset(tail[:, 3:4], 0.0).then_inc(roped2, 1)

            def empty2(name, bank):
                b = filled_bank(name, bank)
                m = int(name[-1])
                two = b.rearrange("p (a b) -> p a b", a=2)
                lo = 2 * bank
                if name in ("q0", "q1"):
                    v.tensor_copy(z2[:, 0, 512 * m:512 * (m + 1)], b).then_inc(bank_emptied_dve, 1)
                elif name == "kv2":
                    v.tensor_copy(z2[:, 0, 1024:1280], b[:, 0:256])
                    v.tensor_copy(v2[:, 0, :], b[:, 256:512]).then_inc(bank_emptied_dve, 1)
                elif name[:2] == "cx":
                    dve.wait_ge(bank_emptied_act, emptied("A", PROD["cc%d" % m], bank))
                    if m == 1:
                        dve.wait_ge(conv_mid, 1)
                    v.tensor_tensor(u_s[:, lo:lo + 2, :], two, cc_s[:, lo:lo + 2, :], ALU.mult
                                    ).then_inc(bank_emptied_dve, 1)
                elif name[:2] == "cb":
                    if bank == 0:
                        dve.wait_ge(conv_mid, m + 1)
                        for c in range(4):
                            v.scalar_tensor_tensor(z_s[:, c, 1:S], u_s[:, c, 0:S - 1], cw2(0, 4 * m + c),
                                                   z_s[:, c, 1:S], ALU.mult, ALU.add)
                        then(v.memset(tail[:, 4:5], 0.0))
                        for c in range(4):
                            last = v.scalar_tensor_tensor(z_s[:, c, 0:S - 1], u_s[:, c, 1:S], cw2(2, 4 * m + c),
                                                          z_s[:, c, 0:S - 1], ALU.mult, ALU.add)
                        then(last)
                    v.tensor_tensor(cbz[:, 4 * m + lo:4 * m + lo + 2, :], two, z_s[:, lo:lo + 2, :], ALU.mult
                                    ).then_inc(bank_emptied_dve, 1)
                    if bank == 1:
                        dve.wait_ge(bank_emptied_dve, emptied("D", PROD[name], 1))
                        v.memset(tail[:, 5:6], 0.0).then_inc(cbz_ready, 2)
                elif name[:3] == "wco":
                    dve.wait_ge(bank_emptied_act, emptied("A", PROD["gc%d" % m], bank))
                    v.tensor_tensor(mrg[:, 4 * m + lo:4 * m + lo + 2, :], two, sg[:, lo:lo + 2, :], ALU.mult
                                    ).then_inc(bank_emptied_dve, 1)
                elif name[:3] == "wao":
                    dve.wait_ge(bank_emptied_act, emptied("A", PROD["ga%d" % m], bank))
                    if 2 * m + bank:
                        dve.wait_ge(merged, 2 * m + bank)
                    v.tensor_tensor(mtmp.rearrange("p (a b) -> p a b", a=2), two, sg2[:, lo:lo + 2, :], ALU.mult
                                    ).then_inc(bank_emptied_dve, 1)
                    dve.wait_ge(bank_emptied_dve, emptied("D", PROD[name], bank))
                    mm_ = mrg[:, 4 * m + lo:4 * m + lo + 2, :]
                    v.tensor_tensor(mm_, mm_, mtmp.rearrange("p (a b) -> p a b", a=2), ALU.add).then_inc(merged, 1)
                else:
                    o = h[:, bank, m * 512:(m + 1) * 512]
                    v.tensor_tensor(o, o, b, ALU.add).then_inc(bank_emptied_dve, 1)

            def cw2(tap, c):
                return prm[:, 1, 88 + tap * 8 + c:89 + tap * 8 + c]

            for kind, a, q in SCHEDULE2:
                if kind == "part":
                    if q % 2 and PRODUCTS[PROD[a]][1][q // 2] == "D":
                        empty2(a, q // 2)
                    if (a, q) == ("kv2", 3):
                        heads_norm()
                    if (a, q) == ("cc0", 3):
                        heads_rope()
                elif kind == "turn":
                    for rnd in range(2):
                        dve.wait_ge(turned_q2, rnd + 1)
                        if rnd == 0:
                            for i in range(2):
                                v.tensor_copy(q2T[:, 2 * i:2 * i + 2, :].rearrange("p a b -> p (a b)"), ps[:, 4 + i, :]
                                              ).then_inc(q2T_dve, 1)
                        else:
                            v.tensor_copy(k2T.rearrange("p a b -> p (a b)"), ps[:, 4, :]).then_inc(q2T_dve, 1)
                else:
                    k = a
                    if k < H2:
                        dve.wait_ge(scores2, k + 1)
                        if k >= 2:
                            dve.wait_ge(exp2, k - 1)
                        then(v.tensor_reduce(mx2[:, k % 2, :], ps[:, 4 + k % 2, :].rearrange("p (a b) -> p a b", a=2),
                                             AX.X, ALU.max))
                        v.tensor_scalar(nmx2[:, k % 2, :], mx2[:, k % 2, :], -(HD2 ** -0.5), None, ALU.mult
                                        ).then_inc(nmx_2, 1)
                    if 1 <= k <= H2:
                        i = k - 1
                        dve.wait_ge(exp2, i + 1)
                        then(v.reciprocal(rs2[:, i % 2, :], sum2[:, i % 2, :]))
                        for half in range(2):
                            o = p2[:, i % 2, half * S:(half + 1) * S]
                            last = v.tensor_scalar(o, o, rs2[:, i % 2, half:half + 1], None, ALU.mult)
                        last.then_inc(scaled2, 1)
                        dve.wait_ge(turned2, i + 1)
                        if i >= 2:
                            dve.wait_ge(o2, i - 1)
                        v.tensor_copy(p2T[:, i % 2, :], ps[:, 6, :]).then_inc(pT2, 1)
            dve.wait_ge(bank_emptied_dve, emptied("D", PROD["wo1"], 1))
            v.memset(tail[:, 6:7], 0.0).then_inc(h_ready, 1)

            norm(3, uN, norm_gain2)
            dve.wait_ge(logits_ready, 1)
            then(v.tensor_copy(lg, ps[:, 4, 0:2 * P].rearrange("p (a b) -> p a b", a=2)[:, :, 0:NG + NE]))
            for half in range(2):
                last = v.max(g8[:, half, :], lg[:, half, 0:NG])
            then(last)
            for half in range(2):
                v.max_index(gi8u[:, half, :], g8[:, half, :], lg[:, half, 0:NG])
            then(v.tensor_scalar(ngm, g8[:, :, 0:1], -1.0, None, ALU.mult))
            v.tensor_copy(gi8, gi8u).then_inc(grp_nmax, 1)
            dve.wait_ge(grp_nmax, 1)
            for half in range(2):
                last = v.tensor_scalar(goh[:, half, :], const("iota64")[:, 0:NG], gi8[:, half, 0:1], None, ALU.is_equal)
            then(last)
            v.tensor_scalar(gohb, goh, -1.0, -NEG, ALU.add, ALU.mult)
            for half in range(2):
                e3 = elm[:, half, :].rearrange("p (a b) -> p a b", a=NG)
                last = v.tensor_tensor(e3, lg[:, half, NG:].rearrange("p (a b) -> p a b", a=NG),
                                       goh[:, half, :].unsqueeze(2).to_broadcast([P, NG, EPG]), ALU.mult)
            then(last)
            for half in range(2):
                e3 = elm[:, half, :].rearrange("p (a b) -> p a b", a=NG)
                last = v.tensor_tensor(e3, e3, gohb[:, half, :].unsqueeze(2).to_broadcast([P, NG, EPG]), ALU.add)
            then(last)
            for half in range(2):
                last = v.max(e8[:, half, :], elm[:, half, :])
            then(last)
            for half in range(2):
                v.max_index(ei8u[:, half, :], e8[:, half, :], elm[:, half, :])
            v.tensor_tensor(dv, e8[:, :, 1:2], e8[:, :, 0:1], ALU.subtract).then_inc(top_diff, 1)
            dve.wait_ge(top_diff, 1)
            then(v.tensor_copy(ei8, ei8u))
            for half in range(2):
                v.tensor_scalar(oh1[:, half, :], const("iota64"), ei8[:, half, 0:1], None, ALU.is_equal)
                last = v.tensor_scalar(oh2[:, half, :], const("iota64"), ei8[:, half, 1:2], None, ALU.is_equal)
            then(last)
            v.tensor_tensor(assign, oh1, oh2, ALU.add).then_inc(assigned, 1)
            dve.wait_ge(grp_exp, 2)
            v.reciprocal(pg, gsum)
            dve.wait_ge(top_exp, 1)
            then(v.tensor_scalar(den, ex, 1.0, None, ALU.add))
            then(v.reciprocal(rden, den))
            then(v.tensor_tensor(w1t, pg, rden, ALU.mult))
            then(v.tensor_tensor(w2t, w1t, ex, ALU.mult))
            for half in range(2):
                last = v.tensor_scalar(oh1[:, half, :], oh1[:, half, :], w1t[:, half, :], None, ALU.mult)
            then(last)
            for half in range(2):
                last = v.scalar_tensor_tensor(wmat[:, half, :], oh2[:, half, :], w2t[:, half, :], oh1[:, half, :],
                                              ALU.mult, ALU.add)
            then(last)
            dve.wait_ge(ranks_ready, 1)
            rank = ps[:, 5, 0:2 * NE].rearrange("p (a b) -> p a b", a=2)
            dve.wait_ge(assigned, 1)
            then(v.scalar_tensor_tensor(slot, rank, 1.0, assign, ALU.add, ALU.mult))
            v.tensor_scalar(slot, slot, -1.0, None, ALU.add)
            then(v.tensor_reduce(cmax_f, ps[:, 5, 2 * NE:3 * NE], AX.X, ALU.max))
            v.tensor_copy(cmax, cmax_f).then_inc(slots_ready, 1)
            dve.wait_ge(slots_ready, 1)

            iota4 = const("slot_iota").rearrange("p (a b) -> p a b", a=GRP)

            def moe_iter(it, e0):
                for half in range(2):
                    sl = slot[:, half, bass.ds(e0, GRP)].unsqueeze(2).to_broadcast([P, GRP, CAP])
                    last = v.tensor_tensor(sel[:, half, :].rearrange("p (a b) -> p a b", a=GRP), iota4, sl, ALU.is_equal)
                last.then_inc(moe_step, 1)
                dve.wait_ge(moe_step, it + 1)
                for half in range(2):
                    wv = wmat[:, half, bass.ds(e0, GRP)].unsqueeze(2).to_broadcast([P, GRP, CAP])
                    last = v.tensor_tensor(selw[:, half, :].rearrange("p (a b) -> p a b", a=GRP),
                                           sel[:, half, :].rearrange("p (a b) -> p a b", a=GRP), wv, ALU.mult)
                last.then_inc(sel_ready, 1)

                dve.wait_ge(gathered, 2 * it + 1)
                v.tensor_copy(xg[:, 0:4, :], ps[:, 0, :].rearrange("p (c s) -> p c s", c=4)).then_inc(xg_dve, 1)
                for j in range(GRP):
                    q = (j ^ 1) * CAP
                    dve.wait_ge(silu_ready, 4 * it + j + 1)
                    v.tensor_tensor(hid[0:CAP, j % 2, :], hsil[q:q + CAP, j % 2, :], ps[q:q + CAP, 2, :], ALU.mult
                                    ).then_inc(act_ready, 1)
                    dve.wait_ge(hid_turned, 4 * it + j + 1)
                    if j >= 2:
                        dve.wait_ge(y_filled, 4 * it + j - 1)
                    v.tensor_copy(aT[:, j % 2, :], ps[:, 5 + j % 2, 0:P]).then_inc(aT_ready, 1)
                dve.wait_ge(y_filled, 4 * it + 4)
                v.tensor_copy(y[:, 0:512], ps[:, 3, :]).then_inc(y_dve, 1)
                for half in range(2):
                    dve.wait_ge(scattered, 2 * it + half + 1)
                    b = (5, 3)[half]
                    v.tensor_tensor(h[:, half, :].rearrange("p (a b) -> p a b", a=2),
                                    h[:, half, :].rearrange("p (a b) -> p a b", a=2), ps[:, b:b + 2, :], ALU.add
                                    ).then_inc(summed, 1)
                dve.wait_ge(summed, 2 * it + 3)
                v.memset(tail[:, 9:10], 0.0)

            dve.sem_inc(summed, 1)
            with nc.vector.Fori(0, NE // GRP) as it:
                moe_iter(it, it * GRP)
            fullest = nc.vector.value_load(cmax[0:1, 0:1], min_val=0, max_val=S)
            with nc.vector.Fori(1, ROUNDS) as r:
                with nc.vector.If(fullest > r * CAP):
                    v.tensor_scalar(slot, slot, -float(CAP), None, ALU.add).then_inc(moe_round, 1)
                    dve.wait_ge(moe_round, r)
                    v.memset(tail[:, 9:10], 0.0)
                    with nc.vector.Fori(0, NE // GRP) as g:
                        moe_iter(r * (NE // GRP) + g, g * GRP)
            v.memset(tail[:, 7:8], 0.0).then_inc(last_ready, 1)

        @block.scalar
        def _(act):
            a_ = nc.scalar.activation

            def norm(k, dst, junk, gain=False):
                if k == 0:
                    act.wait_ge(x_in, 32)
                else:
                    act.wait_ge(h_ready, k)
                for half in range(2):
                    last = a_(junk[:, half, :], h[:, half, :], ACT.Square, accum_out=ssq[:, half:half + 1])
                last.then_inc(ssq_ready, 1)
                act.wait_ge(msq_ready, k + 1)
                a_(rms[:], msq[:], ACT.Sqrt).then_inc(rms_ready, 1)
                act.wait_ge(rstd_ready, k + 1)
                if not gain:
                    a_(dst[:, 1, :], h[:, 1, :], ACT.Copy, scale=rstd[:, 1:2]).then_inc(xn_act, 1)
                else:
                    a_(tail[:, 8:9], rstd[:, 1:2], ACT.Copy).then_inc(xn_act, 1)
                if k == 0:
                    act.wait_ge(small_in, SMALL_IN)
                for c in (2, 3, 6, 7):
                    act.wait_ge(xT_turned, 4 * k + c // 2 + 1)
                    src = ps[:, c // 2, (c % 2) * S:(c % 2 + 1) * S]
                    if not gain:
                        a_(hT[:, c, :], src, ACT.Copy, scale=gcol[:, k, c:c + 1]).then_inc(hT_act, 1)
                    else:
                        a_(hT[:, c, :], src, ACT.Copy).then_inc(hT_act, 1)

            def filled_bank(name, bank):
                step = PROD[name]
                act.wait_ge(bank_filled, filled(step, bank))
                return ps[:, 2 * (step % 2) + bank, :]

            norm(0, xn, xn)
            b = filled_bank("cmp_in", 1)
            a_(gates.rearrange("p a b -> p (a b)"), b[:, 0:48], ACT.Sigmoid)
            a_(glrT[0:16, :], b[0:16, P:P + S], ACT.Copy).then_inc(bank_emptied_act, 1)
            b = filled_bank("kv_tok", 1)
            a_(zkv[:, 1, :], b, ACT.Copy).then_inc(bank_emptied_act, 1)
            act.wait_ge(gate_abs, 1)
            a_(gl_, ga_, ACT.Exp, scale=-1.0).then_inc(act_step, 1)
            act.wait_ge(act_step, 1)
            a_(gl_, gl_, ACT.Ln, bias=1.0).then_inc(gate_log, 1)
            b = filled_bank("q_tok", 1)
            a_(by_pairs(zq[:, 1, :]), b.rearrange("p (g j d) -> p g j d", g=G, j=4), ACT.Copy
               ).then_inc(bank_emptied_act, 1)
            act.wait_ge(cum_ready, 1)
            a_(e_pos, cum, ACT.Exp, scale=1.0 / TAU)
            a_(e_neg, cum, ACT.Exp, scale=-1.0 / TAU)
            a_(decay, blast, ACT.Exp)
            for c in range(2):
                for k in range(4):
                    last = a_(khatT[:, c, k * L:(k + 1) * L], cum[:, c, k * L:(k + 1) * L], ACT.Exp,
                              scale=-1.0 / TAU, bias=blast[:, c, k:k + 1])
            last.then_inc(exps_ready, 1)
            act.wait_ge(bank_emptied_act, 3)
            act.wait_ge(bank_emptied_dve, emptied("D", PROD["q_tok"], 0))
            a_(sq1[:, :, 0:512], zq, ACT.Square)
            a_(sq1[:, :, 512:768].rearrange("p a (r x) -> p a r x", r=2),
               zkv.rearrange("p a (r x) -> p a r x", r=2)[:, :, :, 0:P], ACT.Square).then_inc(sq_q, 1)
            act.wait_ge(cmp_bias_ready, 1)
            for i in range(2):
                for m in range(2):
                    last = a_(gelu_h[:, i, m, :], ps[:, 4 + i, m * 64:m * 64 + 30], ACT.Gelu_apprx_tanh,
                              bias=hid_bias[:, 2 * i + m:2 * i + m + 1])
                last.then_inc(gelu_ready, 1)
            b = filled_bank("gqk", 1)
            a_(gk.rearrange("p a b -> p (a b)"), b, ACT.Copy).then_inc(bank_emptied_act, 1)
            act.wait_ge(ms_heads, 1)
            a_(ss1, r1, ACT.Sqrt).then_inc(rms_heads, 1)
            b = filled_bank("gv", 1)
            a_(gv[:, 1, :], b, ACT.Copy).then_inc(bank_emptied_act, 1)
            for bank in range(2):
                b = filled_bank("gout", bank)
                a_(sil[:, 2 * bank:2 * bank + 2, :].rearrange("p a b -> p (a b)"), b, ACT.Silu
                   ).then_inc(bank_emptied_act, 1)
            act.wait_ge(qk_turned, 1)
            a_(qT[:, 2:4, :].rearrange("p a b -> p (a b)"), ps[:, 1, :], ACT.Copy).then_inc(qkT_act, 1)
            a_(kT.rearrange("p a b -> p (a b)"), ps[:, 2, :], ACT.Copy).then_inc(qkT_act, 1)
            act.wait_ge(gla_o, 1)
            a_(osq.rearrange("p (a b) -> p a b", a=2), ps[:, 2:4, :], ACT.Square).then_inc(gla_sq, 1)
            act.wait_ge(gla_ms, 1)
            a_(ogla_ss, ogla_r, ACT.Sqrt).then_inc(gla_rms, 1)

            SC = HD ** -0.5
            for k in range(QH + 3):
                if k < QH:
                    s_, nm, sm = s_buf[:, k % 2, :], nmx[:, k % 2, :], sums[:, k % 2, :]
                    act.wait_ge(nmx1, k + 1)
                    for br in range(2):
                        for half, lo, hi in ((0, 0, P), (1, P, 384)):
                            o = s_[:, br * 384 + lo:br * 384 + hi]
                            a_(o, o, ACT.Exp, scale=SC, bias=nm[:, 3 * br + half:3 * br + half + 1],
                               accum_out=sm[:, 2 * br + half:2 * br + half + 1])
                    for half in range(2):
                        o = s_[:, 768 + half * NCMP:768 + (half + 1) * NCMP]
                        last = a_(o, o, ACT.Exp, scale=SC, bias=nm[:, 6 + half:7 + half],
                                  accum_out=sm[:, 4 + half:5 + half])
                    last.then_inc(exp1, 1)
                if 1 <= k <= QH:
                    i = k - 1
                    act.wait_ge(turned1, i + 1)
                    if i >= 2:
                        act.wait_ge(o1, i - 1)
                    a_(pT[:, i % 2, 0:512], ps[:, 4, :], ACT.Copy).then_inc(pT1_act, 1)
                if 2 <= k < QH + 2:
                    i = k - 2
                    act.wait_ge(o1, i + 1)
                    r0 = HD * (i % 2)
                    a_(oT[r0:r0 + HD, i // 2, :], ps[r0:r0 + HD, 6, (i % 2) * S:(i % 2 + 1) * S], ACT.Copy
                       ).then_inc(oT1, 1)

            norm(1, xn, xn)

            def ffn_step(k, done):
                for a in range(2):
                    act.wait_ge(ff_filled, 2 * done + a + 1)
                    act.wait_ge(ff_act, 2 * done + 1)
                    for g in range(2):
                        c = 2 * k + a + g * FCH
                        a_(conv_y[:, a, g, :], ps[:, a, g * S:(g + 1) * S], ACT.Identity,
                           scale=prm[:, 1, bass.ds(c, 1)], bias=prm[:, 1, bass.ds(c + 44, 1)]
                           ).then_inc(ff_read_act, 1)
                    act.wait_ge(ff_read_dve, 2 * (2 * done + a) + 2)
                    a_(sil_g[:, a, :], conv_y[:, a, 0, :], ACT.Silu).then_inc(ff_silu, 1)

            act.sem_inc(ff_read_act, 1)
            with nc.scalar.Fori(0, FCH // 4) as i:
                for s in range(2):
                    ffn_step(2 * i + s, 2 * i + s)
            ffn_step(FCH // 2 - 1, FCH // 2 - 1)

            norm(2, xn2, xn2)

            def empty2(name, bank):
                b = filled_bank(name, bank)
                m = int(name[-1])
                if name in ("q0", "q1"):
                    a_(z2[:, 1, 512 * m:512 * (m + 1)], b, ACT.Copy).then_inc(bank_emptied_act, 1)
                elif name == "kv2":
                    a_(z2[:, 1, 1024:1280], b[:, 0:256], ACT.Copy)
                    a_(v2[:, 1, :], b[:, 256:512], ACT.Copy).then_inc(bank_emptied_act, 1)
                elif name[:2] == "cc":
                    if m == 1:
                        act.wait_ge(bank_emptied_dve, emptied("D", PROD["cx0"], 1))
                    a_(cc_s[:, 2 * bank:2 * bank + 2, :].rearrange("p a b -> p (a b)"), b, ACT.Copy
                       ).then_inc(bank_emptied_act, 1)
                else:
                    dst, reader = (sg, "wco0") if name[:2] == "gc" else (sg2, "wao0")
                    if m == 1:
                        act.wait_ge(bank_emptied_dve, emptied("D", PROD[reader], 1))
                    a_(dst[:, 2 * bank:2 * bank + 2, :].rearrange("p a b -> p (a b)"), b, ACT.Sigmoid
                       ).then_inc(bank_emptied_act, 1)

            for kind, a, q in SCHEDULE2:
                if kind == "part":
                    if q % 2 and PRODUCTS[PROD[a]][1][q // 2] == "A":
                        empty2(a, q // 2)
                    if (a, q) == ("kv2", 3):
                        act.wait_ge(bank_emptied_dve, emptied("D", PROD["kv2"], 0))
                        act.wait_ge(bank_emptied_act, emptied("A", PROD["kv2"], 1))
                        for half in range(2):
                            a_(sq2[:, half, :], z2[:, half, :], ACT.Square).then_inc(sq2_ready, 1)
                        act.wait_ge(ms2_ready, 1)
                        a_(ss2, r2, ACT.Sqrt).then_inc(rms2_ready, 1)
                    if a[:2] == "cx" and q == 3:
                        m = int(a[-1])
                        act.wait_ge(bank_emptied_dve, emptied("D", PROD[a], 1))
                        if m == 1:
                            act.wait_ge(cbz_ready, 2)
                        for c in range(4):
                            last = a_(z_s[:, c, :], u_s[:, c, :], ACT.Copy,
                                      scale=prm[:, 1, 96 + 4 * m + c:97 + 4 * m + c])
                        last.then_inc(conv_mid, 1)
                elif kind == "turn":
                    act.wait_ge(turned_q2, 1)
                    for i in range(2, 4):
                        a_(q2T[:, 2 * i:2 * i + 2, :].rearrange("p a b -> p (a b)"), ps[:, 4 + i, :], ACT.Copy
                           ).then_inc(q2T_act, 1)
                else:
                    k = a
                    if k < H2:
                        act.wait_ge(nmx_2, k + 1)
                        if k >= 2:
                            act.wait_ge(turned2, k - 1)
                        for half in range(2):
                            last = a_(p2[:, k % 2, half * S:(half + 1) * S],
                                      ps[:, 4 + k % 2, half * S:(half + 1) * S], ACT.Exp, scale=HD2 ** -0.5,
                                      bias=nmx2[:, k % 2, half:half + 1], accum_out=sum2[:, k % 2, half:half + 1])
                        last.then_inc(exp2, 1)
                    if k >= 2:
                        i = k - 2
                        act.wait_ge(o2, i + 1)
                        a_(o2T[:, i, :], ps[:, 7, (i % 2) * S:(i % 2 + 1) * S], ACT.Copy).then_inc(o2T_ready, 1)

            norm(3, uN, xn_moe, gain=True)
            act.wait_ge(grp_nmax, 1)
            for half in range(2):
                a_(gexp[:, half, :], lg[:, half, 0:NG], ACT.Exp, bias=ngm[:, half, :],
                   accum_out=gsum[:, half, :]).then_inc(grp_exp, 1)
            act.wait_ge(top_diff, 1)
            a_(ex, dv, ACT.Exp).then_inc(top_exp, 1)

            def moe_iter(it):
                act.wait_ge(gathered, 2 * it + 2)
                a_(xg[:, 4:8, :], ps[:, 7, :].rearrange("p (c s) -> p c s", c=4), ACT.Copy).then_inc(xg_act, 1)
                act.wait_ge(selw_turned, it + 1)
                a_(selwT, ps[:, 5, 0:S], ACT.Copy).then_inc(selwT_ready, 1)

                def take_y(j):
                    q = (j ^ 1) * CAP
                    act.wait_ge(y_filled, 4 * it + j + 1)
                    a_(y[j * CAP:(j + 1) * CAP, 512:1024], ps[q:q + CAP, 4, :], ACT.Copy).then_inc(y_act, 1)

                for j in range(GRP):
                    q = (j ^ 1) * CAP
                    act.wait_ge(up_filled, 4 * it + j + 1)
                    if j >= 2:
                        act.wait_ge(act_ready, 4 * it + j - 1)
                    a_(hsil[q:q + CAP, j % 2, :], ps[j * CAP:(j + 1) * CAP, 1, :], ACT.Silu).then_inc(silu_ready, 1)
                    if j >= 1:
                        take_y(j - 1)
                take_y(GRP - 1)

            act.wait_ge(slots_ready, 1)
            with nc.scalar.Fori(0, NE // GRP) as it:
                moe_iter(it)
            fullest = nc.scalar.value_load(cmax[0:1, 0:1], min_val=0, max_val=S)
            with nc.scalar.Fori(1, ROUNDS) as r:
                with nc.scalar.If(fullest > r * CAP):
                    with nc.scalar.Fori(0, NE // GRP) as g:
                        moe_iter(r * (NE // GRP) + g)


SHAPES = {
    "x": (S, D), "attn_norm": (1, D), "w_in": (D, D_IN), "nsa_q_norm": (1, HD), "nsa_k_norm": (3, HD),
    "cmp_pos_k": (CMP_BLOCK, HD), "cmp_pos_v": (CMP_BLOCK, HD), "cmp_w1_k": (2048, 256), "cmp_w2_k": (256, HD),
    "cmp_w1_v": (2048, 256), "cmp_w2_v": (256, HD), "gla_w_gate2": (16, 256), "gla_b_gate": (1, 256),
    "gla_out_norm": (1, GDV), "w_out": (D, D), "ffn_norm": (1, D), "w_up": (D, 2 * FF), "conv_w": (3, 2 * FF),
    "conv_b": (1, 2 * FF), "w_down": (FF, D), "norm1_g_2": (1, D), "w_in_2": (D, D_IN2), "conv_w_2": (3, D),
    "q_norm_g_2": (1, HD2), "k_norm_g_2": (1, HD2), "w_conv_out_2": (D, D), "w_attn_out_2": (D, D),
    "w_o_2": (D, D), "norm2_g_2": (1, D), "w_group_2": (D, NG), "w_router_2": (D, NE),
    "w1_2": (NE, P, KC * DE), "w3_2": (NE, P, KC * DE), "w2_2": (NE, P, (DE // P) * D),
}
ALIAS = {"cmp_pos_k": "pe_k", "cmp_pos_v": "pe_v", "gla_b_gate": "b_gate", "w1_2": "w1", "w3_2": "w3", "w2_2": "w2"}


def kernel(**inputs):
    import concourse.bacc as _bacc
    from concourse.bass_utils import run_bass_kernel_spmd as _run

    nc = _bacc.Bacc("TRN2", target_bir_lowering=False, num_devices=1)
    arrays, t = {}, {}
    for name, shape in SHAPES.items():
        arrays["in_" + name] = np.ascontiguousarray(inputs[name]).reshape(shape)
        t[ALIAS.get(name, name)] = nc.dram_tensor("in_" + name, shape, F32, kind="ExternalInput").ap()
    arrays["in_consts"] = shape_constants()
    t["consts"] = nc.dram_tensor("in_consts", (P, N_CONST), F32, kind="ExternalInput").ap()
    out = nc.dram_tensor("out_0", (1, S, D), F32, kind="ExternalOutput").ap()
    two_blocks(nc, t, out.rearrange("a s d -> (a s) d"))
    r = _run(nc, [arrays], core_ids=[0])
    return r.results[0]["out_0"]
```

```python
from contextlib import ExitStack

import numpy as np
import concourse.bass as bass
from concourse import mybir

F32 = mybir.dt.float32
I32 = mybir.dt.int32
U32 = mybir.dt.uint32
ALU = mybir.AluOpType
ACT = mybir.ActivationFunctionType
AX = mybir.AxisListType

P = 128
S = 256
D = 1024
KC = D // P
EPS = 1e-6
NEG = -1e30

QH, HD, G = 8, 64, 2
NCMP, CMP_STRIDE, CMP_BLOCK = 15, 16, 32
CMP_ROWS = 2 * CMP_STRIDE + NCMP
GH, GDK, GDV, L = 4, 64, 128, 64
TAU = 16.0
FF = 2816
FCH = FF // P
QKV0, KV0, GATE0, GQ0, GV0, GLR0, GOUT0 = 0, 512, 1280, 1304, 1816, 2328, 2344
D_IN = 2856

H2, HD2 = 8, 128
D_IN2 = 6656
CB0, CC0, CX0, Q20, KV20, GC0, GA0 = 0, 1024, 2048, 3072, 4096, 4608, 5632
NE, NG, EPG, DE = 64, 8, 8, 512
CAP = 32
ROUNDS = S // CAP
GRP = P // CAP

CONST_COLS = dict(ident=P, causal3=3 * P, chunk_mask=P, before=P, ones=P, slot_iota=P, iota64=NE,
                  cos1=16, sin1=16, cosc=8, sinc=8, cmp_bias=2 * NCMP, cmp_keep=2 * NCMP,
                  cos2=2 * 64, sin2=2 * 64)
CONST_AT, _n = {}, 0
for _k, _w in CONST_COLS.items():
    CONST_AT[_k] = (_n, _n + _w)
    _n += _w
N_CONST = _n


def shape_constants():
    c = np.zeros((P, N_CONST), np.float32)

    def put(name, a):
        a = np.asarray(a, np.float32)
        a = a.reshape(a.shape[0], -1)
        lo, hi = CONST_AT[name]
        c[:a.shape[0], lo:hi] = a

    i = np.arange(P)
    put("ident", np.eye(P))
    diag = np.where(i[None, :] <= i[:, None], 0.0, NEG)
    put("causal3", np.stack([diag, np.zeros((P, P)), diag], 1))
    put("chunk_mask", (i[:, None] <= i[None, :]) & (i[:, None] // L == i[None, :] // L))
    put("before", i[:, None] < i[None, :])
    put("ones", np.ones((P, P)))
    put("slot_iota", np.broadcast_to(np.tile(np.arange(CAP), GRP), (P, P)))
    put("iota64", np.broadcast_to(np.arange(NE), (P, NE)))
    f = np.float32
    inv = f(500000.0) ** (-np.arange(8, dtype=f) / f(8))
    tok = (np.arange(2)[None, :] * P + i[:, None]).astype(f)
    ang = (tok[:, :, None] * inv).astype(f)
    put("cos1", np.cos(ang))
    put("sin1", np.sin(ang))
    end = (np.arange(NCMP) * CMP_STRIDE + CMP_BLOCK - 1).astype(f)
    angc = (end[:, None] * inv).astype(f)
    put("cosc", np.cos(angc))
    put("sinc", np.sin(angc))
    seen = end[None, None, :] <= tok[:, :, None]
    put("cmp_bias", np.where(seen, 0.0, NEG))
    put("cmp_keep", seen)
    inv2 = f(10000.0) ** (-np.arange(0, 64, 2, dtype=f) / f(64))
    row, col = np.floor(tok / 64), tok % 64
    ang2 = np.concatenate([(row[:, :, None] * inv2), (col[:, :, None] * inv2)], -1).astype(f)
    put("cos2", np.cos(ang2))
    put("sin2", np.sin(ang2))
    return c


UNITS = ["cmp_in", "kv_tok", "q_tok", "cmp1k", "cmp1v", "gqk", "gv", "gout", "wout0", "wout1"]
U_FFN = len(UNITS)
for _i in range(FCH // 2):
    UNITS += [f"up{_i}", f"down{_i}"]
U_BLK2 = len(UNITS)
UNITS += ["q0", "q1", "kv2", "cc0", "cx0", "cb0", "cc1", "cx1", "cb1",
          "gc0", "wco0", "ga0", "wao0", "gc1", "wco1", "ga1", "wao1", "wo0", "wo1"]
UNIT = {n: i for i, n in enumerate(UNITS)}
RING = 4

PRODUCTS = [("cmp_in", "DA"), ("kv_tok", "DA"), ("q_tok", "DA"), ("gqk", "DA"), ("gv", "DA"),
            ("gout", "AA"), ("wout0", "DD"), ("wout1", "DD"),
            ("q0", "DA"), ("q1", "DA"), ("kv2", "DA"),
            ("cc0", "AA"), ("cx0", "DD"), ("cb0", "DD"), ("cc1", "AA"), ("cx1", "DD"), ("cb1", "DD"),
            ("gc0", "AA"), ("wco0", "DD"), ("ga0", "AA"), ("wao0", "DD"),
            ("gc1", "AA"), ("wco1", "DD"), ("ga1", "AA"), ("wao1", "DD"), ("wo0", "DD"), ("wo1", "DD")]
PROD = {n: i for i, (n, _) in enumerate(PRODUCTS)}


def emptied(engine, step, bank):
    flat = "".join(e for _, e in PRODUCTS[:step]) + PRODUCTS[step][1][:bank + 1]
    return flat.count(engine)


def filled(step, bank):
    return 2 * step + bank + 1


ATTN_STEPS = H2 + 2
SCHEDULE2, _k = [], 0
for _n in ("q0", "q1", "kv2", "cc0", "cx0"):
    SCHEDULE2 += [("part", _n, _q) for _q in range(4)]
SCHEDULE2.append(("turn", 0, 0))
for _n in ("cb0", "cc1", "cx1", "cb1"):
    for _q in range(4):
        if _k < ATTN_STEPS:
            SCHEDULE2.append(("attn", _k, 0))
            _k += 1
        SCHEDULE2.append(("part", _n, _q))
for _n in ("gc0", "wco0", "ga0", "wao0", "gc1", "wco1", "ga1", "wao1", "wo0", "wo1"):
    SCHEDULE2 += [("part", _n, _q) for _q in range(4)]


def two_blocks(nc, t, out):
    with ExitStack() as ctx:
        def sb(name, shape, dt=F32):
            return ctx.enter_context(nc.sbuf_tensor(name, shape, dt))

        def sem(name):
            return ctx.enter_context(nc.semaphore(name))

        ps = ctx.enter_context(nc.psum_tensor("ps", [P, 8, 512], F32))
        dense_ring = sb("dense_ring", [P, RING, 4096])
        expert_ring = sb("expert_ring", [P, 2, 3, 4096])
        h = sb("h", [P, 2, D])
        hT = sb("hT", [P, KC, S])
        consts = sb("consts", [P, N_CONST])
        chunk_mask = sb("chunk_mask", [P, P], U32)
        gains = sb("gains", [P, 64 + 192 + 128 + 128 + D])
        gcol = sb("gcol", [P, 3, KC])
        prm_rows = sb("prm_rows", [P, 2, P])
        prm = sb("prm", [P, 2, P])
        router_w = sb("router_w", [P, KC, NG + NE])
        wgate2 = sb("wgate2", [P, S])
        cmp_w2 = sb("cmp_w2", [P, 2, 2, HD])
        ssq = sb("ssq", [P, 2])
        msq = sb("msq", [P, 2])
        rms = sb("rms", [P, 2])
        rstd = sb("rstd", [P, 2])
        tail = sb("tail", [P, 64])
        moe_tokens = sb("moe_tokens", [P, KC, P])
        moe_silu = sb("moe_silu", [P, 2, DE])

        def const(name, rows=P):
            lo, hi = CONST_AT[name]
            return consts[0:rows, lo:hi]

        def by_pairs(z):
            return z.rearrange("p (j g d) -> p g j d", g=G, j=4)

        def gla_index(head, half):
            return (head % 2) * 4 + (head // 2) * 2 + half

        ident = const("ident")
        q_gain1, k_gains1 = gains[:, 0:64], gains[:, 64:256]
        q_gain2, k_gain2, norm_gain2 = gains[:, 256:384], gains[:, 384:512], gains[:, 512:512 + D]
        pe_kT, pe_vT, b_gateT = prm[:, 0, 88:104], prm[:, 0, 104:120], prm[:, 0, 120:122]
        out_gainT = prm[:, 1, 112:113]

        flat0 = expert_ring[:, 0, :, :].rearrange("p a b -> p (a b)")
        flat1 = expert_ring[:, 1, :, :].rearrange("p a b -> p (a b)")

        def carve(flat):
            at = [0]

            def take(*shape):
                n = int(np.prod(shape))
                v = flat[:, at[0]:at[0] + n]
                at[0] += n
                assert at[0] <= flat.shape[1]
                if len(shape) == 2:
                    v = v.rearrange("p (a b) -> p a b", a=shape[0])
                elif len(shape) == 3:
                    v = v.rearrange("p (a b c) -> p a b c", a=shape[0], b=shape[1])
                return v
            return take

        s0 = carve(flat0)
        zq, zkv, ckv = s0(2, 512), s0(2, 512), s0(256)
        sq1 = s0(2, 1024)
        qT, kT, kcT = s0(4, S), s0(2, S), s0(16)
        rope_tmp = s0(4, 64)
        kk = s0(2, 3, S)
        hid_bias = s0(4)
        cmp_hid = s0(256)
        gelu_h = s0(2, 2, 30)
        ss1, r1 = s0(26), s0(26)
        gates = s0(2, 24)
        s_buf = s0(2, 798)
        pT = s0(2, 1024)
        mx, nmx, sums, wts = s0(2, 8), s0(2, 8), s0(2, 8), s0(2, 8)
        s1 = carve(flat1)
        xn = s1(2, D)
        glrT, gq, gk = s1(S), s1(2, S), s1(2, S)
        gla_tmp = s1(4, S)
        gt, ga_ = gla_tmp[:, 0:2, :], gla_tmp[:, 2:4, :]
        gl_, cum, e_pos, e_neg, khatT = (s1(2, S) for _ in range(5))
        blast, decay = s1(2, 4), s1(2, 4)
        qt, kt, khat = s1(2, S), s1(2, S), s1(2, S)
        gv, sil = s1(2, 512), s1(4, S)
        attT = s1(8, P)
        state = gla_tmp.rearrange("p a b -> p (a b)")[:, 0:768].rearrange("p (a b c) -> p a b c", a=2, b=3)
        ogla_ss, ogla_r = s1(8), s1(8)
        oT = hT
        ogla, osq = xn[:, 0, :], xn[:, 1, :]
        f0 = carve(flat0)
        conv_y = f0(2, 2, S)
        sil_g = f0(2, S)
        act_T = f0(2, 2, S)
        b0 = carve(flat0)
        z2 = b0(2, 1280)
        v2 = b0(2, 256)
        sq2 = b0(2, 1280)
        q2T, k2T = b0(H2, S), b0(2, S)
        p2 = b0(2, 512)
        p2T = b0(2, 512)
        mx2, nmx2, sum2, rs2 = b0(2, 2), b0(2, 2), b0(2, 2), b0(2, 2)
        ss2, r2 = b0(20), b0(20)
        b1 = carve(flat1)
        xn2 = b1(2, D)
        cc_s, u_s, z_s = b1(4, S), b1(4, S), b1(4, S)
        cbz, o2T = b1(KC, S), b1(KC, S)
        sg, sg2 = b1(4, S), b1(4, S)
        mtmp = b1(512)
        mrg = xn2.rearrange("p a b -> p (a b)").rearrange("p (c s) -> p c s", c=KC)
        SPARE = [UNIT["ga1"] % RING, UNIT["wo0"] % RING]
        m0, m1 = carve(dense_ring[:, UNIT["wao1"] % RING, :]), carve(dense_ring[:, UNIT["wo1"] % RING, :])
        uN, xn_moe = m0(2, D), m0(2, D)
        lg = m1(2, NG + NE)
        g8, e8 = m1(2, 8), m1(2, 8)
        gi8u, ei8u = m1(2, 8).bitcast(U32), m1(2, 8).bitcast(U32)
        gi8, ei8 = m1(2, 8), m1(2, 8)
        gexp, gsum, pg = m1(2, 8), m1(2, 1), m1(2, 1)
        goh, gohb = m1(2, 8), m1(2, 8)
        elm = m1(2, NE)
        dv, ex, den, rden, w1t, w2t, ngm = (m1(2, 1) for _ in range(7))
        oh1, oh2, assign, wmat = (m1(2, NE) for _ in range(4))
        slot = m1(2, NE)
        cnt = m1(NE)
        cmax_f = m1(1)
        cmax = m1(1).bitcast(I32)
        sel, selw = m1(2, P), m1(2, P)
        selwT = m1(S)
        xg = moe_tokens[:]
        hsil, hid = moe_silu[:], m1(2, DE)
        aT = m1(2, P)
        y = xn_moe[:, 0, :]

        def norm_bank(k, c):
            return ps[:, (4 if k in (1, 3) else 0) + c // 2, (c % 2) * S:(c % 2 + 1) * S]

        consts_in, x_in, rows_in, gains_in = sem("consts_in"), sem("x_in"), sem("rows_in"), sem("gains_in")
        gcol_in, small_in, out_done = sem("gcol_in"), sem("small_in"), sem("out_done")
        dense_loaded = [sem(f"dense_loaded{i}") for i in range(RING)]
        dense_used = sem("dense_used")
        up_loaded = [sem(f"up_loaded{i}") for i in range(2)]
        dn_loaded = [sem(f"dn_loaded{i}") for i in range(2)]
        up_free, dn_free, spare_loaded = sem("up_free"), sem("dn_free"), sem("spare_loaded")
        dve_step, act_step = sem("dve_step"), sem("act_step")
        zeroed = sem("zeroed")
        prm_turned, prm_ready = sem("prm_turned"), sem("prm_ready")
        h_ready = sem("h_ready")
        ssq_ready, msq_ready, rms_ready, rstd_ready = (sem(n) for n in ("ssq_ready", "msq_ready", "rms_ready", "rstd_ready"))
        xn_ready = sem("xn_ready")
        xT_turned, hT_dve, hT_act = sem("xT_turned"), sem("hT_dve"), sem("hT_act")
        bank_filled, bank_emptied_dve, bank_emptied_act = sem("bank_filled"), sem("bank_emptied_dve"), sem("bank_emptied_act")
        emptied_sem = {"D": bank_emptied_dve, "A": bank_emptied_act}
        cmp_rows_ready, cmp_rows_in = sem("cmp_rows_ready"), sem("cmp_rows_in")
        cmp_hidden, cmp_bias_ready, gelu_ready, cmp_kv_ready = (sem(n) for n in ("cmp_hidden", "cmp_bias_ready", "gelu_ready", "cmp_kv_ready"))
        sq_q, ms_heads, rms_heads = sem("sq_q"), sem("ms_heads"), sem("rms_heads")
        roped, qk_turned, qkT_dve, qkT_act = (sem(n) for n in ("roped", "qk_turned", "qkT_dve", "qkT_act"))
        gate_logits, gate_abs, gate_log, cum_ready = (sem(n) for n in ("gate_logits", "gate_abs", "gate_log", "cum_ready"))
        exps_ready, gla_qk_ready, khat_ready, khat_turned, khat_rows = (sem(n) for n in ("exps_ready", "gla_qk_ready", "khat_ready", "khat_turned", "khat_rows"))
        att_filled, att_masked, ds_filled, states_ready = (sem(n) for n in ("att_filled", "att_masked", "ds_filled", "states_ready"))
        gla_o, gla_sq, gla_ms, gla_rms, gla_on, gla_turned, gla_oT = (sem(n) for n in ("gla_o", "gla_sq", "gla_ms", "gla_rms", "gla_on", "gla_turned", "gla_oT"))
        scores1, nmx1, exp1, scaled1, turned1, pT1, o1, oT1 = (sem(n) for n in (
            "scores1", "nmx1", "exp1", "scaled1", "turned1", "pT1", "o1", "oT1"))
        ff_filled, ff_read_act, ff_read_dve, ff_silu, ff_act = (sem(n) for n in (
            "ff_filled", "ff_read_act", "ff_read_dve", "ff_silu", "ff_act"))
        ff_down, ff_added, ffn_chain = sem("ff_down"), sem("ff_added"), sem("ffn_chain")
        conv_mid, cbz_ready = sem("conv_mid"), sem("cbz_ready")
        sq2_ready, ms2_ready, rms2_ready, roped2, turned_q2, q2T_dve, q2T_act = (sem(n) for n in (
            "sq2_ready", "ms2_ready", "rms2_ready", "roped2", "turned_q2", "q2T_dve", "q2T_act"))
        scores2, nmx_2, exp2, scaled2, turned2, pT2, o2, o2T_ready = (sem(n) for n in (
            "scores2", "nmx_2", "exp2", "scaled2", "turned2", "pT2", "o2", "o2T_ready"))
        merged = sem("merged")
        logits_ready, grp_nmax, grp_exp, top_diff, top_exp = (sem(n) for n in (
            "logits_ready", "grp_nmax", "grp_exp", "top_diff", "top_exp"))
        assigned, ranks_ready, slots_ready = sem("assigned"), sem("ranks_ready"), sem("slots_ready")
        sel_ready, selw_turned, selwT_ready = sem("sel_ready"), sem("selw_turned"), sem("selwT_ready")
        gathered, xg_dve, xg_act, up_filled, silu_ready, act_ready, hid_turned, aT_ready = (sem(n) for n in (
            "gathered", "xg_dve", "xg_act", "up_filled", "silu_ready", "act_ready", "hid_turned", "aT_ready"))
        y_filled, y_dve, y_act, scattered, summed = (sem(n) for n in ("y_filled", "y_dve", "y_act", "scattered", "summed"))
        moe_step, moe_round = sem("moe_step"), sem("moe_round")
        last_ready = sem("last_ready")

        block = ctx.enter_context(nc.Block())

        def w_in_view(w, c0, n):
            return t[w][:, c0:c0 + n].rearrange("(p c) n -> p c n", c=KC)

        def w_nat_view(w, c0, n):
            return t[w][:, c0:c0 + n].rearrange("(c p) n -> p c n", p=P)

        def unit_loads(name, slot):
            full = dense_ring[:, slot, :].rearrange("p (c n) -> p c n", c=KC)
            cols2 = {"q": Q20, "cc": CC0, "cx": CX0, "cb": CB0, "gc": GC0, "ga": GA0}
            if name == "cmp_in":
                return [(full[:, :, 0:256], w_in_view("w_in", KV0, 256)),
                        (full[:, :, 256:280], w_in_view("w_in", GATE0, 24)),
                        (full[:, :, 280:296], w_in_view("w_in", GLR0, 16))]
            if name in ("kv_tok", "q_tok", "gqk", "gv", "gout"):
                c0 = {"kv_tok": KV0 + 256, "q_tok": QKV0, "gqk": GQ0, "gv": GV0, "gout": GOUT0}[name]
                return [(full, w_in_view("w_in", c0, 512))]
            if name in ("cmp1k", "cmp1v"):
                src = t["cmp_w1_k" if name == "cmp1k" else "cmp_w1_v"]
                return [(dense_ring[:, slot, :].rearrange("p (c n) -> p c n", n=256),
                         src.rearrange("(c p) n -> p c n", p=P))]
            m = int(name[-1])
            if name[:-1] == "kv":
                return [(full, w_in_view("w_in_2", KV20, 512))]
            if name[:-1] in cols2:
                return [(full, w_in_view("w_in_2", cols2[name[:-1]] + 512 * m, 512))]
            src = {"wout": "w_out", "wco": "w_conv_out_2", "wao": "w_attn_out_2", "wo": "w_o_2"}[name[:-1]]
            return [(full, w_nat_view(src, 512 * m, 512))]

        @block.sync
        def _(sp):
            for half in range(2):
                sp.dma_start(h[:, half, :], t["x"][half * P:(half + 1) * P, :]).then_inc(x_in, 16)

            def released(u):
                k, down = divmod(u - U_FFN, 2)
                if not 0 <= k < FCH // 2:
                    return u + 1
                return U_FFN + (min(2 * k + 3, FCH) if down else max(2 * k, 1))

            def static_units(lo, hi):
                for u in range(lo, hi):
                    if u >= RING:
                        sp.wait_ge(dense_used, released(u - RING))
                    for dst, src in unit_loads(UNITS[u], u % RING):
                        sp.dma_start(dst, src).then_inc(dense_loaded[u % RING], 16)

            sp.dma_start(consts[:], t["consts"]).then_inc(consts_in, 16)
            static_units(0, U_FFN)

            w_up = t["w_up"].rearrange("(p c) n -> p c n", c=KC)
            w_down = t["w_down"].rearrange("(a p) n -> p a n", p=P)

            def ffn_unit(k, s):
                up_slot, dn_slot = (U_FFN + 2 * s) % RING, (U_FFN + 2 * s + 1) % RING
                up = dense_ring[:, up_slot, :].rearrange("p (c g n) -> p c g n", c=KC, g=2)
                sp.wait_ge(dense_used, 2 * k + U_FFN - 3)
                for g in range(2):
                    sp.dma_start(up[:, :, g, :], w_up[:, :, bass.ds(g * FF + k * 256, 256)]
                                 ).then_inc(dense_loaded[up_slot], 8 * 2)
                dn = dense_ring[:, dn_slot, 0:2048].rearrange("p (a n) -> p a n", a=2)
                sp.wait_ge(dense_used, 2 * k + U_FFN - 1)
                sp.dma_start(dn, w_down[:, bass.ds(k * 2, 2), :]).then_inc(dense_loaded[dn_slot], 16)

            with nc.sync.Fori(0, FCH // 4) as i:
                for s in range(2):
                    ffn_unit(2 * i + s, s)
            ffn_unit(FCH // 2 - 1, 0)
            static_units(U_BLK2, len(UNITS))

            def up_load(it, j, slot):
                e = (it % (NE // GRP)) * GRP + j
                sp.wait_ge(up_free, it * GRP + j + 1)
                for k, w in ((0, "w1"), (1, "w3")):
                    sp.dma_start(expert_ring[:, slot, k, :], t[w][bass.ds(e, 1), :, :].rearrange("o p n -> p (o n)")
                                 ).then_inc(up_loaded[slot], 16)

            def down_load(it, j):
                e = (it % (NE // GRP)) * GRP + j
                sp.wait_ge(dn_free, it * GRP + j + 1)
                sp.dma_start(expert_ring[:, j % 2, 2, :], t["w2"][bass.ds(e, 1), :, :].rearrange("o p n -> p (o n)")
                             ).then_inc(dn_loaded[j % 2], 16)

            up_load(0, 0, 0)
            down_load(0, 0)
            for w, unit, slot in (("w1", "ga1", SPARE[0]), ("w3", "wo0", SPARE[1])):
                sp.wait_ge(dense_used, released(UNIT[unit]))
                sp.dma_start(dense_ring[:, slot, :], t[w][2, :, :]).then_inc(spare_loaded, 16)
            up_load(0, 1, 1)
            down_load(0, 1)
            sp.wait_ge(up_free, 3)
            for k, w in ((0, "w1"), (1, "w3")):
                sp.dma_start(expert_ring[:, 0, k, :], t[w][3, :, :]).then_inc(up_loaded[0], 16)
            down_load(0, 2)
            down_load(0, 3)

            with nc.sync.Fori(1, NE // GRP) as it:
                for j in range(GRP):
                    up_load(it, j, (j + 1) % 2)
                    down_load(it, j)
            sp.wait_ge(slots_ready, 1)
            fullest = nc.sync.value_load(cmax[0:1, 0:1], min_val=0, max_val=S)
            with nc.sync.Fori(1, ROUNDS) as r:
                with nc.sync.If(fullest > r * CAP):
                    with nc.sync.Fori(0, NE // GRP) as g:
                        for j in range(GRP):
                            up_load(r * (NE // GRP) + g, j, (j + 1) % 2)
                            down_load(r * (NE // GRP) + g, j)
            sp.wait_ge(last_ready, 1)
            for half in range(2):
                sp.dma_start(out[half * P:(half + 1) * P, :], h[:, half, :]).then_inc(out_done, 16)
            sp.wait_ge(out_done, 32)

        @block.gpsimd
        def _(pool):
            A = prm_rows[:, 0, :]
            B = prm_rows[:, 1, :]
            cw = t["conv_w"].rearrange("k (c n) -> (k c) n", n=P)
            for i, n in enumerate(("attn_norm", "ffn_norm", "norm1_g_2")):
                pool.dma_start(gcol[:, i, :], t[n].rearrange("o (p c) -> p (o c)", c=KC)).then_inc(gcol_in, 16)
            for dst, src in ((A[0:88, :], cw[0:88, :]), (A[88:104, :], t["pe_k"].rearrange("(a b) n -> a (b n)", b=2)),
                             (A[104:120, :], t["pe_v"].rearrange("(a b) n -> a (b n)", b=2)),
                             (A[120:122, :], t["b_gate"].rearrange("o (c n) -> (o c) n", n=P)),
                             (B[0:44, :], cw[88:132, :]),
                             (B[44:88, :], t["conv_b"].rearrange("o (c n) -> (o c) n", n=P)),
                             (B[88:112, :], t["conv_w_2"].rearrange("k (c n) -> (k c) n", n=P)),
                             (B[112:113, :], t["gla_out_norm"])):
                pool.dma_start(dst, src).then_inc(rows_in, 16)
            pool.dma_start(wgate2[0:16, :], t["gla_w_gate2"]).then_inc(small_in, 16)
            for i, n in enumerate(("cmp_w2_k", "cmp_w2_v")):
                pool.dma_start(cmp_w2[:, i, :, :], t[n].rearrange("(m p) d -> p m d", p=P)).then_inc(small_in, 16)
            pool.dma_start(router_w[:, :, 0:NG], t["w_group_2"].rearrange("(p c) n -> p c n", c=KC)).then_inc(small_in, 16)
            pool.dma_start(router_w[:, :, NG:], t["w_router_2"].rearrange("(p c) n -> p c n", c=KC)).then_inc(small_in, 16)
            for dst, n in ((q_gain1, "nsa_q_norm"), (k_gains1, "nsa_k_norm"), (q_gain2, "q_norm_g_2"),
                           (k_gain2, "k_norm_g_2"), (norm_gain2, "norm2_g_2")):
                pool.dma_start(dst, t[n].rearrange("a b -> (a b)").partition_broadcast(P)).then_inc(gains_in, 16)

        GCOL_IN, ROWS_IN, SMALL_IN, GAINS_IN = 16 * 3, 16 * 8, 16 * 5, 16 * 5

        @block.tensor
        def _(pe):
            mm = nc.tensor.matmul
            turn = nc.tensor.transpose

            def slot_view(u):
                return dense_ring[:, u % RING, :].rearrange("p (c n) -> p c n", c=KC)

            def norm_turn(k, src):
                if k == 0:
                    pe.wait_ge(consts_in, 16)
                view = src.rearrange("p a (n c) -> p a c n", c=KC)
                for half in range(2):
                    pe.wait_ge(xn_ready, 2 * k + half + 1)
                    for c in range(KC):
                        last = turn(norm_bank(k, c)[:, half * P:(half + 1) * P], view[:, half, c, :], ident)
                        if half and c % 2:
                            last.then_inc(xT_turned, 1)

            def wait_hT(k):
                pe.wait_ge(hT_dve, 4 * (k + 1))
                pe.wait_ge(hT_act, 4 * (k + 1))

            def wait_bank(step, bank):
                if step >= 2:
                    eng = PRODUCTS[step - 2][1][bank]
                    pe.wait_ge(emptied_sem[eng], emptied(eng, step - 2, bank))

            def release(step):
                pe.wait_ge(bank_filled, filled(step, 1))
                pe.sem_inc(dense_used, 1)

            def part(name, xT, rows, q):
                u, step = UNIT[name], PROD[name]
                w = slot_view(u)
                if q == 0:
                    pe.wait_ge(dense_loaded[u % RING], dense_value(u))
                pair = 2 * (step % 2)
                bank = q // 2
                if q % 2 == 0:
                    wait_bank(step, bank)
                if q == 1 and name not in ("kv_tok", "gqk", "wout0", "q0"):
                    release(step - 1)
                if rows:
                    for c in range(4 * (q % 2), 4 * (q % 2) + 4):
                        last = mm(ps[:, pair + bank, :], xT[:, c, bank * P:(bank + 1) * P], w[:, c, :],
                                  start=(c == 0), stop=(c == KC - 1))
                else:
                    o = ps[:, pair + bank, (q % 2) * S:(q % 2 + 1) * S]
                    for c in range(KC):
                        last = mm(o, w[:, c, q * P:(q + 1) * P], xT[:, c, :], start=(c == 0), stop=(c == KC - 1))
                if q % 2 == 1:
                    last.then_inc(bank_filled, 1)

            def dense_value(u):
                n = 0
                for v in range(u % RING, u + 1, RING):
                    n += 3 if v == 0 else 2 if UNITS[v].startswith("up") else 1
                return 16 * n

            norm_turn(0, xn)
            wait_hT(0)
            u, w = UNIT["cmp_in"], slot_view(UNIT["cmp_in"])
            pe.wait_ge(dense_loaded[u % RING], dense_value(u))
            for i in range(2):
                for c in range(KC):
                    last = mm(ps[:, 0, i * S:(i + 1) * S], w[:, c, i * P:(i + 1) * P], hT[:, c, :],
                              start=(c == 0), stop=(c == KC - 1))
            last.then_inc(bank_filled, 1)
            for half in range(2):
                for c in range(KC):
                    mm(ps[:, 1, half * 24:(half + 1) * 24], hT[:, c, half * P:(half + 1) * P], w[:, c, 256:280],
                       start=(c == 0), stop=(c == KC - 1))
            for c in range(KC):
                last = mm(ps[0:16, 1, P:P + S], w[:, c, 280:296], hT[:, c, :], start=(c == 0), stop=(c == KC - 1))
            last.then_inc(bank_filled, 1)
            pe.wait_ge(bank_filled, filled(0, 1))
            pe.sem_inc(dense_used, 1)
            pe.wait_ge(rows_in, ROWS_IN)
            turn(ps[:, 7, 0:122], prm_rows[0:122, 0, :], ident[0:122, 0:122])
            turn(ps[:, 7, 128:241], prm_rows[0:113, 1, :], ident[0:113, 0:113]).then_inc(prm_turned, 1)
            for q in range(4):
                part("kv_tok", hT, True, q)
            pe.wait_ge(small_in, SMALL_IN)
            pe.wait_ge(bank_emptied_act, 1)
            pe.wait_ge(prm_ready, 1)
            for c in range(2):
                last = mm(ps[:, 7, c * S:(c + 1) * S], wgate2[0:16, c * P:(c + 1) * P], glrT[0:16, :],
                          start=True, stop=True)
            last.then_inc(gate_logits, 1)
            for q in range(4):
                part("q_tok", hT, True, q)

            pe.wait_ge(bank_emptied_dve, 1)
            w1_cmp = []
            for name in ("cmp1k", "cmp1v"):
                u = UNIT[name]
                w1_cmp.append(dense_ring[:, u % RING, :].rearrange("p (c n) -> p c n", n=256))
                pe.wait_ge(dense_loaded[u % RING], dense_value(u))
            for c in range(16):
                for i in range(2):
                    windows = kk[:, i, :, :].rearrange("p a b -> p (a b)")[:, 2 * c:2 * c + CMP_STRIDE * (CMP_ROWS - 1) + 1:CMP_STRIDE]
                    last = mm(ps[64 * i:64 * i + CMP_ROWS, 4, 0:256], windows, w1_cmp[i][:, c, :],
                              start=(c == 0), stop=(c == 15))
            last.then_inc(cmp_rows_ready, 1)
            release(PROD["q_tok"])
            pe.wait_ge(cmp_rows_ready, 1)
            pe.sem_inc(dense_used, 2)
            for q in range(2):
                part("gqk", hT, False, q)
            for i in range(2):
                pe.wait_ge(cmp_rows_in, 2)
                rows = slice(64 * i, 64 * i + CMP_ROWS)
                for m in range(2):
                    last = turn(ps[:, 5 - i, m * 64:m * 64 + CMP_ROWS], cmp_hid[rows, m * P:(m + 1) * P],
                                ident[rows, rows])
                last.then_inc(cmp_hidden, 1)
            for q in range(2, 4):
                part("gqk", hT, False, q)
            for i in range(2):
                pe.wait_ge(gelu_ready, i + 1)
                for g in range(G):
                    for m in range(2):
                        last = mm(ps[0:NCMP, 6, i * P + g * HD:i * P + (g + 1) * HD],
                                  gelu_h[:, i, m, g * NCMP:(g + 1) * NCMP], cmp_w2[:, i, m, :],
                                  start=(m == 0), stop=(m == 1))
            last.then_inc(cmp_kv_ready, 1)
            for q in range(4):
                part("gv", hT, True, q)
            for q in range(4):
                part("gout", hT, False, q)

            release(PROD["gout"])
            pe.wait_ge(roped, 1)
            pe.wait_ge(bank_emptied_dve, emptied("D", PROD["gv"], 1))
            pe.wait_ge(bank_emptied_act, emptied("A", PROD["gout"], 1))
            for j in range(4):
                for half in range(2):
                    last = turn(ps[:, j // 2, (j % 2) * S + half * P:(j % 2) * S + (half + 1) * P],
                                zq[:, half, j * P:(j + 1) * P], ident)
            for br in range(2):
                for half in range(2):
                    turn(ps[:, 2, br * S + half * P:br * S + (half + 1) * P],
                         zkv[:, half, br * 256:br * 256 + P], ident)
            turn(ps[:, 3, 0:NCMP], ckv[0:NCMP, 0:P], ident[0:NCMP, 0:NCMP]).then_inc(qk_turned, 1)

            pe.wait_ge(khat_ready, 1)
            pe.wait_ge(gate_abs, 1)
            for c in range(2):
                for half in range(2):
                    last = turn(ps[:, 7, half * S + c * P:half * S + (c + 1) * P],
                                khatT[:, c, half * P:(half + 1) * P], ident)
            last.then_inc(khat_turned, 1)
            pe.wait_ge(gla_qk_ready, 2)
            pe.wait_ge(cmp_bias_ready, 1)
            pe.wait_ge(gelu_ready, 2)
            for hh in range(GH):
                r0 = GDK * (hh % 2)
                for half in range(2):
                    i = gla_index(hh, half)
                    last = mm(ps[:, 4 + i // 4, (i % 4) * P:(i % 4 + 1) * P],
                              kt[r0:r0 + GDK, hh // 2, half * P:(half + 1) * P],
                              qt[r0:r0 + GDK, hh // 2, half * P:(half + 1) * P], start=True, stop=True)
            last.then_inc(att_filled, 1)
            pe.wait_ge(khat_rows, 1)
            pe.wait_ge(qkT_dve, 2)
            pe.wait_ge(qkT_act, 2)
            for hh in range(GH):
                for c in range(3):
                    r0 = L * (c % 2)
                    col = (hh // 2 * 2 + c // 2) * P
                    last = mm(ps[GDK * (hh % 2):GDK * (hh % 2) + GDK, c % 2, col:col + P],
                              khat[r0:r0 + L, c // 2, hh * GDK:(hh + 1) * GDK],
                              gv[r0:r0 + L, c // 2, hh * GDV:(hh + 1) * GDV], start=True, stop=True,
                              skip_group_check=True)
            last.then_inc(ds_filled, 1)
            pe.wait_ge(att_masked, 1)
            pe.wait_ge(states_ready, 1)
            for hh in range(GH):
                for half in range(2):
                    i = gla_index(hh, half)
                    bank, col = 2 + i // 4, (i % 4) * P
                    mm(ps[:, bank, col:col + P], attT[:, i, :], gv[:, half, hh * GDV:(hh + 1) * GDV],
                       start=True, stop=False, skip_group_check=True)
                    for c in (2 * half, 2 * half + 1):
                        if c == 0:
                            continue
                        r0, t0 = GDK * (hh % 2), L * (c % 2)
                        last = mm(ps[t0:t0 + L, bank, col:col + P],
                                  qt[r0:r0 + GDK, hh // 2, c * L:(c + 1) * L],
                                  state[r0:r0 + GDK, hh // 2, c - 1, :], start=False, stop=(c % 2 == 1),
                                  skip_group_check=True)
            def scores_of1(k):
                g, j = k // 4, k % 4
                r0, b = HD * g, 2 * (k % 2)
                if k >= 2:
                    pe.wait_ge(nmx1, k - 1)
                for br in range(2):
                    mm(ps[:, b + br, 0:P], qT[r0:r0 + HD, j, 0:P], kT[r0:r0 + HD, br, 0:P], start=True, stop=True)
                    mm(ps[:, b + br, P:3 * P], qT[r0:r0 + HD, j, P:S], kT[r0:r0 + HD, br, :], start=True, stop=True)
                for half in range(2):
                    last = mm(ps[:, b, 384 + half * NCMP:384 + (half + 1) * NCMP],
                              qT[r0:r0 + HD, j, half * P:(half + 1) * P], kcT[r0:r0 + HD, 0:NCMP],
                              start=True, stop=True)
                last.then_inc(scores1, 1)

            last.then_inc(gla_o, 1)
            scores_of1(0)
            pe.wait_ge(gla_on, 1)
            for hh in range(GH):
                for half in range(2):
                    last = turn(ps[:, 4 + hh // 2, (hh % 2) * S + half * P:(hh % 2) * S + (half + 1) * P],
                                ogla[:, gla_index(hh, half) * P:(gla_index(hh, half) + 1) * P], ident)
            last.then_inc(gla_turned, 1)
            scores_of1(1)
            pe.wait_ge(gla_oT, 2)

            for k in range(QH + 2):
                if 2 <= k + 1 < QH:
                    scores_of1(k + 1)
                if 1 <= k <= QH:
                    i = k - 1
                    pe.wait_ge(scaled1, i + 1)
                    if i >= 1:
                        pe.wait_ge(pT1, i)
                    for blk in range(6):
                        turn(ps[:, 4 + blk // 4, (blk % 4) * P:(blk % 4 + 1) * P],
                             s_buf[:, i % 2, blk * P:(blk + 1) * P], ident)
                    for half in range(2):
                        last = turn(ps[0:NCMP, 5, S + half * P:S + (half + 1) * P],
                                    s_buf[:, i % 2, 768 + half * NCMP:768 + (half + 1) * NCMP], ident)
                    last.then_inc(turned1, 1)
                if k >= 2:
                    i = k - 2
                    g = i // 4
                    pe.wait_ge(pT1, i + 1)
                    if i >= 2:
                        pe.wait_ge(oT1, i - 1)
                    r0 = HD * (i % 2)
                    o = ps[r0:r0 + HD, 6 + i % 2, 0:S]
                    pt = pT[:, i % 2, :]
                    for br in range(2):
                        vcol = br * 256 + P + g * HD
                        mm(o, zkv[:, 0, vcol:vcol + HD], pt[:, br * 384:br * 384 + S], start=(br == 0), stop=False,
                           skip_group_check=True)
                        mm(o[:, P:S], zkv[:, 1, vcol:vcol + HD], pt[:, br * 384 + S:br * 384 + 384], start=False,
                           stop=False, skip_group_check=True)
                    mm(o, ckv[0:NCMP, P + g * HD:P + (g + 1) * HD], pt[0:NCMP, 768:1024], start=False, stop=True,
                       skip_group_check=True).then_inc(o1, 1)

            pe.wait_ge(oT1, QH)
            for n in range(2):
                for q in range(4):
                    part(f"wout{n}", oT, True, q)

            release(PROD["wout1"])
            norm_turn(1, xn)
            wait_hT(1)

            def ffn_up(s, loaded, k, first=False):
                up_slot = (U_FFN + 2 * s) % RING
                up = dense_ring[:, up_slot, :].rearrange("p (c g n) -> p c g n", c=KC, g=2)
                pe.wait_ge(dense_loaded[up_slot], loaded)
                for a in range(2):
                    pe.wait_ge(ff_read_act, 2 * (2 * k + a) + 1)
                    pe.wait_ge(ff_read_dve, 2 * (2 * k + a) + 1)
                    for g in range(2):
                        for c in range(KC):
                            last = mm(ps[:, 2 * s + a, g * S:(g + 1) * S], up[:, c, g, a * P:(a + 1) * P], hT[:, c, :],
                                      start=(c == 0), stop=(c == KC - 1))
                    last.then_inc(ff_filled, 1)
                    if a == 0 and not first:
                        pe.wait_ge(ff_filled, 2 * k)
                        pe.wait_ge(ff_down, k)
                        pe.sem_inc(dense_used, 1)

            def ffn_down(s, loaded, k, final=False):
                dn_slot = (U_FFN + 2 * s + 1) % RING
                dn = dense_ring[:, dn_slot, 0:2048].rearrange("p (a n) -> p a n", a=2)
                pe.wait_ge(dense_loaded[dn_slot], loaded)
                pe.wait_ge(ff_added, k + 1)
                for a in range(2):
                    pe.wait_ge(ff_act, 2 * k + a + 2)
                    for half in range(2):
                        for n in range(2):
                            last = mm(ps[:, 4 + half * 2 + n, :], act_T[:, s, a, half * P:(half + 1) * P],
                                      dn[:, a, n * 512:(n + 1) * 512], start=(a == 0), stop=(a == 1))
                    if a == 0:
                        if final:
                            pe.wait_ge(ff_down, k + 1)
                        else:
                            pe.wait_ge(ff_filled, 2 * k + 4)
                        pe.sem_inc(dense_used, 1)
                last.then_inc(ff_down, 1)

            u0 = U_FFN
            pe.sem_inc(ff_down, 1)
            ffn_up(0, dense_value(u0), 0, first=True)
            with nc.tensor.Fori(0, FCH // 4) as i:
                for s in range(2):
                    ffn_up(1 - s, dense_value(u0 + 2 * (s + 1)) + 32 * i, 2 * i + s + 1)
                    ffn_down(s, dense_value(u0 + 2 * s + 1) + 16 * i, 2 * i + s)
            ffn_down(0, dense_value(u0 + FCH - 1), FCH // 2 - 1, final=True)
            pe.wait_ge(ff_down, FCH // 2 + 1)
            pe.sem_inc(dense_used, 1)

            norm_turn(2, xn2)
            wait_hT(2)
            def scores_of(k):
                if k >= 2:
                    pe.wait_ge(exp2, k - 1)
                for half in range(2):
                    last = mm(ps[:, 4 + k % 2, half * S:(half + 1) * S], q2T[:, k, half * P:(half + 1) * P],
                              k2T[:, k // 4, :], start=True, stop=True)
                last.then_inc(scores2, 1)

            def attend(k):
                if 1 <= k <= H2:
                    i = k - 1
                    pe.wait_ge(scaled2, i + 1)
                    if i >= 1:
                        pe.wait_ge(pT2, i)
                    for kb in range(2):
                        for half in range(2):
                            last = turn(ps[:, 6, kb * S + half * P:kb * S + (half + 1) * P],
                                        p2[:, i % 2, half * S + kb * P:half * S + (kb + 1) * P], ident)
                    last.then_inc(turned2, 1)
                if k >= 2:
                    i = k - 2
                    pe.wait_ge(pT2, i + 1)
                    if i >= 1:
                        pe.wait_ge(o2T_ready, i)
                    for kb in range(2):
                        last = mm(ps[:, 7, (i % 2) * S:(i % 2 + 1) * S], v2[:, kb, (i // 4) * P:(i // 4 + 1) * P],
                                  p2T[:, i % 2, kb * S:(kb + 1) * S], start=(kb == 0), stop=(kb == 1))
                    last.then_inc(o2, 1)
                    if k == ATTN_STEPS - 1:
                        pe.wait_ge(o2, H2)
                        pe.sem_inc(up_free, 1)
                        pe.sem_inc(dn_free, 1)

            head = None
            for kind, a, q in SCHEDULE2:
                if kind == "part":
                    if a in ("q0", "q1", "kv2"):
                        part(a, hT, True, q)
                    elif a[:2] in ("cc", "cx", "cb", "gc", "ga"):
                        part(a, hT, False, q)
                    elif a[:3] == "wco":
                        pe.wait_ge(cbz_ready, 4)
                        part(a, cbz, False, q)
                    elif a[:3] == "wao":
                        pe.wait_ge(o2T_ready, H2)
                        part(a, o2T, False, q)
                    else:
                        pe.wait_ge(merged, 4)
                        part(a, mrg, True, q)
                    if head is not None:
                        attend(head)
                        head = None
                elif kind == "turn":
                    for rnd, heads in enumerate(((0, 1, 2, 3, 4, 5, 6, 7), (8, 9))):
                        pe.wait_ge(roped2, 1)
                        if rnd:
                            pe.wait_ge(q2T_dve, 2)
                            pe.wait_ge(q2T_act, 2)
                        for n, hh in enumerate(heads):
                            for half in range(2):
                                last = turn(ps[:, 4 + n // 2, (n % 2) * S + half * P:(n % 2) * S + (half + 1) * P],
                                            z2[:, half, hh * P:(hh + 1) * P], ident)
                        last.then_inc(turned_q2, 1)
                    pe.wait_ge(q2T_dve, 3)
                else:
                    if a < H2:
                        scores_of(a)
                    head = a
            release(PROD["wo1"])
            pe.sem_inc(up_free, 1)
            pe.sem_inc(dn_free, 1)

            norm_turn(3, uN)
            wait_hT(3)
            for half in range(2):
                for c in range(KC):
                    last = mm(ps[:, 4, half * P:half * P + NG + NE], hT[:, c, half * P:(half + 1) * P],
                              router_w[:, c, :], start=(c == 0), stop=(c == KC - 1))
            last.then_inc(logits_ready, 1)
            pe.wait_ge(assigned, 1)
            before, ones = const("before"), const("ones")
            mm(ps[:, 5, 0:NE], before, assign[:, 0, :], start=True, stop=True)
            mm(ps[:, 5, NE:2 * NE], ones, assign[:, 0, :], start=True, stop=False)
            mm(ps[:, 5, NE:2 * NE], before, assign[:, 1, :], start=False, stop=True)
            mm(ps[:, 5, 2 * NE:3 * NE], ones, assign[:, 0, :], start=True, stop=False)
            mm(ps[:, 5, 2 * NE:3 * NE], ones, assign[:, 1, :], start=False, stop=True).then_inc(ranks_ready, 1)

            uview = uN.rearrange("p a (n c) -> p a c n", c=KC)

            def gather(it):
                for c in range(KC):
                    for half in range(2):
                        last = mm(ps[:, (0, 7)[c // 4], (c % 4) * P:(c % 4 + 1) * P], uview[:, half, c, :],
                                  sel[:, half, :], start=(half == 0), stop=(half == 1))
                    if c % 4 == 3:
                        last.then_inc(gathered, 1)

            def turn_hidden(it, j):
                pe.wait_ge(act_ready, 4 * it + j + 1)
                rows = hid[0:CAP, j % 2, :].rearrange("p (n m) -> p m n", m=4)
                for m in range(4):
                    last = mm(ps[:, 5 + j % 2, m * CAP:(m + 1) * CAP], rows[:, m, :], ident[0:CAP, 0:CAP],
                              start=True, stop=True)
                last.then_inc(hid_turned, 1)

            def expert_up(it, j, first):
                if first and j < 3:
                    pe.wait_ge((up_loaded[0], up_loaded[1], spare_loaded)[j], 32)
                    w = [expert_ring[:, j, k, :] if j < 2 else dense_ring[:, SPARE[k], :] for k in range(2)]
                else:
                    pe.wait_ge(up_loaded[(j + 1) % 2], 32 * (2 * it + (j + 1) // 2))
                    w = [expert_ring[:, (j + 1) % 2, k, :] for k in range(2)]
                if j == 0:
                    pe.wait_ge(xg_dve, it + 1)
                    pe.wait_ge(xg_act, it + 1)
                for c in range(KC):
                    for k, q in ((0, j), (1, j ^ 1)):
                        last = mm(ps[q * CAP:(q + 1) * CAP, 1 + k, :], xg[:, c, j * CAP:(j + 1) * CAP],
                                  w[k][:, c * DE:(c + 1) * DE], start=(c == 0), stop=(c == KC - 1))
                    if c == 5 and j >= 1:
                        if j == 1:
                            pe.wait_ge(selwT_ready, it + 1)
                        turn_hidden(it, j - 1)
                last.then_inc(up_filled, 1)
                pe.wait_ge(up_filled, 4 * it + j + 1)
                pe.sem_inc(up_free, 1)

            def expert_down(it, j):
                pe.wait_ge(dn_loaded[j % 2], 16 * (2 * it + j // 2 + 1))
                pe.wait_ge(aT_ready, 4 * it + j + 1)
                w = expert_ring[:, j % 2, 2, :].rearrange("p (m n) -> p m n", m=4)
                for m in range(4):
                    for n, q in ((0, j), (1, j ^ 1)):
                        last = mm(ps[q * CAP:(q + 1) * CAP, 3 + n, :], aT[:, j % 2, m * CAP:(m + 1) * CAP],
                                  w[:, m, n * 512:(n + 1) * 512], start=(m == 0), stop=(m == 3))
                last.then_inc(y_filled, 1)
                pe.wait_ge(y_filled, 4 * it + j + 1)
                pe.sem_inc(dn_free, 1)

            def moe_iter(it, first=False):
                pe.wait_ge(sel_ready, it + 1)
                gather(it)
                pe.wait_ge(summed, 2 * it + 1)
                for half in range(2):
                    last = turn(ps[:, 5, half * P:(half + 1) * P], selw[:, half, :], ident)
                last.then_inc(selw_turned, 1)
                expert_up(it, 0, first)
                for j in range(1, GRP):
                    expert_up(it, j, first)
                    expert_down(it, j - 1)
                turn_hidden(it, GRP - 1)
                expert_down(it, GRP - 1)
                pe.wait_ge(y_dve, it + 1)
                pe.wait_ge(y_act, 4 * it + 4)
                for half in range(2):
                    b = (5, 3)[half]
                    for n in range(2):
                        last = mm(ps[:, b + n, :], selwT[:, half * P:(half + 1) * P], y[:, n * 512:(n + 1) * 512],
                                  start=True, stop=True)
                    last.then_inc(scattered, 1)

            pe.wait_ge(slots_ready, 1)
            moe_iter(0, first=True)
            with nc.tensor.Fori(1, NE // GRP) as it:
                moe_iter(it)
            fullest = nc.tensor.value_load(cmax[0:1, 0:1], min_val=0, max_val=S)
            with nc.tensor.Fori(1, ROUNDS) as r:
                with nc.tensor.If(fullest > r * CAP):
                    with nc.tensor.Fori(0, NE // GRP) as g:
                        moe_iter(r * (NE // GRP) + g)

        @block.vector
        def _(dve):
            v = nc.vector
            steps = [0]

            def then(ins):
                steps[0] += 1
                ins.then_inc(dve_step, 1)
                dve.wait_ge(dve_step, steps[0])

            v.memset(kk[:, :, 2, :], 0.0).then_inc(zeroed, 1)
            v.memset(attT, 0.0).then_inc(zeroed, 1)
            v.memset(ss1, 1.0)
            v.memset(tail[:, 11:12], 1.0).then_inc(zeroed, 1)
            dve.wait_ge(zeroed, 3)

            def norm_rows(k, dst, half, gain=None):
                n = 2 * k + half + 1
                col = slice(half, half + 1)
                dve.wait_ge(ssq_ready, n)
                v.tensor_scalar(msq[:, col], ssq[:, col], 1.0 / D, EPS, ALU.mult, ALU.add).then_inc(msq_ready, 1)
                dve.wait_ge(rms_ready, n)
                v.reciprocal(rstd[:, col], rms[:, col]).then_inc(rstd_ready, 1)
                if gain is None:
                    dve.wait_ge(rstd_ready, n)
                    v.tensor_scalar(dst[:, half, :], h[:, half, :], rstd[:, col], None, ALU.mult).then_inc(xn_ready, 1)
                else:
                    dve.wait_ge(rstd_ready, n)
                    v.scalar_tensor_tensor(dst[:, half, :], h[:, half, :], rstd[:, col], gain, ALU.mult, ALU.mult
                                           ).then_inc(xn_ready, 1)

            def norm_take(k, gain=False):
                if k == 0:
                    dve.wait_ge(gcol_in, GCOL_IN)
                for c in (0, 1, 4, 5):
                    dve.wait_ge(xT_turned, 4 * k + c // 2 + 1)
                    if not gain:
                        v.tensor_scalar(hT[:, c, :], norm_bank(k, c), gcol[:, k, c:c + 1], None, ALU.mult
                                        ).then_inc(hT_dve, 1)
                    else:
                        v.tensor_copy(hT[:, c, :], norm_bank(k, c)).then_inc(hT_dve, 1)

            def filled_bank(name, bank):
                step = PROD[name]
                dve.wait_ge(bank_filled, filled(step, bank))
                return ps[:, 2 * (step % 2) + bank, :]

            for half in range(2):
                norm_rows(0, xn, half)
            norm_take(0)
            dve.wait_ge(consts_in, 16)
            dve.wait_ge(prm_turned, 1)
            v.tensor_copy(prm.rearrange("p a b -> p (a b)")[:, 0:122], ps[:, 7, 0:122])
            then(v.tensor_copy(prm.rearrange("p a b -> p (a b)")[:, 128:241], ps[:, 7, 128:241]))
            v.tensor_copy(kk[:, 0, 2, 0:32:2], pe_kT)
            then(v.tensor_copy(kk[:, 1, 2, 0:32:2], pe_vT))
            v.tensor_copy(chunk_mask[:], const("chunk_mask")).then_inc(prm_ready, 1)
            b = filled_bank("cmp_in", 0)
            for i in range(2):
                for g in range(G):
                    r0 = HD * g
                    v.tensor_copy(kk[0:HD, i, g, :], b[r0:r0 + HD, i * S:(i + 1) * S])
                    last = v.tensor_copy(kk[HD:P, i, g, 0:S - 1], b[r0:r0 + HD, i * S + 1:(i + 1) * S])
            last.then_inc(bank_emptied_dve, 1)
            b = filled_bank("kv_tok", 0)
            v.tensor_copy(zkv[:, 0, :], b).then_inc(bank_emptied_dve, 1)
            dve.wait_ge(gate_logits, 1)
            for c in range(2):
                last = v.tensor_scalar(gt[:, c, :], ps[:, 7, c * S:(c + 1) * S], b_gateT[:, c:c + 1], None, ALU.add)
            then(last)
            v.scalar_tensor_tensor(ga_, gt, -1.0, gt, ALU.mult, ALU.max).then_inc(gate_abs, 1)
            b = filled_bank("q_tok", 0)
            v.tensor_copy(by_pairs(zq[:, 0, :]), b.rearrange("p (g j d) -> p g j d", g=G, j=4)
                          ).then_inc(bank_emptied_dve, 1)
            dve.wait_ge(gate_log, 1)
            then(v.scalar_tensor_tensor(gt, gt, 0.0, gl_, ALU.min, ALU.subtract))
            for c in range(2):
                for k in range(S // L):
                    last = v.tensor_tensor_scan(cum[:, c, k * L:(k + 1) * L], const("ones")[:, 0:L],
                                                gt[:, c, k * L:(k + 1) * L], 0.0, ALU.mult, ALU.add)
            then(last)
            v.tensor_scalar(blast, cum[:, :, L - 1::L], 1.0 / TAU, None, ALU.mult).then_inc(cum_ready, 1)
            dve.wait_ge(cmp_rows_ready, 1)
            for i in range(2):
                rows = slice(64 * i, 64 * i + CMP_ROWS)
                v.tensor_copy(cmp_hid[rows, :], ps[rows, 4, 0:256]).then_inc(cmp_rows_in, 1)
            for i in range(2):
                dve.wait_ge(cmp_hidden, i + 1)
                last = v.tensor_copy(hid_bias[:, 2 * i:2 * i + 2], ps[:, 5 - i, 32:32 + 65:64])
            last.then_inc(cmp_bias_ready, 1)
            b = filled_bank("gqk", 0)
            v.tensor_copy(gq.rearrange("p a b -> p (a b)"), b).then_inc(bank_emptied_dve, 1)
            dve.wait_ge(sq_q, 1)
            v.tensor_reduce(ss1[:, 0:16].rearrange("p (a b) -> p a b", a=2),
                            sq1[:, :, 0:512].rearrange("p a (b d) -> p a b d", d=HD), AX.X, ALU.add)
            v.tensor_reduce(ss1[:, 16:24], sq1[:, :, 512:768].rearrange("p a (b d) -> p a b d", d=HD), AX.X, ALU.add)
            dve.wait_ge(cmp_kv_ready, 1)
            then(v.tensor_copy(ckv[0:NCMP, :], ps[0:NCMP, 6, 0:256]))
            then(v.tensor_tensor(sq1[0:NCMP, 0, 768:896], ckv[0:NCMP, 0:P], ckv[0:NCMP, 0:P], ALU.mult))
            then(v.tensor_reduce(ss1[0:NCMP, 24:26], sq1[0:NCMP, 0, 768:896].rearrange("p (b d) -> p b d", d=HD),
                                 AX.X, ALU.add))
            v.tensor_scalar(r1, ss1, 1.0 / HD, EPS, ALU.mult, ALU.add).then_inc(ms_heads, 1)
            dve.wait_ge(exps_ready, 1)
            v.scalar_tensor_tensor(qt, gq, GDK ** -0.5, e_pos, ALU.mult, ALU.mult).then_inc(gla_qk_ready, 1)
            dve.wait_ge(bank_emptied_act, emptied("A", PROD["gqk"], 1))
            v.tensor_tensor(kt, gk, e_neg, ALU.mult).then_inc(gla_qk_ready, 1)
            v.tensor_tensor(khatT, gk, khatT, ALU.mult).then_inc(khat_ready, 1)
            b = filled_bank("gv", 0)
            v.tensor_copy(gv[:, 0, :], b).then_inc(bank_emptied_dve, 1)

            dve.wait_ge(rms_heads, 1)
            then(v.reciprocal(r1, ss1))
            dve.wait_ge(gains_in, GAINS_IN)
            dve.wait_ge(bank_emptied_act, emptied("A", PROD["q_tok"], 1))
            zq4 = zq.rearrange("p a (b d) -> p (a b) d", d=HD)
            zk4 = zkv.rearrange("p a (r x d) -> p a r x d", r=2, d=HD)
            v.tensor_tensor(zq4, zq4, r1[:, 0:16].unsqueeze(2).to_broadcast([P, 16, HD]), ALU.mult)
            for half in range(2):
                for br in range(2):
                    zk = zk4[:, half, br, 0:2, :]
                    i = 16 + half * 4 + br * 2
                    v.tensor_tensor(zk, zk, r1[:, i:i + 2].unsqueeze(2).to_broadcast([P, 2, HD]), ALU.mult)
            ck = ckv[0:NCMP, 0:P].rearrange("p (b d) -> p b d", d=HD)
            then(v.tensor_tensor(ck, ck, r1[0:NCMP, 24:26].unsqueeze(2).to_broadcast([NCMP, 2, HD]), ALU.mult))
            v.tensor_tensor(zq4, zq4, q_gain1.unsqueeze(1).to_broadcast([P, 16, HD]), ALU.mult)
            for half in range(2):
                for br in range(2):
                    zk = zk4[:, half, br, 0:2, :]
                    gn = k_gains1[:, (1 + br) * HD:(2 + br) * HD]
                    v.tensor_tensor(zk, zk, gn.unsqueeze(1).to_broadcast([P, 2, HD]), ALU.mult)
            then(v.tensor_tensor(ck, ck, k_gains1[0:NCMP, 0:HD].unsqueeze(1).to_broadcast([NCMP, 2, HD]), ALU.mult))

            def rope(x, cos, sin, rows, n):
                x1, x2 = x[:, :, 0:8], x[:, :, 8:16]
                c, s_ = cos.unsqueeze(1).to_broadcast([rows, n, 8]), sin.unsqueeze(1).to_broadcast([rows, n, 8])
                tm = [rope_tmp[0:rows, i, 0:n * 8].rearrange("p (a b) -> p a b", b=8) for i in range(4)]
                v.tensor_tensor(tm[0], x1, c, ALU.mult)
                v.tensor_tensor(tm[1], x2, s_, ALU.mult)
                v.tensor_tensor(tm[2], x2, c, ALU.mult)
                then(v.tensor_tensor(tm[3], x1, s_, ALU.mult))
                v.tensor_tensor(x1, tm[0], tm[1], ALU.subtract)
                then(v.tensor_tensor(x2, tm[2], tm[3], ALU.add))

            cos1, sin1 = const("cos1"), const("sin1")
            for half in range(2):
                c, s_ = cos1[:, half * 8:(half + 1) * 8], sin1[:, half * 8:(half + 1) * 8]
                rope(zq.rearrange("p a (b d) -> p a b d", d=HD)[:, half], c, s_, P, QH)
                for br in range(2):
                    rope(zk4[:, half, br, 0:2, :], c, s_, P, 2)
            rope(ck, const("cosc", NCMP), const("sinc", NCMP), NCMP, 2)
            v.memset(tail[:, 0:1], 0.0).then_inc(roped, 1)
            dve.wait_ge(qk_turned, 1)
            v.tensor_copy(qT[:, 0:2, :].rearrange("p a b -> p (a b)"), ps[:, 0, :]).then_inc(qkT_dve, 1)
            v.tensor_copy(kcT[:, 0:NCMP], ps[:, 3, 0:NCMP]).then_inc(qkT_dve, 1)

            dve.wait_ge(khat_turned, 1)
            v.tensor_copy(khat.rearrange("p a b -> p (a b)"), ps[:, 7, :]).then_inc(khat_rows, 1)
            dve.wait_ge(att_filled, 1)
            for i in range(2):
                last = v.copy_predicated(attT[:, 4 * i:4 * i + 4, :],
                                         chunk_mask[:].unsqueeze(1).to_broadcast([P, 4, P]),
                                         ps[:, 4 + i, :].rearrange("p (a b) -> p a b", a=4))
            last.then_inc(att_masked, 1)
            dve.wait_ge(ds_filled, 1)
            dS = ps[:, 0:2, :].rearrange("p b (a c n) -> p a b c n", a=2, c=2)
            then(v.tensor_copy(state[:, :, 0, :], dS[:, :, 0, 0, :]))
            for c in range(1, 3):
                for i in range(2):
                    last = v.scalar_tensor_tensor(state[:, i, c, :], state[:, i, c - 1, :], decay[:, i, c:c + 1],
                                                  dS[:, i, c % 2, c // 2, :], ALU.mult, ALU.add)
                then(last) if c == 1 else last.then_inc(states_ready, 1)
            dve.wait_ge(gla_sq, 1)
            then(v.tensor_reduce(ogla_ss, osq.rearrange("p (a b) -> p a b", b=P), AX.X, ALU.add))
            v.tensor_scalar(ogla_r, ogla_ss, 1.0 / GDV, EPS, ALU.mult, ALU.add).then_inc(gla_ms, 1)
            dve.wait_ge(gla_rms, 1)
            then(v.reciprocal(ogla_r, ogla_ss))
            v.tensor_tensor(ogla.rearrange("p (a b) -> p a b", b=P),
                            ps[:, 2:4, :].rearrange("p a b -> p (a b)").rearrange("p (a b) -> p a b", b=P),
                            ogla_r.unsqueeze(2).to_broadcast([P, 8, P]), ALU.mult).then_inc(gla_on, 1)
            causal3 = const("causal3")

            def mask_scores(k):
                b, s_ = 2 * (k % 2), s_buf[:, k % 2, :]
                m, nm = mx[:, k % 2, :], nmx[:, k % 2, :]
                dve.wait_ge(scores1, k + 1)
                if k >= 2:
                    dve.wait_ge(turned1, k - 1)
                    dve.wait_ge(exp1, k - 1)
                v.tensor_tensor(s_[:, 0:768].rearrange("p (a b) -> p a b", a=2), ps[:, b:b + 2, 0:384],
                                causal3.unsqueeze(1).to_broadcast([P, 2, 384]), ALU.add)
                then(v.tensor_tensor(s_[:, 768:798], ps[:, b, 384:414], const("cmp_bias"), ALU.add))
                v.tensor_reduce(m[:, 0:6], s_[:, 0:768].rearrange("p (a b) -> p a b", b=P), AX.X, ALU.max)
                then(v.tensor_reduce(m[:, 6:8], s_[:, 768:798].rearrange("p (a b) -> p a b", b=NCMP), AX.X, ALU.max))
                then(v.tensor_tensor(m[:, 1:6:3], m[:, 1:6:3], m[:, 2:6:3], ALU.max))
                v.tensor_scalar(nm, m, -(HD ** -0.5), None, ALU.mult).then_inc(nmx1, 1)

            mask_scores(0)
            dve.wait_ge(gla_turned, 1)
            for i in range(2):
                v.scalar_tensor_tensor(oT[:, 4 + 2 * i:6 + 2 * i, :], ps[:, 4 + i, :].rearrange("p (a b) -> p a b", a=2),
                                       out_gainT, sil[:, 2 * i:2 * i + 2, :], ALU.mult, ALU.mult).then_inc(gla_oT, 1)

            for k in range(QH + 2):
                if 1 <= k < QH:
                    mask_scores(k)
                if 1 <= k <= QH:
                    i = k - 1
                    s_, sm, wt = s_buf[:, i % 2, :], sums[:, i % 2, :], wts[:, i % 2, :]
                    dve.wait_ge(exp1, i + 1)
                    then(v.reciprocal(wt[:, 0:6], sm[:, 0:6]))
                    gate = gates[:, :, 3 * i:3 * i + 3].rearrange("p a b -> p b a")
                    v.tensor_tensor(wt[:, 0:4].rearrange("p (a b) -> p a b", a=2),
                                    wt[:, 0:4].rearrange("p (a b) -> p a b", a=2), gate[:, 1:3, :], ALU.mult)
                    then(v.tensor_tensor(wt[:, 4:6], wt[:, 4:6], gate[:, 0, :], ALU.mult))
                    for br in range(2):
                        o = br * 384
                        v.tensor_scalar(s_[:, o:o + P], s_[:, o:o + P], wt[:, 2 * br:2 * br + 1], None, ALU.mult)
                        v.tensor_scalar(s_[:, o + P:o + 384], s_[:, o + P:o + 384], wt[:, 2 * br + 1:2 * br + 2],
                                        None, ALU.mult)
                    for half in range(2):
                        o = 768 + half * NCMP
                        last = v.scalar_tensor_tensor(s_[:, o:o + NCMP], s_[:, o:o + NCMP], wt[:, 4 + half:5 + half],
                                                      const("cmp_keep")[:, half * NCMP:(half + 1) * NCMP],
                                                      ALU.mult, ALU.mult)
                    last.then_inc(scaled1, 1)
            def add_rows(name, n, half):
                b = filled_bank(name, half)
                o = h[:, half, n * 512:(n + 1) * 512]
                v.tensor_tensor(o, o, b, ALU.add).then_inc(bank_emptied_dve, 1)

            def half_done(name, half):
                dve.wait_ge(bank_emptied_dve, emptied("D", PROD[name], half))
                v.memset(tail[:, 1:2], 0.0).then_inc(h_ready, 1)

            for half in range(2):
                add_rows("wout0", 0, half)
            for half in range(2):
                add_rows("wout1", 1, half)
                half_done("wout1", half)
                norm_rows(1, xn, half)
            norm_take(1)

            def taps(k):
                return [prm[:, 0, bass.ds(k, 1)], prm[:, 0, bass.ds(k + 44, 1)]]

            def ffn_step(k, s, first=False):
                for a in range(2):
                    dve.wait_ge(ff_read_act, 2 * (2 * k + a) + 9)
                    for g in range(2):
                        u = ps[:, 2 * s + a, g * S:(g + 1) * S]
                        w0, w1 = taps(2 * k + a + g * FCH)
                        yy = conv_y[:, a, g, :]
                        v.scalar_tensor_tensor(yy[:, 1:S], u[:, 0:S - 1], w1, yy[:, 1:S], ALU.mult, ALU.add
                                               ).then_inc(ffn_chain, 1)
                        dve.wait_ge(ffn_chain, 2 * (2 * k + a) + g + 1)
                        v.scalar_tensor_tensor(yy[:, 2:S], u[:, 0:S - 2], w0, yy[:, 2:S], ALU.mult, ALU.add
                                               ).then_inc(ff_read_dve, 1)
                    dve.wait_ge(ff_silu, 2 * k + a + 1)
                    dve.wait_ge(ff_read_dve, 2 * (2 * k + a) + 9)
                    v.tensor_tensor(act_T[:, s, a, :], sil_g[:, a, :], conv_y[:, a, 1, :], ALU.mult).then_inc(ff_act, 1)
                if not first:
                    add_down(k)

            def add_down(k):
                dve.wait_ge(ff_added, k)
                dve.wait_ge(ff_down, k + 1)
                for half in range(2):
                    for n in range(2):
                        o = h[:, half, n * 512:(n + 1) * 512]
                        last = v.tensor_tensor(o, o, ps[:, 4 + half * 2 + n, :], ALU.add)
                last.then_inc(ff_added, 1)

            for s_one in (ff_act, ff_added):
                dve.sem_inc(s_one, 1)
            dve.sem_inc(ff_read_dve, 7)
            ffn_step(0, 0, first=True)
            with nc.vector.Fori(0, FCH // 4) as i:
                for s in range(2):
                    ffn_step(2 * i + s + 1, 1 - s)
            LAST = FCH // 2
            dve.wait_ge(ff_added, LAST)
            dve.wait_ge(ff_down, LAST + 1)
            for half in range(2):
                for n in range(2):
                    o = h[:, half, n * 512:(n + 1) * 512]
                    last = v.tensor_tensor(o, o, ps[:, 4 + half * 2 + n, :], ALU.add)
                last.then_inc(h_ready, 1)
            dve.wait_ge(h_ready, 4)

            for half in range(2):
                norm_rows(2, xn2, half)
            norm_take(2)
            z5 = z2.rearrange("p a (b d) -> p (a b) d", d=P)
            cos2, sin2 = const("cos2"), const("sin2")

            def heads_norm():
                dve.wait_ge(sq2_ready, 2)
                then(v.tensor_reduce(ss2, sq2.rearrange("p a (b d) -> p (a b) d", d=P), AX.X, ALU.add))
                v.tensor_scalar(r2, ss2, 1.0 / HD2, EPS, ALU.mult, ALU.add).then_inc(ms2_ready, 1)

            def heads_rope():
                dve.wait_ge(rms2_ready, 1)
                then(v.reciprocal(r2, ss2))
                then(v.tensor_tensor(z5, z5, r2.unsqueeze(2).to_broadcast([P, 20, P]), ALU.mult))
                for half in range(2):
                    zh = z2[:, half, :].rearrange("p (b d) -> p b d", d=P)
                    v.tensor_tensor(zh[:, 0:8, :], zh[:, 0:8, :], q_gain2.unsqueeze(1).to_broadcast([P, 8, P]), ALU.mult)
                    last = v.tensor_tensor(zh[:, 8:10, :], zh[:, 8:10, :],
                                           k_gain2.unsqueeze(1).to_broadcast([P, 2, P]), ALU.mult)
                then(last)
                for half in range(2):
                    zh = z2[:, half, :].rearrange("p (b i e) -> p b i e", i=64, e=2)
                    x0, x1 = zh[:, :, :, 0], zh[:, :, :, 1]
                    c = cos2[:, half * 64:(half + 1) * 64].unsqueeze(1).to_broadcast([P, 10, 64])
                    s_ = sin2[:, half * 64:(half + 1) * 64].unsqueeze(1).to_broadcast([P, 10, 64])
                    tm = [sq2[:, i // 2, (i % 2) * 640:(i % 2 + 1) * 640].rearrange("p (b i) -> p b i", i=64)
                          for i in range(4)]
                    v.tensor_tensor(tm[0], x0, c, ALU.mult)
                    v.tensor_tensor(tm[1], x1, s_, ALU.mult)
                    v.tensor_tensor(tm[2], x0, s_, ALU.mult)
                    then(v.tensor_tensor(tm[3], x1, c, ALU.mult))
                    v.tensor_tensor(x0, tm[0], tm[1], ALU.subtract)
                    then(v.tensor_tensor(x1, tm[2], tm[3], ALU.add))
                v.memset(tail[:, 3:4], 0.0).then_inc(roped2, 1)

            def empty2(name, bank):
                b = filled_bank(name, bank)
                m = int(name[-1])
                two = b.rearrange("p (a b) -> p a b", a=2)
                lo = 2 * bank
                if name in ("q0", "q1"):
                    v.tensor_copy(z2[:, 0, 512 * m:512 * (m + 1)], b).then_inc(bank_emptied_dve, 1)
                elif name == "kv2":
                    v.tensor_copy(z2[:, 0, 1024:1280], b[:, 0:256])
                    v.tensor_copy(v2[:, 0, :], b[:, 256:512]).then_inc(bank_emptied_dve, 1)
                elif name[:2] == "cx":
                    dve.wait_ge(bank_emptied_act, emptied("A", PROD["cc%d" % m], bank))
                    if m == 1:
                        dve.wait_ge(conv_mid, 1)
                    v.tensor_tensor(u_s[:, lo:lo + 2, :], two, cc_s[:, lo:lo + 2, :], ALU.mult
                                    ).then_inc(bank_emptied_dve, 1)
                elif name[:2] == "cb":
                    if bank == 0:
                        dve.wait_ge(conv_mid, m + 1)
                        for c in range(4):
                            v.scalar_tensor_tensor(z_s[:, c, 1:S], u_s[:, c, 0:S - 1], cw2(0, 4 * m + c),
                                                   z_s[:, c, 1:S], ALU.mult, ALU.add)
                        then(v.memset(tail[:, 4:5], 0.0))
                        for c in range(4):
                            last = v.scalar_tensor_tensor(z_s[:, c, 0:S - 1], u_s[:, c, 1:S], cw2(2, 4 * m + c),
                                                          z_s[:, c, 0:S - 1], ALU.mult, ALU.add)
                        then(last)
                    v.tensor_tensor(cbz[:, 4 * m + lo:4 * m + lo + 2, :], two, z_s[:, lo:lo + 2, :], ALU.mult
                                    ).then_inc(bank_emptied_dve, 1)
                    if bank == 1:
                        dve.wait_ge(bank_emptied_dve, emptied("D", PROD[name], 1))
                        v.memset(tail[:, 5:6], 0.0).then_inc(cbz_ready, 2)
                elif name[:3] == "wco":
                    dve.wait_ge(bank_emptied_act, emptied("A", PROD["gc%d" % m], bank))
                    v.tensor_tensor(mrg[:, 4 * m + lo:4 * m + lo + 2, :], two, sg[:, lo:lo + 2, :], ALU.mult
                                    ).then_inc(bank_emptied_dve, 1)
                elif name[:3] == "wao":
                    dve.wait_ge(bank_emptied_act, emptied("A", PROD["ga%d" % m], bank))
                    if 2 * m + bank:
                        dve.wait_ge(merged, 2 * m + bank)
                    v.tensor_tensor(mtmp.rearrange("p (a b) -> p a b", a=2), two, sg2[:, lo:lo + 2, :], ALU.mult
                                    ).then_inc(bank_emptied_dve, 1)
                    dve.wait_ge(bank_emptied_dve, emptied("D", PROD[name], bank))
                    mm_ = mrg[:, 4 * m + lo:4 * m + lo + 2, :]
                    v.tensor_tensor(mm_, mm_, mtmp.rearrange("p (a b) -> p a b", a=2), ALU.add).then_inc(merged, 1)
                else:
                    o = h[:, bank, m * 512:(m + 1) * 512]
                    v.tensor_tensor(o, o, b, ALU.add).then_inc(bank_emptied_dve, 1)
                    if name == "wo1":
                        half_done(name, bank)
                        norm_rows(3, uN, bank, norm_gain2)

            def cw2(tap, c):
                return prm[:, 1, 88 + tap * 8 + c:89 + tap * 8 + c]

            for kind, a, q in SCHEDULE2:
                if kind == "part":
                    if q % 2 and PRODUCTS[PROD[a]][1][q // 2] == "D":
                        empty2(a, q // 2)
                    if (a, q) == ("kv2", 3):
                        heads_norm()
                    if (a, q) == ("cc0", 3):
                        heads_rope()
                elif kind == "turn":
                    for rnd in range(2):
                        dve.wait_ge(turned_q2, rnd + 1)
                        if rnd == 0:
                            for i in range(2):
                                v.tensor_copy(q2T[:, 2 * i:2 * i + 2, :].rearrange("p a b -> p (a b)"), ps[:, 4 + i, :]
                                              ).then_inc(q2T_dve, 1)
                        else:
                            v.tensor_copy(k2T.rearrange("p a b -> p (a b)"), ps[:, 4, :]).then_inc(q2T_dve, 1)
                else:
                    k = a
                    if k < H2:
                        dve.wait_ge(scores2, k + 1)
                        if k >= 2:
                            dve.wait_ge(exp2, k - 1)
                        then(v.tensor_reduce(mx2[:, k % 2, :], ps[:, 4 + k % 2, :].rearrange("p (a b) -> p a b", a=2),
                                             AX.X, ALU.max))
                        v.tensor_scalar(nmx2[:, k % 2, :], mx2[:, k % 2, :], -(HD2 ** -0.5), None, ALU.mult
                                        ).then_inc(nmx_2, 1)
                    if 1 <= k <= H2:
                        i = k - 1
                        dve.wait_ge(exp2, i + 1)
                        then(v.reciprocal(rs2[:, i % 2, :], sum2[:, i % 2, :]))
                        for half in range(2):
                            o = p2[:, i % 2, half * S:(half + 1) * S]
                            last = v.tensor_scalar(o, o, rs2[:, i % 2, half:half + 1], None, ALU.mult)
                        last.then_inc(scaled2, 1)
                        dve.wait_ge(turned2, i + 1)
                        if i >= 2:
                            dve.wait_ge(o2, i - 1)
                        v.tensor_copy(p2T[:, i % 2, :], ps[:, 6, :]).then_inc(pT2, 1)

            norm_take(3, gain=True)
            dve.wait_ge(logits_ready, 1)
            then(v.tensor_copy(lg, ps[:, 4, 0:2 * P].rearrange("p (a b) -> p a b", a=2)[:, :, 0:NG + NE]))
            for half in range(2):
                last = v.max(g8[:, half, :], lg[:, half, 0:NG])
            then(last)
            for half in range(2):
                v.max_index(gi8u[:, half, :], g8[:, half, :], lg[:, half, 0:NG])
            then(v.tensor_scalar(ngm, g8[:, :, 0:1], -1.0, None, ALU.mult))
            v.tensor_copy(gi8, gi8u).then_inc(grp_nmax, 1)
            dve.wait_ge(grp_nmax, 1)
            for half in range(2):
                last = v.tensor_scalar(goh[:, half, :], const("iota64")[:, 0:NG], gi8[:, half, 0:1], None, ALU.is_equal)
            then(last)
            v.tensor_scalar(gohb, goh, -1.0, -NEG, ALU.add, ALU.mult)
            for half in range(2):
                e3 = elm[:, half, :].rearrange("p (a b) -> p a b", a=NG)
                last = v.tensor_tensor(e3, lg[:, half, NG:].rearrange("p (a b) -> p a b", a=NG),
                                       goh[:, half, :].unsqueeze(2).to_broadcast([P, NG, EPG]), ALU.mult)
            then(last)
            for half in range(2):
                e3 = elm[:, half, :].rearrange("p (a b) -> p a b", a=NG)
                last = v.tensor_tensor(e3, e3, gohb[:, half, :].unsqueeze(2).to_broadcast([P, NG, EPG]), ALU.add)
            then(last)
            for half in range(2):
                last = v.max(e8[:, half, :], elm[:, half, :])
            then(last)
            for half in range(2):
                v.max_index(ei8u[:, half, :], e8[:, half, :], elm[:, half, :])
            v.tensor_tensor(dv, e8[:, :, 1:2], e8[:, :, 0:1], ALU.subtract).then_inc(top_diff, 1)
            dve.wait_ge(top_diff, 1)
            then(v.tensor_copy(ei8, ei8u))
            for half in range(2):
                v.tensor_scalar(oh1[:, half, :], const("iota64"), ei8[:, half, 0:1], None, ALU.is_equal)
                last = v.tensor_scalar(oh2[:, half, :], const("iota64"), ei8[:, half, 1:2], None, ALU.is_equal)
            then(last)
            v.tensor_tensor(assign, oh1, oh2, ALU.add).then_inc(assigned, 1)
            dve.wait_ge(grp_exp, 2)
            v.reciprocal(pg, gsum)
            dve.wait_ge(top_exp, 1)
            then(v.tensor_scalar(den, ex, 1.0, None, ALU.add))
            then(v.reciprocal(rden, den))
            then(v.tensor_tensor(w1t, pg, rden, ALU.mult))
            then(v.tensor_tensor(w2t, w1t, ex, ALU.mult))
            for half in range(2):
                last = v.tensor_scalar(oh1[:, half, :], oh1[:, half, :], w1t[:, half, :], None, ALU.mult)
            then(last)
            for half in range(2):
                last = v.scalar_tensor_tensor(wmat[:, half, :], oh2[:, half, :], w2t[:, half, :], oh1[:, half, :],
                                              ALU.mult, ALU.add)
            then(last)
            dve.wait_ge(ranks_ready, 1)
            rank = ps[:, 5, 0:2 * NE].rearrange("p (a b) -> p a b", a=2)
            dve.wait_ge(assigned, 1)
            then(v.scalar_tensor_tensor(slot, rank, 1.0, assign, ALU.add, ALU.mult))
            v.tensor_scalar(slot, slot, -1.0, None, ALU.add)
            then(v.tensor_reduce(cmax_f, ps[:, 5, 2 * NE:3 * NE], AX.X, ALU.max))
            v.tensor_copy(cmax, cmax_f).then_inc(slots_ready, 1)
            dve.wait_ge(slots_ready, 1)

            iota4 = const("slot_iota").rearrange("p (a b) -> p a b", a=GRP)

            def moe_iter(it, e0):
                for half in range(2):
                    sl = slot[:, half, bass.ds(e0, GRP)].unsqueeze(2).to_broadcast([P, GRP, CAP])
                    last = v.tensor_tensor(sel[:, half, :].rearrange("p (a b) -> p a b", a=GRP), iota4, sl, ALU.is_equal)
                last.then_inc(moe_step, 1)
                dve.wait_ge(moe_step, it + 1)
                for half in range(2):
                    wv = wmat[:, half, bass.ds(e0, GRP)].unsqueeze(2).to_broadcast([P, GRP, CAP])
                    last = v.tensor_tensor(selw[:, half, :].rearrange("p (a b) -> p a b", a=GRP),
                                           sel[:, half, :].rearrange("p (a b) -> p a b", a=GRP), wv, ALU.mult)
                last.then_inc(sel_ready, 1)

                dve.wait_ge(gathered, 2 * it + 1)
                v.tensor_copy(xg[:, 0:4, :], ps[:, 0, :].rearrange("p (c s) -> p c s", c=4)).then_inc(xg_dve, 1)
                for j in range(GRP):
                    q = (j ^ 1) * CAP
                    dve.wait_ge(silu_ready, 4 * it + j + 1)
                    v.tensor_tensor(hid[0:CAP, j % 2, :], hsil[q:q + CAP, j % 2, :], ps[q:q + CAP, 2, :], ALU.mult
                                    ).then_inc(act_ready, 1)
                    dve.wait_ge(hid_turned, 4 * it + j + 1)
                    if j >= 2:
                        dve.wait_ge(y_filled, 4 * it + j - 1)
                    v.tensor_copy(aT[:, j % 2, :], ps[:, 5 + j % 2, 0:P]).then_inc(aT_ready, 1)
                dve.wait_ge(y_filled, 4 * it + 4)
                v.tensor_copy(y[:, 0:512], ps[:, 3, :]).then_inc(y_dve, 1)
                for half in range(2):
                    dve.wait_ge(scattered, 2 * it + half + 1)
                    b = (5, 3)[half]
                    v.tensor_tensor(h[:, half, :].rearrange("p (a b) -> p a b", a=2),
                                    h[:, half, :].rearrange("p (a b) -> p a b", a=2), ps[:, b:b + 2, :], ALU.add
                                    ).then_inc(summed, 1)
                dve.wait_ge(summed, 2 * it + 3)
                v.memset(tail[:, 9:10], 0.0)

            dve.sem_inc(summed, 1)
            with nc.vector.Fori(0, NE // GRP) as it:
                moe_iter(it, it * GRP)
            fullest = nc.vector.value_load(cmax[0:1, 0:1], min_val=0, max_val=S)
            with nc.vector.Fori(1, ROUNDS) as r:
                with nc.vector.If(fullest > r * CAP):
                    v.tensor_scalar(slot, slot, -float(CAP), None, ALU.add).then_inc(moe_round, 1)
                    dve.wait_ge(moe_round, r)
                    v.memset(tail[:, 9:10], 0.0)
                    with nc.vector.Fori(0, NE // GRP) as g:
                        moe_iter(r * (NE // GRP) + g, g * GRP)
            v.memset(tail[:, 7:8], 0.0).then_inc(last_ready, 1)

        @block.scalar
        def _(act):
            a_ = nc.scalar.activation

            def norm(k, junk, gain=False):
                a_(tail[:, 10:11], tail[:, 11:12], ACT.Sqrt)
                if k == 0:
                    act.wait_ge(x_in, 32)
                for half in range(2):
                    n, col = 2 * k + half + 1, slice(half, half + 1)
                    if k:
                        act.wait_ge(h_ready, n - 2)
                    a_(junk[:, half, :], h[:, half, :], ACT.Square, accum_out=ssq[:, col]).then_inc(ssq_ready, 1)
                    act.wait_ge(msq_ready, n)
                    a_(rms[:, col], msq[:, col], ACT.Sqrt).then_inc(rms_ready, 1)
                if k == 0:
                    act.wait_ge(gcol_in, GCOL_IN)
                for c in (2, 3, 6, 7):
                    act.wait_ge(xT_turned, 4 * k + c // 2 + 1)
                    if not gain:
                        a_(hT[:, c, :], norm_bank(k, c), ACT.Copy, scale=gcol[:, k, c:c + 1]).then_inc(hT_act, 1)
                    else:
                        a_(hT[:, c, :], norm_bank(k, c), ACT.Copy).then_inc(hT_act, 1)

            def filled_bank(name, bank):
                step = PROD[name]
                act.wait_ge(bank_filled, filled(step, bank))
                return ps[:, 2 * (step % 2) + bank, :]

            act.wait_ge(zeroed, 3)
            norm(0, xn)
            b = filled_bank("cmp_in", 1)
            a_(gates.rearrange("p a b -> p (a b)"), b[:, 0:48], ACT.Sigmoid)
            a_(glrT[0:16, :], b[0:16, P:P + S], ACT.Copy).then_inc(bank_emptied_act, 1)
            b = filled_bank("kv_tok", 1)
            a_(zkv[:, 1, :], b, ACT.Copy).then_inc(bank_emptied_act, 1)
            act.wait_ge(gate_abs, 1)
            a_(gl_, ga_, ACT.Exp, scale=-1.0).then_inc(act_step, 1)
            act.wait_ge(act_step, 1)
            a_(gl_, gl_, ACT.Ln, bias=1.0).then_inc(gate_log, 1)
            b = filled_bank("q_tok", 1)
            a_(by_pairs(zq[:, 1, :]), b.rearrange("p (g j d) -> p g j d", g=G, j=4), ACT.Copy
               ).then_inc(bank_emptied_act, 1)
            act.wait_ge(cum_ready, 1)
            a_(e_pos, cum, ACT.Exp, scale=1.0 / TAU)
            a_(e_neg, cum, ACT.Exp, scale=-1.0 / TAU)
            a_(decay, blast, ACT.Exp)
            for c in range(2):
                for k in range(4):
                    last = a_(khatT[:, c, k * L:(k + 1) * L], cum[:, c, k * L:(k + 1) * L], ACT.Exp,
                              scale=-1.0 / TAU, bias=blast[:, c, k:k + 1])
            last.then_inc(exps_ready, 1)
            act.wait_ge(bank_emptied_act, 3)
            act.wait_ge(bank_emptied_dve, emptied("D", PROD["q_tok"], 0))
            a_(sq1[:, :, 0:512], zq, ACT.Square)
            a_(sq1[:, :, 512:768].rearrange("p a (r x) -> p a r x", r=2),
               zkv.rearrange("p a (r x) -> p a r x", r=2)[:, :, :, 0:P], ACT.Square).then_inc(sq_q, 1)
            act.wait_ge(cmp_bias_ready, 1)
            for i in range(2):
                for m in range(2):
                    last = a_(gelu_h[:, i, m, :].rearrange("p (g n) -> p g n", g=G),
                              ps[:, 5 - i, m * 64:m * 64 + 32].rearrange("p (g n) -> p g n", g=G)[:, :, 0:NCMP],
                              ACT.Gelu_apprx_tanh,
                              bias=hid_bias[:, 2 * i + m:2 * i + m + 1])
                last.then_inc(gelu_ready, 1)
            b = filled_bank("gqk", 1)
            a_(gk.rearrange("p a b -> p (a b)"), b, ACT.Copy).then_inc(bank_emptied_act, 1)
            act.wait_ge(ms_heads, 1)
            a_(ss1, r1, ACT.Sqrt).then_inc(rms_heads, 1)
            b = filled_bank("gv", 1)
            a_(gv[:, 1, :], b, ACT.Copy).then_inc(bank_emptied_act, 1)
            for bank in range(2):
                b = filled_bank("gout", bank)
                a_(sil[:, 2 * bank:2 * bank + 2, :].rearrange("p a b -> p (a b)"), b, ACT.Silu
                   ).then_inc(bank_emptied_act, 1)
            act.wait_ge(qk_turned, 1)
            a_(qT[:, 2:4, :].rearrange("p a b -> p (a b)"), ps[:, 1, :], ACT.Copy).then_inc(qkT_act, 1)
            a_(kT.rearrange("p a b -> p (a b)"), ps[:, 2, :], ACT.Copy).then_inc(qkT_act, 1)
            act.wait_ge(gla_o, 1)
            a_(osq.rearrange("p (a b) -> p a b", a=2), ps[:, 2:4, :], ACT.Square).then_inc(gla_sq, 1)
            act.wait_ge(gla_ms, 1)
            a_(ogla_ss, ogla_r, ACT.Sqrt).then_inc(gla_rms, 1)

            SC = HD ** -0.5
            for k in range(QH + 3):
                if k < QH:
                    s_, nm, sm = s_buf[:, k % 2, :], nmx[:, k % 2, :], sums[:, k % 2, :]
                    act.wait_ge(nmx1, k + 1)
                    for br in range(2):
                        for half, lo, hi in ((0, 0, P), (1, P, 384)):
                            o = s_[:, br * 384 + lo:br * 384 + hi]
                            a_(o, o, ACT.Exp, scale=SC, bias=nm[:, 3 * br + half:3 * br + half + 1],
                               accum_out=sm[:, 2 * br + half:2 * br + half + 1])
                    for half in range(2):
                        o = s_[:, 768 + half * NCMP:768 + (half + 1) * NCMP]
                        last = a_(o, o, ACT.Exp, scale=SC, bias=nm[:, 6 + half:7 + half],
                                  accum_out=sm[:, 4 + half:5 + half])
                    last.then_inc(exp1, 1)
                if k >= 3:
                    i = k - 3
                    act.wait_ge(o1, i + 1)
                    r0 = HD * (i % 2)
                    a_(oT[r0:r0 + HD, i // 2, :], ps[r0:r0 + HD, 6 + i % 2, 0:S], ACT.Copy).then_inc(oT1, 1)
                if 1 <= k <= QH:
                    i = k - 1
                    act.wait_ge(turned1, i + 1)
                    if i >= 2:
                        act.wait_ge(o1, i - 1)
                    a_(pT[:, i % 2, 0:512], ps[:, 4, :], ACT.Copy)
                    a_(pT[:, i % 2, 512:768], ps[:, 5, 0:S], ACT.Copy)
                    a_(pT[0:NCMP, i % 2, 768:1024], ps[0:NCMP, 5, S:2 * S], ACT.Copy).then_inc(pT1, 1)

            norm(1, xn)

            def ffn_step(k, s):
                for a in range(2):
                    act.wait_ge(ff_filled, 2 * k + a + 1)
                    act.wait_ge(ff_act, 2 * k + 1)
                    for g in range(2):
                        c = 2 * k + a + g * FCH
                        a_(conv_y[:, a, g, :], ps[:, 2 * s + a, g * S:(g + 1) * S], ACT.Identity,
                           scale=prm[:, 1, bass.ds(c, 1)], bias=prm[:, 1, bass.ds(c + 44, 1)]
                           ).then_inc(ff_read_act, 1)
                    act.wait_ge(ff_read_dve, 2 * (2 * k + a) + 8)
                    a_(sil_g[:, a, :], conv_y[:, a, 0, :], ACT.Silu).then_inc(ff_silu, 1)

            act.sem_inc(ff_read_act, 7)
            with nc.scalar.Fori(0, FCH // 4) as i:
                for s in range(2):
                    ffn_step(2 * i + s, s)
            ffn_step(FCH // 2 - 1, 0)

            norm(2, xn2)

            def empty2(name, bank):
                b = filled_bank(name, bank)
                m = int(name[-1])
                if name in ("q0", "q1"):
                    a_(z2[:, 1, 512 * m:512 * (m + 1)], b, ACT.Copy).then_inc(bank_emptied_act, 1)
                elif name == "kv2":
                    a_(z2[:, 1, 1024:1280], b[:, 0:256], ACT.Copy)
                    a_(v2[:, 1, :], b[:, 256:512], ACT.Copy).then_inc(bank_emptied_act, 1)
                elif name[:2] == "cc":
                    if m == 1:
                        act.wait_ge(bank_emptied_dve, emptied("D", PROD["cx0"], 1))
                    a_(cc_s[:, 2 * bank:2 * bank + 2, :].rearrange("p a b -> p (a b)"), b, ACT.Copy
                       ).then_inc(bank_emptied_act, 1)
                else:
                    dst, reader = (sg, "wco0") if name[:2] == "gc" else (sg2, "wao0")
                    if m == 1:
                        act.wait_ge(bank_emptied_dve, emptied("D", PROD[reader], 1))
                    a_(dst[:, 2 * bank:2 * bank + 2, :].rearrange("p a b -> p (a b)"), b, ACT.Sigmoid
                       ).then_inc(bank_emptied_act, 1)

            for kind, a, q in SCHEDULE2:
                if kind == "part":
                    if q % 2 and PRODUCTS[PROD[a]][1][q // 2] == "A":
                        empty2(a, q // 2)
                    if (a, q) == ("kv2", 3):
                        act.wait_ge(bank_emptied_dve, emptied("D", PROD["kv2"], 0))
                        act.wait_ge(bank_emptied_act, emptied("A", PROD["kv2"], 1))
                        for half in range(2):
                            a_(sq2[:, half, :], z2[:, half, :], ACT.Square).then_inc(sq2_ready, 1)
                        act.wait_ge(ms2_ready, 1)
                        a_(ss2, r2, ACT.Sqrt).then_inc(rms2_ready, 1)
                    if a[:2] == "cx" and q == 3:
                        m = int(a[-1])
                        act.wait_ge(bank_emptied_dve, emptied("D", PROD[a], 1))
                        if m == 1:
                            act.wait_ge(cbz_ready, 2)
                        for c in range(4):
                            last = a_(z_s[:, c, :], u_s[:, c, :], ACT.Copy,
                                      scale=prm[:, 1, 96 + 4 * m + c:97 + 4 * m + c])
                        last.then_inc(conv_mid, 1)
                elif kind == "turn":
                    act.wait_ge(turned_q2, 1)
                    for i in range(2, 4):
                        a_(q2T[:, 2 * i:2 * i + 2, :].rearrange("p a b -> p (a b)"), ps[:, 4 + i, :], ACT.Copy
                           ).then_inc(q2T_act, 1)
                else:
                    k = a
                    if k < H2:
                        act.wait_ge(nmx_2, k + 1)
                        if k >= 2:
                            act.wait_ge(turned2, k - 1)
                        for half in range(2):
                            last = a_(p2[:, k % 2, half * S:(half + 1) * S],
                                      ps[:, 4 + k % 2, half * S:(half + 1) * S], ACT.Exp, scale=HD2 ** -0.5,
                                      bias=nmx2[:, k % 2, half:half + 1], accum_out=sum2[:, k % 2, half:half + 1])
                        last.then_inc(exp2, 1)
                    if k >= 2:
                        i = k - 2
                        act.wait_ge(o2, i + 1)
                        a_(o2T[:, i, :], ps[:, 7, (i % 2) * S:(i % 2 + 1) * S], ACT.Copy).then_inc(o2T_ready, 1)

            norm(3, xn_moe, gain=True)
            act.wait_ge(grp_nmax, 1)
            for half in range(2):
                a_(gexp[:, half, :], lg[:, half, 0:NG], ACT.Exp, bias=ngm[:, half, :],
                   accum_out=gsum[:, half, :]).then_inc(grp_exp, 1)
            act.wait_ge(top_diff, 1)
            a_(ex, dv, ACT.Exp).then_inc(top_exp, 1)

            def moe_iter(it):
                act.wait_ge(gathered, 2 * it + 2)
                a_(xg[:, 4:8, :], ps[:, 7, :].rearrange("p (c s) -> p c s", c=4), ACT.Copy).then_inc(xg_act, 1)
                act.wait_ge(selw_turned, it + 1)
                a_(selwT, ps[:, 5, 0:S], ACT.Copy).then_inc(selwT_ready, 1)

                def take_y(j):
                    q = (j ^ 1) * CAP
                    act.wait_ge(y_filled, 4 * it + j + 1)
                    a_(y[j * CAP:(j + 1) * CAP, 512:1024], ps[q:q + CAP, 4, :], ACT.Copy).then_inc(y_act, 1)

                for j in range(GRP):
                    q = (j ^ 1) * CAP
                    act.wait_ge(up_filled, 4 * it + j + 1)
                    if j >= 2:
                        act.wait_ge(act_ready, 4 * it + j - 1)
                    a_(hsil[q:q + CAP, j % 2, :], ps[j * CAP:(j + 1) * CAP, 1, :], ACT.Silu).then_inc(silu_ready, 1)
                    if j >= 1:
                        take_y(j - 1)
                take_y(GRP - 1)

            act.wait_ge(slots_ready, 1)
            with nc.scalar.Fori(0, NE // GRP) as it:
                moe_iter(it)
            fullest = nc.scalar.value_load(cmax[0:1, 0:1], min_val=0, max_val=S)
            with nc.scalar.Fori(1, ROUNDS) as r:
                with nc.scalar.If(fullest > r * CAP):
                    with nc.scalar.Fori(0, NE // GRP) as g:
                        moe_iter(r * (NE // GRP) + g)


SHAPES = {
    "x": (S, D), "attn_norm": (1, D), "w_in": (D, D_IN), "nsa_q_norm": (1, HD), "nsa_k_norm": (3, HD),
    "cmp_pos_k": (CMP_BLOCK, HD), "cmp_pos_v": (CMP_BLOCK, HD), "cmp_w1_k": (2048, 256), "cmp_w2_k": (256, HD),
    "cmp_w1_v": (2048, 256), "cmp_w2_v": (256, HD), "gla_w_gate2": (16, 256), "gla_b_gate": (1, 256),
    "gla_out_norm": (1, GDV), "w_out": (D, D), "ffn_norm": (1, D), "w_up": (D, 2 * FF), "conv_w": (3, 2 * FF),
    "conv_b": (1, 2 * FF), "w_down": (FF, D), "norm1_g_2": (1, D), "w_in_2": (D, D_IN2), "conv_w_2": (3, D),
    "q_norm_g_2": (1, HD2), "k_norm_g_2": (1, HD2), "w_conv_out_2": (D, D), "w_attn_out_2": (D, D),
    "w_o_2": (D, D), "norm2_g_2": (1, D), "w_group_2": (D, NG), "w_router_2": (D, NE),
    "w1_2": (NE, P, KC * DE), "w3_2": (NE, P, KC * DE), "w2_2": (NE, P, (DE // P) * D),
}
ALIAS = {"cmp_pos_k": "pe_k", "cmp_pos_v": "pe_v", "gla_b_gate": "b_gate", "w1_2": "w1", "w3_2": "w3", "w2_2": "w2"}


def kernel(**inputs):
    import concourse.bacc as _bacc
    from concourse.bass_utils import run_bass_kernel_spmd as _run

    nc = _bacc.Bacc("TRN2", target_bir_lowering=False, num_devices=1)
    arrays, t = {}, {}
    for name, shape in SHAPES.items():
        arrays["in_" + name] = np.ascontiguousarray(inputs[name]).reshape(shape)
        t[ALIAS.get(name, name)] = nc.dram_tensor("in_" + name, shape, F32, kind="ExternalInput").ap()
    arrays["in_consts"] = shape_constants()
    t["consts"] = nc.dram_tensor("in_consts", (P, N_CONST), F32, kind="ExternalInput").ap()
    out = nc.dram_tensor("out_0", (1, S, D), F32, kind="ExternalOutput").ap()
    two_blocks(nc, t, out.rearrange("a s d -> (a s) d"))
    r = _run(nc, [arrays], core_ids=[0])
    return r.results[0]["out_0"]
```
